# Optimizing a Trainium2 kernel written in Bass

```python
import math
import jax, jax.numpy as jnp
from jax import lax
import numpy as np

D_MODEL = 1024
BATCH = 1
SEQ = 1024
DEPTH = 1

CHUNK = 64
Q_BLOCK = 128
PLE_DIM = 256
D_FF = 4 * D_MODEL
EPS = 1e-6

GLA_HEADS = 4
GLA_DK = D_MODEL // 16
GLA_DV = D_MODEL // 8
GLA_GATE_RANK = 16
GLA_TAU = 16.0
GLA_WIDTH = GLA_HEADS * GLA_DV

MLA_HEADS = 8
MLA_NOPE = 64
MLA_ROPE = 32
MLA_V = 64
MLA_QK = MLA_NOPE + MLA_ROPE
MLA_Q_RANK = 256
MLA_KV_RANK = 128
MLA_WIDTH = MLA_HEADS * MLA_V
ROPE_THETA = 10000.0

D_MIX = GLA_WIDTH + MLA_WIDTH
IN_SPLITS = (GLA_HEADS * GLA_DK, GLA_HEADS * GLA_DK, GLA_WIDTH, GLA_GATE_RANK,
             GLA_WIDTH, MLA_Q_RANK, MLA_KV_RANK, MLA_ROPE)
D_IN = (GLA_HEADS * GLA_DK * 2 + GLA_WIDTH * 2 + GLA_GATE_RANK
        + MLA_Q_RANK + MLA_KV_RANK + MLA_ROPE)


def rms_norm(x, g):
    xf = x.astype(jnp.float32)
    y = xf * lax.rsqrt(jnp.mean(xf * xf, axis=-1, keepdims=True) + EPS)
    return (y * g.astype(jnp.float32)).astype(x.dtype)

def split_cols(t, sizes):
    out, start = [], 0
    for s in sizes:
        out.append(t[..., start:start + s])
        start += s
    return out

def rope_cos_sin(positions):
    inv_freq = ROPE_THETA ** (-jnp.arange(0, MLA_ROPE, 2, dtype=jnp.float32) / MLA_ROPE)
    ang = positions.astype(jnp.float32)[..., None] * inv_freq
    return jnp.cos(ang)[:, :, None, :], jnp.sin(ang)[:, :, None, :]

def apply_rope(x, cos, sin):
    half = x.shape[-1] // 2
    x1, x2 = x[..., :half], x[..., half:]
    c, s = cos.astype(x.dtype), sin.astype(x.dtype)
    return jnp.concatenate([x1 * c - x2 * s, x2 * c + x1 * s], axis=-1)

def gla_chunked(q, k, v, log_a):
    out_dtype = v.dtype
    B, S, H, DK = q.shape
    DV = v.shape[-1]
    NC = S // CHUNK

    def to_chunks(t):
        return t.astype(jnp.float32).reshape(B, NC, CHUNK, H, -1).transpose(1, 0, 3, 2, 4)

    qc, kc, vc, gc = to_chunks(q), to_chunks(k), to_chunks(v), to_chunks(log_a)
    causal = jnp.tril(jnp.ones((CHUNK, CHUNK), dtype=bool))[:, :, None]

    def step(state, inp):
        qi, ki, vi, gi = inp
        b = jnp.cumsum(gi, axis=2)
        b_last = b[:, :, -1:, :]
        o_inter = jnp.einsum('bhtk,bhkv->bhtv', qi * jnp.exp(b), state)
        diff = b[:, :, :, None, :] - b[:, :, None, :, :]
        decay = jnp.exp(jnp.where(causal, diff, -jnp.inf))
        scores = jnp.einsum('bhtk,bhsk,bhtsk->bhts', qi, ki, decay)
        o_intra = jnp.einsum('bhts,bhsv->bhtv', scores, vi)
        k_dec = ki * jnp.exp(b_last - b)
        state = state * jnp.exp(b_last[:, :, 0, :, None]) + jnp.einsum('bhsk,bhsv->bhkv', k_dec, vi)
        return state, o_inter + o_intra

    state0 = jnp.zeros((B, H, DK, DV), dtype=jnp.float32)
    _, oc = lax.scan(step, state0, (qc, kc, vc, gc))
    return oc.transpose(1, 0, 3, 2, 4).reshape(B, S, H, DV).astype(out_dtype)

def mla_attention(q, k, v):
    S = q.shape[1]
    scale = 1.0 / math.sqrt(MLA_QK)
    outs = []
    for blk in range(S // Q_BLOCK):
        qs, qe = blk * Q_BLOCK, (blk + 1) * Q_BLOCK
        qb, kb, vb = q[:, qs:qe], k[:, :qe], v[:, :qe]
        logits = jnp.einsum('bqhd,bkhd->bhqk', qb, kb).astype(jnp.float32) * scale
        q_chunk = (jnp.arange(qs, qe) // CHUNK)[:, None]
        k_chunk = (jnp.arange(qe) // CHUNK)[None, :]
        logits = jnp.where(k_chunk <= q_chunk, logits, -jnp.inf)
        probs = jax.nn.softmax(logits, axis=-1).astype(vb.dtype)
        outs.append(jnp.einsum('bhqk,bkhd->bqhd', probs, vb))
    return jnp.concatenate(outs, axis=1)

def first_inputs(seed: int = 0) -> dict:
    key = jax.random.key(seed)
    ks = jax.random.split(key, 24)
    f32 = jnp.float32

    def w(k, shape, fan_in):
        return jax.random.normal(k, shape, f32) * (fan_in ** -0.5)

    def gain(k, shape):
        return 1.0 + 0.1 * jax.random.normal(k, shape, f32)

    x = jax.random.normal(ks[0], (BATCH, SEQ, D_MODEL), f32)
    p = jax.random.normal(ks[1], (DEPTH, BATCH, SEQ, PLE_DIM), f32)
    offset = jax.random.randint(ks[2], (BATCH,), 0, 64, dtype=jnp.int32) * CHUNK
    positions = (offset[:, None] + jnp.arange(SEQ, dtype=jnp.int32)[None, :]).astype(jnp.int32)
    return {
        "x": x,
        "p": p,
        "positions": positions,
        "attn_norm": gain(ks[3], (DEPTH, D_MODEL)),
        "w_in": w(ks[4], (DEPTH, D_MODEL, D_IN), D_MODEL),
        "gla_gate_w2": w(ks[5], (DEPTH, GLA_GATE_RANK, GLA_HEADS * GLA_DK), GLA_GATE_RANK),
        "gla_gate_b": 0.1 * jax.random.normal(ks[6], (DEPTH, GLA_HEADS * GLA_DK), f32),
        "gla_out_norm": gain(ks[7], (DEPTH, GLA_DV)),
        "mla_q_norm": gain(ks[8], (DEPTH, MLA_Q_RANK)),
        "mla_w_uq": w(ks[9], (DEPTH, MLA_Q_RANK, MLA_HEADS * MLA_QK), MLA_Q_RANK),
        "mla_kv_norm": gain(ks[10], (DEPTH, MLA_KV_RANK)),
        "mla_w_ukv": w(ks[11], (DEPTH, MLA_KV_RANK, MLA_HEADS * (MLA_NOPE + MLA_V)), MLA_KV_RANK),
        "qk_norm_q": gain(ks[12], (DEPTH, MLA_QK)),
        "qk_norm_k": gain(ks[13], (DEPTH, MLA_QK)),
        "w_out": w(ks[14], (DEPTH, D_MIX, D_MODEL), D_MIX),
        "mlp_norm": gain(ks[15], (DEPTH, D_MODEL)),
        "w_mlp_up": w(ks[16], (DEPTH, D_MODEL, D_FF), D_MODEL),
        "w_mlp_down": w(ks[17], (DEPTH, D_FF, D_MODEL), D_FF),
        "ple_norm": gain(ks[18], (DEPTH, D_MODEL)),
        "w_ple_gate": w(ks[19], (DEPTH, D_MODEL, D_MODEL), D_MODEL),
        "b_ple_gate": 0.1 * jax.random.normal(ks[20], (DEPTH, D_MODEL), f32),
        "w_ple_proj": w(ks[21], (DEPTH, PLE_DIM, D_MODEL), PLE_DIM),
    }

def first_block(x, p, positions, attn_norm, w_in, gla_gate_w2, gla_gate_b, gla_out_norm,
              mla_q_norm, mla_w_uq, mla_kv_norm, mla_w_ukv, qk_norm_q, qk_norm_k,
              w_out, mlp_norm, w_mlp_up, w_mlp_down, ple_norm, w_ple_gate, b_ple_gate,
              w_ple_proj):
    B, S, _ = x.shape
    cos, sin = rope_cos_sin(positions)
    h = x
    for i in range(DEPTH):
        n = rms_norm(h, attn_norm[i])
        z = n @ w_in[i]
        gq, gk, gv, g_low, g_r, c_q, c_kv, k_r = split_cols(z, IN_SPLITS)

        q_g = gq.reshape(B, S, GLA_HEADS, GLA_DK) * (GLA_DK ** -0.5)
        k_g = gk.reshape(B, S, GLA_HEADS, GLA_DK)
        v_g = gv.reshape(B, S, GLA_HEADS, GLA_DV)
        log_a = jax.nn.log_sigmoid((g_low @ gla_gate_w2[i] + gla_gate_b[i]).astype(jnp.float32)) / GLA_TAU
        log_a = log_a.reshape(B, S, GLA_HEADS, GLA_DK)
        o_g = gla_chunked(q_g, k_g, v_g, log_a)
        o_g = rms_norm(o_g, gla_out_norm[i]).reshape(B, S, GLA_WIDTH) * jax.nn.silu(g_r)

        q_m = (rms_norm(c_q, mla_q_norm[i]) @ mla_w_uq[i]).reshape(B, S, MLA_HEADS, MLA_QK)
        kv = (rms_norm(c_kv, mla_kv_norm[i]) @ mla_w_ukv[i]).reshape(B, S, MLA_HEADS, MLA_NOPE + MLA_V)
        k_nope, v_m = kv[..., :MLA_NOPE], kv[..., MLA_NOPE:]
        k_rope = jnp.broadcast_to(k_r[:, :, None, :], (B, S, MLA_HEADS, MLA_ROPE))
        k_m = jnp.concatenate([k_nope, k_rope], axis=-1)
        q_m = rms_norm(q_m, qk_norm_q[i])
        k_m = rms_norm(k_m, qk_norm_k[i])
        q_m = jnp.concatenate([q_m[..., :MLA_NOPE], apply_rope(q_m[..., MLA_NOPE:], cos, sin)], axis=-1)
        k_m = jnp.concatenate([k_m[..., :MLA_NOPE], apply_rope(k_m[..., MLA_NOPE:], cos, sin)], axis=-1)
        o_m = mla_attention(q_m, k_m, v_m).reshape(B, S, MLA_WIDTH)

        h = h + jnp.concatenate([o_g, o_m], axis=-1) @ w_out[i]

        m = rms_norm(h, mlp_norm[i])
        h = h + jnp.square(jax.nn.relu(m @ w_mlp_up[i])) @ w_mlp_down[i]

        gate = jax.nn.sigmoid(rms_norm(h, ple_norm[i]) @ w_ple_gate[i] + b_ple_gate[i])
        h = h + (p[i] @ w_ple_proj[i]) * gate
    return h


POOL_WINDOWS = (2, 4, 8, 16)
N_POOL_GROUPS = len(POOL_WINDOWS)
POOL_WIDTH = D_MODEL // 2
POOL_GC = POOL_WIDTH // N_POOL_GROUPS
HEAD_DIM = 64
N_Q_HEADS = (D_MODEL // 2) // HEAD_DIM
N_KV_HEADS = 2
GROUP = N_Q_HEADS // N_KV_HEADS
ATTN_WIDTH = N_Q_HEADS * HEAD_DIM
KV_WIDTH = N_KV_HEADS * HEAD_DIM
WINDOW = 128
BLOCK = 128
NEG_INF = -1e30
ROPE_THETA_2 = 500000.0
ROT_DIM = HEAD_DIM // 4
N_BRANCHES = 2
GATE_WIDTH = N_BRANCHES * D_MODEL
IN_SPLITS_2 = (POOL_WIDTH, POOL_WIDTH + ATTN_WIDTH, POOL_WIDTH + ATTN_WIDTH + KV_WIDTH,
             POOL_WIDTH + ATTN_WIDTH + 2 * KV_WIDTH)
IN_WIDTH = POOL_WIDTH + ATTN_WIDTH + 2 * KV_WIDTH + GATE_WIDTH
D_FF_2 = 4 * D_MODEL


def _rmsnorm(x, g):
    xf = x.astype(jnp.float32)
    r = lax.rsqrt(jnp.mean(xf * xf, axis=-1, keepdims=True) + EPS)
    return (xf * r * g.astype(jnp.float32)).astype(x.dtype)

def _partial_rotary(t, cos, sin):
    half = ROT_DIM // 2
    t1 = t[..., :half]
    t2 = t[..., half:ROT_DIM]
    c = cos[None, :, None, :].astype(t.dtype)
    s = sin[None, :, None, :].astype(t.dtype)
    return jnp.concatenate([t1 * c - t2 * s, t2 * c + t1 * s, t[..., ROT_DIM:]], axis=-1)

def _multiscale_pool(u, w_pool, pool_scale):
    B, S, _ = u.shape
    uf = u.astype(jnp.float32)
    cs = jnp.pad(jnp.cumsum(uf, axis=1), ((0, 0), (1, 0), (0, 0)))
    t = jnp.arange(S)
    pooled = []
    for gi, w in enumerate(POOL_WINDOWS):
        c = cs[..., gi * POOL_GC:(gi + 1) * POOL_GC]
        upper = c[:, 1:]
        lower = jnp.pad(c[:, :S + 1 - w], ((0, 0), (w - 1, 0), (0, 0)))
        count = jnp.minimum(t + 1, w).astype(jnp.float32)[None, :, None]
        pooled.append((upper - lower) / count)
    pooled = jnp.stack(pooled, axis=2)
    diff = (pooled - uf.reshape(B, S, N_POOL_GROUPS, POOL_GC)).astype(u.dtype)
    mixed = jnp.einsum('bsgc,gcd->bsgd', diff, w_pool)
    return mixed.reshape(B, S, POOL_WIDTH) * pool_scale

def _sliding_window_sink_attention(q, k, v, sinks):
    B, S = q.shape[0], q.shape[1]
    nb = S // BLOCK
    qb = q.reshape(B, nb, BLOCK, N_KV_HEADS, GROUP, HEAD_DIM)

    def with_prev(t):
        tb = t.reshape(B, nb, BLOCK, N_KV_HEADS, HEAD_DIM)
        prev = jnp.pad(tb[:, :-1], ((0, 0), (1, 0), (0, 0), (0, 0), (0, 0)))
        return jnp.concatenate([prev, tb], axis=2)

    kk = with_prev(k)
    vv = with_prev(v)
    scale = HEAD_DIM ** -0.5
    s = jnp.einsum('bnqhgd,bnkhd->bnhgqk', qb, kk).astype(jnp.float32) * scale
    qi = jnp.arange(BLOCK)[:, None]
    kj = jnp.arange(2 * BLOCK)[None, :]
    rel = qi + BLOCK - kj
    band = (rel >= 0) & (rel < WINDOW)
    has_prev = (jnp.arange(nb) > 0)[:, None, None] | (kj >= BLOCK)[None]
    valid = band[None] & has_prev
    s = jnp.where(valid[None, :, None, None], s, NEG_INF)
    sink = jnp.broadcast_to(sinks.astype(jnp.float32).reshape(1, 1, N_KV_HEADS, GROUP, 1, 1),
                            s.shape[:-1] + (1,))
    p = jax.nn.softmax(jnp.concatenate([s, sink], axis=-1), axis=-1)[..., :-1]
    o = jnp.einsum('bnhgqk,bnkhd->bnqhgd', p.astype(v.dtype), vv)
    return o.reshape(B, S, ATTN_WIDTH)

def second_inputs(seed: int = 0) -> dict:
    key = jax.random.key(seed)
    ks = jax.random.split(key, 16)
    nrm = jax.random.normal
    f32 = jnp.float32

    def gain(k):
        return 1.0 + 0.1 * nrm(k, (DEPTH, D_MODEL), f32)

    return {
        "x": nrm(ks[0], (BATCH, SEQ, D_MODEL), f32),
        "g_mix_pre": gain(ks[1]),
        "w_in": nrm(ks[2], (DEPTH, D_MODEL, IN_WIDTH), f32) * D_MODEL ** -0.5,
        "b_in": 0.02 * nrm(ks[3], (DEPTH, IN_WIDTH), f32),
        "w_pool": nrm(ks[4], (DEPTH, N_POOL_GROUPS, POOL_GC, POOL_GC), f32) * POOL_GC ** -0.5,
        "pool_scale": 1.0 + 0.1 * nrm(ks[5], (DEPTH, POOL_WIDTH), f32),
        "attn_sinks": 0.5 * nrm(ks[6], (DEPTH, N_Q_HEADS), f32),
        "w_branch_pool": nrm(ks[7], (DEPTH, POOL_WIDTH, D_MODEL), f32) * POOL_WIDTH ** -0.5,
        "w_branch_attn": nrm(ks[8], (DEPTH, ATTN_WIDTH, D_MODEL), f32) * ATTN_WIDTH ** -0.5,
        "w_out": nrm(ks[9], (DEPTH, D_MODEL, D_MODEL), f32) * D_MODEL ** -0.5,
        "g_mix_post": gain(ks[10]),
        "g_mlp_pre": gain(ks[11]),
        "w_up": nrm(ks[12], (DEPTH, D_MODEL, D_FF_2), f32) * D_MODEL ** -0.5,
        "w_down": nrm(ks[13], (DEPTH, D_FF_2, D_MODEL), f32) * D_FF_2 ** -0.5,
        "g_mlp_post": gain(ks[14]),
    }

def second_block(x, g_mix_pre, w_in, b_in, w_pool, pool_scale, attn_sinks, w_branch_pool,
              w_branch_attn, w_out, g_mix_post, g_mlp_pre, w_up, w_down, g_mlp_post):
    B, S, _ = x.shape
    pos = jnp.arange(S, dtype=jnp.float32)
    inv_freq = ROPE_THETA_2 ** (-jnp.arange(0, ROT_DIM, 2, dtype=jnp.float32) / ROT_DIM)
    ang = pos[:, None] * inv_freq[None, :]
    cos, sin = jnp.cos(ang), jnp.sin(ang)

    for l in range(DEPTH):
        h = _rmsnorm(x, g_mix_pre[l])
        proj = jnp.einsum('bsd,de->bse', h, w_in[l]) + b_in[l]
        u_pool, q, k, v, gates = jnp.split(proj, IN_SPLITS_2, axis=-1)

        y_pool = _multiscale_pool(u_pool, w_pool[l], pool_scale[l])

        q = _partial_rotary(q.reshape(B, S, N_Q_HEADS, HEAD_DIM), cos, sin)
        k = _partial_rotary(k.reshape(B, S, N_KV_HEADS, HEAD_DIM), cos, sin)
        v = v.reshape(B, S, N_KV_HEADS, HEAD_DIM)
        y_attn = _sliding_window_sink_attention(
            q.reshape(B, S, N_KV_HEADS, GROUP, HEAD_DIM), k, v, attn_sinks[l])

        g = jax.nn.sigmoid(gates.astype(jnp.float32)).astype(x.dtype)
        g_pool, g_attn = g[..., :D_MODEL], g[..., D_MODEL:]
        merged = (g_pool * jnp.einsum('bsc,cd->bsd', y_pool, w_branch_pool[l])
                  + g_attn * jnp.einsum('bsc,cd->bsd', y_attn, w_branch_attn[l]))
        mix = jnp.einsum('bsd,de->bse', merged, w_out[l])
        x = x + _rmsnorm(mix, g_mix_post[l])

        h2 = _rmsnorm(x, g_mlp_pre[l])
        ff = jnp.einsum('bsf,fd->bsd',
                        jnp.square(jax.nn.relu(jnp.einsum('bsd,df->bsf', h2, w_up[l]))), w_down[l])
        x = x + _rmsnorm(ff, g_mlp_post[l])
    return x


def setup_inputs(seed=0):
    out = dict(first_inputs(seed))
    for name, value in second_inputs(seed + 1).items():
        if name != "x":
            out[name + "_2"] = value
    return out


def reference(
    x, p, positions, attn_norm, w_in, gla_gate_w2, gla_gate_b, gla_out_norm, mla_q_norm,
    mla_w_uq, mla_kv_norm, mla_w_ukv, qk_norm_q, qk_norm_k, w_out, mlp_norm, w_mlp_up,
    w_mlp_down, ple_norm, w_ple_gate, b_ple_gate, w_ple_proj, g_mix_pre_2, w_in_2, b_in_2,
    w_pool_2, pool_scale_2, attn_sinks_2, w_branch_pool_2, w_branch_attn_2, w_out_2,
    g_mix_post_2, g_mlp_pre_2, w_up_2, w_down_2, g_mlp_post_2,
):
    x = first_block(
        x, p, positions, attn_norm, w_in, gla_gate_w2, gla_gate_b, gla_out_norm, mla_q_norm,
        mla_w_uq, mla_kv_norm, mla_w_ukv, qk_norm_q, qk_norm_k, w_out, mlp_norm, w_mlp_up,
        w_mlp_down, ple_norm, w_ple_gate, b_ple_gate, w_ple_proj,
    )
    return second_block(
        x, g_mix_pre_2, w_in_2, b_in_2, w_pool_2, pool_scale_2, attn_sinks_2, w_branch_pool_2,
        w_branch_attn_2, w_out_2, g_mix_post_2, g_mlp_pre_2, w_up_2, w_down_2, g_mlp_post_2,
    )


_drawn_inputs = setup_inputs


def setup_inputs(seed=0):
    import zlib

    import numpy as np

    out = dict(_drawn_inputs(seed))
    spreads = {}
    factors = {'gla_gate_b': 2.89,
     'mla_q_norm': 6.879,
     'mla_kv_norm': 3.632,
     'qk_norm_q': 6.492,
     'qk_norm_k': 6.408,
     'ple_norm': 14.731,
     'b_ple_gate': 14.937,
     'b_in_2': 4.556,
     'attn_sinks_2': 8.0,
     'gla_gate_w2': 3.274,
     'gla_out_norm': 3.25}
    for name, (base, spread) in spreads.items():
        noise = np.random.default_rng([zlib.crc32(name.encode()), seed]).standard_normal(out[name].shape)
        drawn = base * np.exp(spread * noise) if base else spread * noise
        out[name] = __import__('jax').numpy.asarray(drawn.astype(out[name].dtype))
    for name, factor in factors.items():
        out[name] = (out[name] * factor).astype(out[name].dtype)
    return out
```

```python
import math
from contextlib import ExitStack

import concourse.bass as bass
import numpy as np
from concourse import mybir

F32 = mybir.dt.float32
F32R = mybir.dt.float32r
I32 = mybir.dt.int32
ACT = mybir.ActivationFunctionType
ALU = mybir.AluOpType
AX_X = mybir.AxisListType.X

P = 128
S = 1024
D = 1024
DT = D // P
HALF = 512
WIN = S // P
EPS = 1e-6

CHUNK = 64
GH, GDK, GDV, GRANK = 4, 64, 128, 16
NCH = S // CHUNK
MH, NOPE, ROPE, QKD = 8, 64, 32, 96
LEVELS = [32, 16, 8, 4, 2, 1]
HD, NQ, NKV = 64, 8, 2
POOL_W = (2, 4, 8, 16)
NEG = -1e30

B_PP, B_WIN, B_WOUT, B_MLP1 = 0, 2, 18, 26
B_GATE, B_WIN2, B_MRG, B_WO2, B_MLP2, B_END = 90, 98, 108, 132, 140, 204
O_PP, O_WIN, O_WOUT, O_UP1, O_H1, O_GATE, O_WIN2, O_Y, O_WO2, O_UP2, O_H2 = (
    0, 2, 10, 18, 26, 58, 66, 74, 82, 90, 98)
C_ATTN, C_MLP, C_PLE, C_BPLE, C_MIXPRE, C_MIXPOST, C_MLPPRE, C_MLPPOST = range(0, 64, 8)
C_BIN, C_POOLS, C_GATEB, C_GOUT, C_QN, C_KVN, C_QKQ, C_QKK, C_SINK = 64, 90, 94, 96, 97, 99, 100, 101, 102
NCOL = 110


def build(nc, t):
    ctx = ExitStack()
    with ctx:
        base = (nc.sbuf_base + 31) // 32 * 32
        nc.bump_sbuf(int(207.75 * 1024) + base - nc.sbuf_base)

        def at(name, shape, kb, dt=F32):
            return nc.alloc_sbuf_tensor_at(name, shape, dt, offset=base + int(kb * 1024))

        def sem(name):
            return ctx.enter_context(nc.semaphore(name))

        XB, PB, QB_, WB, TB, RB, CB = 0, 32, 96, 160, 184, 192, 204
        X = at("X", [P, DT, S], XB)
        opP_hi, opP_lo = at("opP_hi", [P, DT, S], PB, F32R), at("opP_lo", [P, DT, S], PB + 32, F32R)
        opQ_hi, opQ_lo = at("opQ_hi", [P, DT, S], QB_, F32R), at("opQ_lo", [P, DT, S], QB_ + 32, F32R)
        w_stage = at("w_stage", [P, 2, 1024], WB)
        w_hi, w_lo = at("w_hi", [P, 2, 1024], WB + 8, F32R), at("w_lo", [P, 2, 1024], WB + 16, F32R)
        T = at("T", [P, 2, S], TB)
        R = at("R", [P, S], RB)
        ssq = at("ssq", [P, S], RB + 4)
        sqs = at("sqs", [P, S], RB + 8)
        ones = at("ones", [P, P], CB)
        ident = at("ident", [P, P], CB + 0.5)
        col = at("col", [P, NCOL], CB + 1)
        small = at("small", [P, 64], CB + 1.5)
        eps_c, one_c, halfpi_c = small[:, 0:1], small[:, 1:2], small[:, 2:3]

        p_hi, p_lo = at("p_hi", [P, 2, S], QB_, F32R), at("p_lo", [P, 2, S], QB_ + 8, F32R)
        p_f = at("p_f", [P, 2, S], QB_ + 16)
        ppout = at("ppout", [P, DT, S], QB_ + 32)
        Z = at("Z", [P, 16, S], QB_)
        Bc = at("Bc", [P, 2, S], PB)
        E = at("E", [P, 2, S], PB + 8)
        KE = at("KE", [P, 2, S], PB + 16)
        QE = at("QE", [P, 2 * S // 2], PB + 24)
        lmask = at("lmask", [P, len(LEVELS), CHUNK], PB + 28, I32)
        dmask = at("dmask", [P, P], PB + 29.5)
        gw2 = at("gw2", [P, 256], PB + 30)
        QX = at("QX", [P, 2, S], PB + 32)
        KDT = at("KDT", [P, WIN, 256], PB + 40)
        ST8 = at("ST8", [P, 2, NCH, P], PB + 48)
        VT = at("VT", [P, WIN, 512], XB)
        SC = at("SC", [P, 2, 2, WIN, P], XB + 16)
        reset = at("reset", [P, S], XB + 16)
        decay = small[:, 8:40]
        head_root = [KE[:, 0, :], KE[:, 1, :], E[:, 0, :], E[:, 1, :]]
        head_gate = [Bc[:, 0, :], Bc[:, 1, :], QX[:, 0, :], QX[:, 1, :]]
        QK = at("QK", [P, 2, 2, S], PB)
        SQ = at("SQ", [P, 2, S], PB + 16)
        SW = at("SW", [P, 2, S], PB + 24)
        RR = at("RR", [P, 2, S], PB + 32)
        CT, SN = at("CT", [P, S], PB + 40), at("SN", [P, S], PB + 44)
        PR = at("PR", [P, 2, S], PB + 48)
        PT = at("PT", [P, 2, S], PB + 56)
        VM = at("VM", [P, WIN, 512], XB)
        OT = at("OT", [P, WIN, 512], XB + 16)
        wq_h = at("wq_h", [P, 2, 192], QB_ + 16)
        wk_h = at("wk_h", [P, 2, 64], QB_ + 17.5)
        wv_m = at("wv_m", [P, 512], QB_ + 18)
        freq = at("freq", [P, 1], QB_ + 20)
        sgn = at("sgn", [P, 1], QB_ + 20.03125)
        pos_i = at("pos_i", [P, S], QB_ + 24, I32)
        ang, kf, ki = at("ang", [P, S], PB + 16), at("kf", [P, S], PB + 20), at("ki", [P, S], PB + 24, I32)
        nmx = small[:, 40:44]
        den = small[:, 44:48]
        Z2 = at("Z2", [P, 10, S], QB_)
        tabC, tabS = at("tabC", [P, S], QB_ + 40), at("tabS", [P, S], QB_ + 44)
        swq = at("swq", [P, 4, S], QB_)
        swk = at("swk", [P, S], QB_ + 48)
        kpad = at("kpad", [P, P + S], QB_ + 52)
        vpad = at("vpad", [P, WIN + 1, P], QB_ + 56.5)
        O2 = at("O2", [P, 512], QB_ + 61)
        S2 = at("S2", [P, NQ, 256], QB_)
        P2 = at("P2", [P, NQ, 256], QB_ + 8)
        PT2 = at("PT2", [P, NQ, 2, P], QB_ + 40)
        kb2 = at("kb2", [P, 2, 256], QB_ + 48)
        mask2 = at("mask2", [P, 2, 256], QB_ + 50)
        qb2 = at("qb2", [P, 2, 4, P], RB + 8)
        wpool = at("wpool", [P, 4, P], RB + 4)
        icnt = at("icnt", [P, 4, 16], CB + 1.75)
        m8, e8, d8, r8 = (small[:, 48 + 0:56], small[:, 56:64], small[:, 8:16], small[:, 16:24])
        nm8 = small[:, 24:32]
        Xre = at("Xre", [P, DT, S], PB + 32)

        ps = ctx.enter_context(nc.psum_tensor("ps", [P, 8, HALF], F32))

        def banks(a, n):
            return ps[:, a:a + n, :].rearrange("p a b -> p (a b)")

        w_landed = [sem("w_landed0"), sem("w_landed1")]
        w_hi_done, w_lo_done = sem("w_hi_done"), sem("w_lo_done")
        mm_done, evac_done = sem("mm_done"), sem("evac_done")
        operand_hi, operand_ready = sem("operand_hi"), sem("operand_ready")
        sq_done, ssq_done, stat_done, r_done = sem("sq_done"), sem("ssq_done"), sem("stat_done"), sem("r_done")
        x_landed = [sem(f"x_landed{k}") for k in range(DT)]
        x_back = [sem(f"x_back{k}") for k in range(DT)]
        p_landed, cst_landed, ones_set = sem("p_landed"), sem("cst_landed"), sem("ones_set")
        pp_mm, pp_evac, pp_spilled = sem("pp_mm"), sem("pp_evac"), sem("pp_spilled")
        act_step, dve_step, pool_step = sem("act_step"), sem("dve_step"), sem("pool_step")
        relu_sq = sem("relu_sq")
        pp_back, gated, pp_used, x_upd = sem("pp_back"), sem("gated"), sem("pp_used"), sem("x_upd")
        y_stored = sem("y_stored")
        g = {n: sem("gla_" + n) for n in (
            "consts", "logit", "lin", "soft", "cum", "exps", "kdec", "tr", "trc", "upd", "states",
            "lexp", "lq", "lk", "lmm", "lcp", "out", "oraw", "sq", "nst", "rn", "sig", "fin")}
        m = {n: sem("mla_" + n) for n in (
            "w0", "w1", "misc", "stat", "r", "lat", "vmm", "vev", "tab", "proj", "pev", "krot", "sq", "nst",
            "rr", "nrm", "swap", "rope", "qk", "mx", "exp", "tr", "trc", "pv", "ofree", "otr", "otc",
            "done", "sfree", "inv", "pfree", "prepfree", "angle", "sin")}
        s = {n: sem("swa_" + n) for n in (
            "consts", "z", "pool", "ptmp", "pmm", "y", "vtr", "vtc", "zero", "swap", "rope", "blk", "qk", "sc", "mx",
            "exp", "den", "tra", "tca", "trb", "tcb", "pv", "on", "otr", "otc", "spill", "sig", "mrg", "mt")}
        fin, x2_spilled = sem("fin"), sem("x2_spilled")

        def bc(ap, shape):
            return ap.to_broadcast(shape)

        class Link:

            def __init__(self, eng, steps):
                self.eng, self.steps, self.n = eng, steps, 0

            def __call__(self, ins):
                ins.then_inc(self.steps, 1)
                self.n += 1
                self.eng.wait_ge(self.steps, self.n)

        def stream(eng, b0, n, body, n0=0):
            with eng.Fori(0, n // 2) as i:
                for j in range(2):
                    body(i * 2 + (b0 + j), i + b0 // 2, i * 2 + (n0 + j), j)

        block = ctx.enter_context(nc.Block())

        @block.sync
        def _(sp):
            def load(b, turn, n, slot):
                if not (isinstance(b, int) and b < 2):
                    sp.wait_ge(w_lo_done, b - 1)
                sp.dma_start(w_stage[:, slot, :], t["w_stream"][bass.ds(b * P, P), :]).then_inc(w_landed[slot], 16)

            load(0, 0, 0, 0)
            load(1, 0, 1, 1)
            stream(sp, 2, B_WOUT, load)
            sp.wait_ge(g["fin"], GH)

            def head_weights(h, slot):
                if not isinstance(h, int) or h >= 2:
                    sp.wait_ge(m["proj"], h * 4 - 4)
                sp.dma_start(wq_h[:, slot, :], t["w_uq"][bass.ds(h * P, P), :]).then_inc(m[f"w{slot}"], 16)
                sp.dma_start(wk_h[:, slot, :], t["w_uk"][bass.ds(h * P, P), :]).then_inc(m[f"w{slot}"], 16)

            def swap(h, slot):
                sp.wait_ge(m["nrm"], h * 2 + 2)
                if not isinstance(h, int) or h >= 1:
                    sp.wait_ge(m["rope"], h)
                sp.dma_start(SW[64:80, :, :], QK[80:96, slot, :, :]).then_inc(m["swap"], 16)
                sp.dma_start(SW[80:96, :, :], QK[64:80, slot, :, :]).then_inc(m["swap"], 16)

            head_weights(0, 0)
            head_weights(1, 1)
            swap(0, 0)
            with sp.Fori(0, MH // 2 - 1) as i:
                head_weights(i * 2 + 2, 0)
                swap(i * 2 + 1, 1)
                head_weights(i * 2 + 3, 1)
                swap(i * 2 + 2, 0)
            swap(MH - 1, 1)

            sp.wait_ge(m["done"], 4)
            for k in range(DT):
                sp.dma_start(X[:, k, :], t["xT"][k * P:(k + 1) * P, :]).then_inc(x_back[k], 16)
            stream(sp, B_WOUT + 2, B_END - B_WOUT - 2, load)

        @block.gpsimd
        def _(pool):
            link = Link(pool, pool_step)
            pool.dma_start(col[:, :], t["cols"]).then_inc(cst_landed, 16)
            pool.dma_start(ident[:, :], t["ident"]).then_inc(cst_landed, 16)
            pool.dma_start(p_f[:, :, :], t["pT"].rearrange("(k p) n -> p k n", p=P)).then_inc(p_landed, 16)
            for k in range(DT):
                pool.dma_start(X[:, k, :], t["xT"][k * P:(k + 1) * P, :]).then_inc(x_landed[k], 16)
            pool.memset(ones[:, :], 1.0).then_inc(ones_set, 1)
            pool.memset(eps_c, EPS).then_inc(ones_set, 1)
            pool.memset(one_c, 1.0).then_inc(ones_set, 1)
            pool.memset(halfpi_c, math.pi / 2).then_inc(ones_set, 1)
            pool.wait_ge(pp_evac, 8)
            pool.dma_start(t["pp_spill"].rearrange("(k p) n -> p k n", p=P), ppout[:, :, :]).then_inc(pp_spilled, 16)

            pool.wait_ge(mm_done, B_WOUT)
            pool.dma_start(lmask[:, :, :], t["lmask"]).then_inc(g["consts"], 16)
            pool.dma_start(dmask[:, :], t["dmask"]).then_inc(g["consts"], 16)
            pool.dma_start(gw2[0:GRANK, :], t["gw2"]).then_inc(g["consts"], 16)
            pool.wait_ge(operand_ready, O_WOUT)
            pool.wait_ge(ssq_done, 9)
            link(pool.memset(reset[:, :], 1.0))
            pool.memset(reset[:, :].rearrange("p (c k) -> p c k", k=CHUNK)[:, :, 0:1], 0.0).then_inc(g["cum"], 1)

            pool.wait_ge(g["fin"], GH)
            pool.dma_start(wv_m[:, :], t["w_uv"]).then_inc(m["misc"], 16)
            pool.dma_start(freq[64:96, :], t["freq"]).then_inc(m["misc"], 16)
            pool.dma_start(sgn[64:96, :], t["sgn"]).then_inc(m["misc"], 16)
            pool.dma_start(pos_i[64:96, :], t["positions"].partition_broadcast(ROPE)).then_inc(m["misc"], 16)

            pool.wait_ge(pp_spilled, 16)
            pool.wait_ge(operand_ready, O_H1 + 32)
            pool.dma_start(T[:, 1, :], t["pp_spill"][0:P, :]).then_inc(pp_back, 16)
            with pool.Fori(1, DT) as i:
                pool.wait_ge(pp_used, i)
                pool.wait_ge(pp_spilled, 16)
                pool.dma_start(T[:, 1, :], t["pp_spill"][bass.ds(i * P, P), :]).then_inc(pp_back, 16)

            pool.wait_ge(x_upd, DT)
            pool.dma_start(t["x_spill"].rearrange("(k p) n -> p k n", p=P), X[:, :, :]).then_inc(s["spill"], 16)
            pool.wait_ge(mm_done, B_WIN2)
            pool.dma_start(tabC[:, :], t["tabC"]).then_inc(s["consts"], 16)
            pool.dma_start(tabS[:, :], t["tabS"]).then_inc(s["consts"], 16)
            pool.dma_start(icnt[:, :, :], t["icnt"]).then_inc(s["consts"], 16)
            pool.wait_ge(r_done, 4)
            pool.dma_start(wpool[:, :, :], t["w_pool"]).then_inc(s["consts"], 16)
            pool.memset(kpad[:, 0:P], 0.0).then_inc(s["zero"], 1)
            pool.memset(vpad[:, 0, :], 0.0).then_inc(s["zero"], 1)
            pool.memset(swk[:, :], 0.0).then_inc(s["zero"], 1)
            pool.wait_ge(s["pool"], 4)
            pool.wait_ge(s["pmm"], 4)
            pool.memset(swq[:, :, :], 0.0).then_inc(s["zero"], 1)
            pool.wait_ge(s["zero"], 4)
            pool.wait_ge(s["z"], 9)
            for a in (0, 64):
                for u, v in ((a, a + 8), (a + 8, a)):
                    pool.dma_start(swq[u:u + 8, :, :], Z2[v:v + 8, 4:8, :]).then_inc(s["swap"], 16)
                    pool.dma_start(swk[u:u + 8, :], Z2[v:v + 8, 8, :]).then_inc(s["swap"], 16)
            pool.wait_ge(s["rope"], 2)
            pool.dma_start(mask2[:, :, :], t["mask2"]).then_inc(s["consts"], 16)

            pool.wait_ge(mm_done, B_WO2)
            pool.wait_ge(s["spill"], 16)
            for k in range(DT):
                pool.dma_start(Xre[:, k, :], t["x_spill"][k * P:(k + 1) * P, :]).then_inc(x_landed[k], 16)
            pool.wait_ge(s["mt"], DT)
            pool.dma_start(t["x_spill"].rearrange("(k p) n -> p k n", p=P), X[:, :, :]).then_inc(x2_spilled, 16)
            pool.wait_ge(x2_spilled, 16)
            pool.wait_ge(mm_done, B_MLP2 + 56)
            for k in range(DT):
                pool.dma_start(Xre[:, k, :], t["x_spill"][k * P:(k + 1) * P, :]).then_inc(x_landed[k], 16)
            for k in range(DT):
                pool.wait_ge(fin, k + 1)
                pool.dma_start(t["out"][k * P:(k + 1) * P, :], X[:, k, :]).then_inc(y_stored, 16)
            pool.wait_ge(y_stored, 16 * DT)

        @block.scalar
        def _(act):
            link = Link(act, act_step)

            def w_high(b, turn, slot):
                act.wait_ge(w_landed[slot], turn * 16 + 16)
                if not isinstance(b, int) or b >= 2:
                    act.wait_ge(mm_done, b - 1)
                act.activation(w_hi[:, slot, :], w_stage[:, slot, :], ACT.Copy).then_inc(w_hi_done, 1)

            def settle(done=ones_set, value=4):
                act.wait_ge(done, value)

            def next_high(b, turn, slot):
                w_high(b + 1, turn + slot, 1 - slot)

            def square_free(norm, n):
                act.wait_ge(ssq_done, n + (9 * norm + 1))

            def square(src, norm, n, waited=False):
                if not waited:
                    square_free(norm, n)
                act.activation(sqs[:, :], src, ACT.Square).then_inc(sq_done, 1)

            def one(ap, n):
                return ap[:, n:n + 1] if isinstance(n, int) else ap[:, bass.ds(n, 1)]

            def tile(ap, n):
                return ap[:, n, :] if isinstance(n, int) else ap[:, bass.ds(n, 1), :].rearrange("p a b -> p (a b)")

            def high(hi, src, cbase, n):
                settle()
                act.activation(tile(hi, n), src, ACT.Copy, scale=one(col, n + cbase)).then_inc(operand_hi, 1)

            def inverse_root(norm, users_done):
                act.wait_ge(evac_done, users_done)
                act.wait_ge(stat_done, norm + 1)
                link(act.activation(R[:, :], banks(4, 2), ACT.Ln, scale=1.0 / D, bias=eps_c))
                act.activation(R[:, :], R[:, :], ACT.Exp, scale=-0.5).then_inc(r_done, 1)

            act.wait_ge(ones_set, 4)
            act.wait_ge(p_landed, 16)
            w_high(0, 0, 0)
            for k in range(2):
                act.activation(p_hi[:, k, :], p_f[:, k, :], ACT.Copy).then_inc(operand_hi, 1)
            w_high(1, 0, 1)
            act.wait_ge(cst_landed, 32)
            for k in range(DT):
                act.wait_ge(x_landed[k], 16)
                high(opP_hi, X[:, k, :], C_ATTN, k)
                square(X[:, k, :], 0, k)
            w_high(2, 1, 0)
            inverse_root(0, 0)

            stream(act, B_WIN, 16, lambda b, turn, n, slot: next_high(b, turn, slot))

            act.wait_ge(g["lin"], 2)
            link(act.activation(E[:, :, :], KE[:, :, :], ACT.Abs))
            link(act.activation(E[:, :, :], E[:, :, :], ACT.Exp, scale=-1.0))
            act.activation(E[:, :, :], E[:, :, :], ACT.Ln, bias=one_c).then_inc(g["soft"], 1)
            act.wait_ge(g["cum"], 4)
            act.activation(E[:, :, :], Bc[:, :, :], ACT.Exp, scale=1.0 / 16).then_inc(g["exps"], 1)
            act.activation(decay.rearrange("p (a c) -> p a c", a=2),
                           Bc[:, :, :].rearrange("p a (c k) -> p a c k", k=CHUNK)[:, :, :, CHUNK - 1],
                           ACT.Exp, scale=1.0 / 16).then_inc(g["exps"], 1)
            for w in range(WIN):
                act.wait_ge(g["tr"], w + 1)
                act.activation(VT[:, w, :], ps[:, 4 + w % 2, :], ACT.Copy).then_inc(g["trc"], 1)
            act.wait_ge(g["kdec"], 1)
            act.activation(E[:, :, :], E[:, :, :], ACT.Exp, scale=1.0 / 16).then_inc(g["exps"], 1)
            for w in range(WIN):
                act.wait_ge(g["tr"], WIN + w + 1)
                act.activation(KDT[:, w, :], ps[:, 4 + w % 2, 0:256], ACT.Copy).then_inc(g["trc"], 1)
            for lv in range(len(LEVELS)):
                act.wait_ge(g["lexp"], 2 * lv + 2)
                act.activation(E[:, :, :], E[:, :, :], ACT.Exp, scale=1.0 / 16).then_inc(g["exps"], 1)
            for h in range(GH):
                act.wait_ge(g["out"], h + 1)
                act.activation(Z[:, 4 + h, :], banks(2 * h, 2), ACT.Copy).then_inc(g["oraw"], 1)
                act.wait_ge(g["oraw"], h + 1)
                act.activation(T[:, h % 2, :], Z[:, 4 + h, :], ACT.Square).then_inc(g["sq"], 1)
                act.wait_ge(g["nst"], h + 1)
                root = head_root[h]
                link(act.activation(root, banks(2 * h, 2), ACT.Ln, scale=1.0 / GDV, bias=eps_c))
                act.activation(root, root, ACT.Exp, scale=-0.5).then_inc(g["rn"], 1)
            for h in range(GH):
                act.activation(head_gate[h], Z[:, 12 + h, :], ACT.Sigmoid).then_inc(g["sig"], 1)

            act.wait_ge(g["fin"], GH)
            act.activation(SQ[:, 0, :], Z[:, 0, :], ACT.Square).then_inc(m["sq"], 1)
            act.activation(SQ[:, 1, :], Z[:, 1, :], ACT.Square).then_inc(m["sq"], 1)
            act.activation(SW[:, 0, :], Z[:, 2, :], ACT.Square).then_inc(m["sq"], 1)
            for a, width in ((0, 256), (1, 128)):
                act.wait_ge(m["stat"], a + 1)
                link(act.activation(RR[:, a, :], banks(2 * a, 2), ACT.Ln, scale=1.0 / width, bias=eps_c))
                act.activation(RR[:, a, :], RR[:, a, :], ACT.Exp, scale=-0.5).then_inc(m["r"], 1)
            for w in range(WIN):
                act.wait_ge(m["vmm"], w + 1)
                act.activation(VM[:, w, :], ps[:, 4 + w % 2, :], ACT.Copy).then_inc(m["vev"], 1)
            act.wait_ge(m["angle"], 1)
            act.activation(SN[64:96, :], ang[64:96, :], ACT.Sin).then_inc(m["sin"], 1)
            link(act.activation(CT[64:96, :], ang[64:96, :], ACT.Abs))
            act.activation(CT[64:96, :], CT[64:96, :], ACT.Sin, scale=-1.0, bias=halfpi_c[64:96, :]).then_inc(m["sin"], 1)

            def prep(h, slot, part):
                if part < 4:
                    a, hf = part // 2, part % 2
                    rows = QKD if a == 0 else NOPE
                    act.wait_ge(m["proj"], h * 4 + part + 1)
                    if part == 0:
                        act.wait_ge(m["prepfree"], h + 1)
                    act.activation(QK[0:rows, slot, a, hf * HALF:(hf + 1) * HALF], ps[0:rows, 7, :], ACT.Copy)\
                       .then_inc(m["pev"], 1)
                    if part == 3:
                        act.activation(QK[64:96, slot, 1, :], Z[64:96, 3, :], ACT.Copy).then_inc(m["krot"], 1)
                        act.wait_ge(m["pev"], h * 8 + 4)
                        act.wait_ge(m["krot"], h + 1)
                        act.activation(SQ[0:QKD, :, :], QK[0:QKD, slot, :, :], ACT.Square).then_inc(m["sq"], 1)
                else:
                    a, hf = part // 2 - 2, part % 2
                    dst = RR[0:QKD, a, hf * HALF:(hf + 1) * HALF]
                    act.wait_ge(m["nst"], h * 4 + part - 3)
                    if part == 4 and (not isinstance(h, int) or h):
                        act.wait_ge(m["nrm"], h * 2)
                    act.activation(dst, ps[0:QKD, 7, :], ACT.Ln, scale=1.0 / QKD, bias=eps_c[0:QKD, :])\
                       .then_inc(m["pev"], 1)
                    act.wait_ge(m["pev"], h * 8 + part + 1)
                    act.activation(dst, dst, ACT.Exp, scale=-0.5).then_inc(m["rr"], 1)

            def soft(u, qt, slot):
                width = (qt + 1) * P
                act.wait_ge(m["mx"], u + 1)
                act.wait_ge(m["pfree"], u + 1)
                act.activation(PR[:, slot, 0:width], banks(2 * slot, 2)[:, 0:width], ACT.Exp, scale=1.0 / math.sqrt(QKD),
                               bias=nmx[:, slot:slot + 1], accum_out=den[:, slot:slot + 1]).then_inc(m["exp"], 1)

            act.wait_ge(m["tab"], 2)
            act.sem_inc(m["pfree"], 2)
            act.sem_inc(m["prepfree"], 2)
            act.sem_inc(m["exp"], 2)
            act.wait_ge(m["lat"], 3)
            for part in range(8):
                prep(0, 0, part)
            def head_pair(i, last):
                for j in range(2):
                    h = i * 2 + j
                    for qt in range(8):
                        soft(h * 8 + qt, qt, qt % 2)
                        if not (last and j == 1):
                            prep(h + 1, 1 - j, qt)
            with act.Fori(0, MH // 2 - 1) as i:
                head_pair(i, False)
            head_pair(MH // 2 - 1, True)
            for f in range(4):
                act.wait_ge(m["otr"], f + 1)
                act.activation(Z[:, 8 + f, :], banks(2 * (f % 2), 2), ACT.Copy).then_inc(m["otc"], 1)

            act.wait_ge(m["done"], 4)
            for k in range(DT):
                act.wait_ge(m["otc"], min(k + 1, 4))
                act.activation(opP_hi[:, k, :], Z[:, 8 + k, :], ACT.Copy).then_inc(operand_hi, 1)

            def wout_step(b, turn, n, slot):
                next_high(b, turn, slot)
                act.wait_ge(evac_done, b + 1)
                square_free(1, n)
                high(opQ_hi, tile(X, n), C_MLP, n)
                square(tile(X, n), 1, n, True)
            act.wait_ge(operand_ready, O_UP1)
            stream(act, B_WOUT, 8, wout_step)
            inverse_root(1, B_MLP1)

            def mlp(b0, hi, count0, down_last, last_group_steps):
                def up(gi):
                    def body(b, turn, n, slot):
                        next_high(b, turn, slot)
                        act.wait_ge(relu_sq, gi * 8 + n + (count0 + 1))
                        settle()
                        act.activation(tile(hi, n), T[:, slot, :], ACT.Copy).then_inc(operand_hi, 1)
                    return body

                def group(gi, down):
                    for n_blocks, off, body in ((8, 0, up(gi)), (8, 8, down)):
                        with act.Fori(0, n_blocks // 2) as i:
                            for j in range(2):
                                body(gi * 16 + i * 2 + (b0 + off + j), gi * 8 + i + (b0 + off) // 2, i * 2 + j, j)
                with act.Fori(0, 3) as gi:
                    group(gi, lambda b, turn, n, slot: next_high(b, turn, slot))
                with act.Fori(0, 4) as i:
                    for j in range(2):
                        up(3)(i * 2 + (b0 + 48 + j), i + (b0 + 48) // 2, i * 2 + j, j)
                last_group_steps()

            def down1():
                def body(b, turn, n, slot):
                    next_high(b, turn, slot)
                    act.wait_ge(evac_done, b + 1)
                    square_free(2, n)
                    high(opQ_hi, tile(X, n), C_PLE, n)
                    square(tile(X, n), 2, n, True)
                stream(act, B_MLP1 + 56, 8, body)

            mlp(B_MLP1, opP_hi, 0, None, down1)
            inverse_root(2, B_GATE)

            def gate_step(b, turn, n, slot):
                next_high(b, turn, slot)
                act.wait_ge(evac_done, b + 1)
                settle()
                act.activation(T[:, 0, :], T[:, 0, :], ACT.Sigmoid, bias=one(col, n + C_BPLE)).then_inc(gated, 1)
                act.wait_ge(x_upd, n + 1)
                square_free(3, n)
                high(opP_hi, tile(X, n), C_MIXPRE, n)
                square(tile(X, n), 3, n, True)
            stream(act, B_GATE, 8, gate_step)
            inverse_root(3, B_WIN2)

            def win2_step(b, turn, n, slot):
                next_high(b, turn, slot)
                act.wait_ge(evac_done, b + 1)
                settle()
                act.activation(tile(Z2, n), tile(Z2, n), ACT.Identity, bias=one(col, n + C_BIN)).then_inc(s["z"], 1)
            stream(act, B_WIN2, 10, win2_step)

            act.wait_ge(s["spill"], 16)
            for gi in range(4):
                act.wait_ge(s["pmm"], gi + 1)
                act.activation(X[:, gi, :], banks(2 * (gi % 2), 2), ACT.Copy,
                               scale=col[:, C_POOLS + gi:C_POOLS + gi + 1]).then_inc(s["y"], 1)
            for w in range(2):
                act.wait_ge(s["vtr"], w + 1)
                act.activation(vpad[:, 1 + 4 * w:5 + 4 * w, :].rearrange("p a b -> p (a b)"), ps[:, 4 + w, :], ACT.Copy)\
                   .then_inc(s["vtc"], 1)
            act.wait_ge(s["rope"], 2)
            act.wait_ge(r_done, 4)

            def blocks_in(n, slot):
                if not isinstance(n, int) or n >= 2:
                    act.wait_ge(s["qk"], n - 1)
                cols = bass.ds(n * P, P)
                settle()
                act.activation(qb2[:, slot, :, :], Z2[:, 4:8, cols], ACT.Copy).then_inc(s["blk"], 1)
                act.activation(kb2[:, slot, :], kpad[:, bass.ds(n * P, 2 * P)], ACT.Copy).then_inc(s["blk"], 1)

            def attend(n, slot, more):
                if more:
                    blocks_in(n + 1, 1 - slot)
                act.wait_ge(s["mx"], n + 1)
                if not isinstance(n, int) or n >= 1:
                    act.wait_ge(s["trb"], n)
                    act.wait_ge(s["den"], n)
                for h in range(NQ):
                    act.activation(P2[:, h, :], S2[:, h, :], ACT.Exp, bias=nm8[:, h:h + 1], accum_out=d8[:, h:h + 1])\
                       .then_inc(s["exp"], 1)
                act.activation(e8, m8, ACT.Exp).then_inc(s["exp"], 1)
                for name, half in (("tra", 0), ("trb", 1)):
                    act.wait_ge(s[name], n + 1)
                    if half == 0 and (not isinstance(n, int) or n >= 1):
                        act.wait_ge(s["pv"], n)
                    act.activation(PT2[:, 4 * half:4 * half + 4, :, :].rearrange("p a b c -> p (a b c)"), banks(4, 2), ACT.Copy)\
                       .then_inc(s["tca" if half == 0 else "tcb"], 1)
                act.wait_ge(s["otr"], n + 1)
                settle()
                act.activation(X[:, 4:8, bass.ds(n * P, P)], ps[:, 6, :].rearrange("p (a b) -> p a b", a=4), ACT.Copy)\
                   .then_inc(s["otc"], 1)

            blocks_in(0, 0)
            attend(0, 0, True)
            with act.Fori(0, 3) as i:
                attend(i * 2 + 1, 1, True)
                attend(i * 2 + 2, 0, True)
            attend(7, 1, False)

            act.wait_ge(s["y"], 4)
            act.wait_ge(s["otc"], 8)
            for k in range(DT):
                act.activation(opQ_hi[:, k, :], X[:, k, :], ACT.Copy).then_inc(operand_hi, 1)

            act.wait_ge(operand_ready, O_WO2)
            with act.Fori(0, 4) as i:
                for j in range(2):
                    for q in range(3):
                        o = 3 * j + q
                        next_high(i * 6 + (B_MRG + o), i * 3 + (B_MRG + o) // 2, o % 2)
                        if q < 2:
                            act.wait_ge(evac_done, i * 6 + (B_MRG + o + 1))
                            settle()
                            act.activation(T[:, q, :], T[:, q, :], ACT.Sigmoid,
                                           bias=one(col, i * 2 + (C_BIN + 10 + 8 * q + j))).then_inc(s["sig"], 1)

            for k in range(DT):
                act.wait_ge(s["mrg"], k + 2)
                if k == 0:
                    act.wait_ge(mm_done, B_WO2)
                act.activation(opQ_hi[:, k, :], X[:, k, :], ACT.Copy).then_inc(operand_hi, 1)

            def wo2_step(b, turn, n, slot):
                next_high(b, turn, slot)
                act.wait_ge(evac_done, b + 1)
                square(tile(X, n), 4, n)
            act.wait_ge(operand_ready, O_UP2)
            stream(act, B_WO2, 8, wo2_step)
            inverse_root(4, B_MLP2)
            for k in range(DT):
                act.wait_ge(s["mt"], k + 1)
                high(opP_hi, X[:, k, :], C_MLPPRE, k)
                square(X[:, k, :], 5, k)
            act.wait_ge(s["mt"], DT)
            inverse_root(5, B_MLP2)

            def down2():
                def body(b, turn, n, slot):
                    next_high(b, turn, slot)
                    act.wait_ge(evac_done, b + 1)
                    square(tile(X, n), 6, n)
                stream(act, B_MLP2 + 56, 6, body)
                body(B_END - 2, B_END // 2 - 1, 6, 0)
                act.wait_ge(evac_done, B_END)
                square(X[:, 7, :], 6, 7)

            mlp(B_MLP2, opQ_hi, 32, None, down2)
            inverse_root(6, B_END)

        @block.vector
        def _(v):
            link = Link(v, dve_step)

            def w_low(b, turn, slot):
                v.wait_ge(w_hi_done, b + 1)
                v.tensor_tensor(w_lo[:, slot, :], w_stage[:, slot, :], w_hi[:, slot, :].bitcast(F32), ALU.subtract)\
                 .then_inc(w_lo_done, 1)

            def next_low(b, turn, slot):
                w_low(b + 1, turn, 1 - slot)

            def tile(ap, n):
                return ap[:, n, :] if isinstance(n, int) else ap[:, bass.ds(n, 1), :].rearrange("p a b -> p (a b)")

            def one(ap, n):
                return ap[:, n:n + 1] if isinstance(n, int) else ap[:, bass.ds(n, 1)]

            def low(hi, lo, src, count, n, cbase=None):
                v.wait_ge(operand_hi, n + (count + 1))
                h = tile(hi, n).bitcast(F32)
                if cbase is None:
                    ins = v.tensor_tensor(tile(lo, n), src, h, ALU.subtract)
                else:
                    ins = v.scalar_tensor_tensor(tile(lo, n), src, one(col, n + cbase), h, ALU.mult, ALU.subtract)
                ins.then_inc(operand_ready, 1)

            def add_square(norm, n):
                v.wait_ge(ssq_done, n + (9 * norm + 1))
                v.wait_ge(sq_done, n + (8 * norm + 1))
                v.tensor_tensor(ssq[:, :], ssq[:, :], sqs[:, :], ALU.add).then_inc(ssq_done, 1)

            def zero_squares(norm):
                if norm:
                    v.wait_ge(stat_done, norm)
                v.memset(ssq[:, :], 0.0).then_inc(ssq_done, 1)

            zero_squares(0)
            w_low(0, 0, 0)
            for k in range(2):
                low(p_hi, p_lo, p_f[:, k, :], O_PP, k)
            w_low(1, 0, 1)
            v.wait_ge(cst_landed, 32)
            for k in range(DT):
                low(opP_hi, opP_lo, X[:, k, :], O_WIN, k, C_ATTN)
                add_square(0, k)
            w_low(2, 1, 0)
            for n in range(DT):
                v.wait_ge(pp_mm, n + 1)
                v.tensor_copy(ppout[:, n, :], banks(2 * (n % 4), 2)).then_inc(pp_evac, 1)
            v.wait_ge(pp_evac, 8)
            v.sem_inc(evac_done, 2)

            v.wait_ge(r_done, 1)
            v.wait_ge(pp_spilled, 16)

            def win_step(b, turn, n, slot):
                next_low(b, turn, slot)
                v.wait_ge(mm_done, b + 1)
                v.tensor_tensor(tile(Z, n), banks(2 * slot, 2), R[:, :], ALU.mult).then_inc(evac_done, 1)
            stream(v, B_WIN, 16, win_step)

            v.wait_ge(g["logit"], 2)
            v.wait_ge(evac_done, B_WOUT)
            for pr in range(2):
                v.tensor_scalar(KE[:, pr, :], banks(2 * pr, 2), col[:, C_GATEB + pr:C_GATEB + pr + 1], None,
                                ALU.add).then_inc(g["lin"], 1)
            v.wait_ge(g["soft"], 1)
            kef = KE[:, :, :].rearrange("p a b -> p (a b)")
            link(v.scalar_tensor_tensor(kef, kef, 0.0, E[:, :, :].rearrange("p a b -> p (a b)"), ALU.min, ALU.subtract))
            v.wait_ge(g["cum"], 1)
            for pr in range(2):
                v.tensor_tensor_scan(Bc[:, pr, :], reset[:, :], KE[:, pr, :], 0.0, ALU.mult, ALU.add).then_inc(g["cum"], 1)
            v.wait_ge(g["cum"], 3)
            v.sem_inc(g["cum"], 1)
            q_t, k_t = Z[:, 4:6, :], Z[:, 6:8, :]
            chunks = [P, 2 * NCH, CHUNK]
            Bf = Bc[:, :, :].rearrange("p a (c k) -> p (a c) k", k=CHUNK)
            Ef = E[:, :, :].rearrange("p a (c k) -> p (a c) k", k=CHUNK)
            v.wait_ge(g["exps"], 2)
            v.scalar_tensor_tensor(QX[:, :, :].rearrange("p a b -> p (a b)"), q_t.rearrange("p a b -> p (a b)"),
                                   GDK ** -0.5, E[:, :, :].rearrange("p a b -> p (a b)"), ALU.mult, ALU.mult)\
             .then_inc(g["states"], 1)
            v.wait_ge(g["states"], 1)
            v.tensor_tensor(Ef, bc(Bf[:, :, CHUNK - 1:CHUNK], chunks), Bf, ALU.subtract).then_inc(g["kdec"], 1)
            v.wait_ge(g["exps"], 3)
            v.tensor_tensor(KE[:, :, :], k_t, E[:, :, :], ALU.mult).then_inc(g["kdec"], 1)
            for hf in range(2):
                v.wait_ge(g["lmm"], hf + 1)
                v.tensor_tensor(SC[:, hf, :, :, :].rearrange("p a w t -> p (a w) t"),
                                banks(0, 4).rearrange("p (x t) -> p x t", t=P),
                                bc(dmask[:, :].unsqueeze(1), [P, 2 * WIN, P]), ALU.mult).then_inc(g["lcp"], 1)
            for pr in range(2):
                v.memset(ST8[:, pr, 0, :], 0.0).then_inc(g["states"], 1)
            for pr in range(2):
                v.wait_ge(g["upd"], pr + 1)
                for c in range(NCH - 1):
                    v.wait_ge(g["states"], 3 + pr * 15 + c if c else 3)
                    bank = 4 * 1 + 2 * (c % 2) + (c // 2) // 4
                    u = ps[:, bank, ((c // 2) % 4) * P:((c // 2) % 4 + 1) * P]
                    v.scalar_tensor_tensor(ST8[:, pr, c + 1, :], ST8[:, pr, c, :], decay[:, pr * NCH + c:pr * NCH + c + 1],
                                           u, ALU.mult, ALU.add).then_inc(g["states"], 1)
            for lv, size in enumerate(LEVELS):
                nodes = 2 * S // (2 * size)
                Bn = Bc[:, :, :].rearrange("p a b -> p (a b)").rearrange("p (n s l) -> p n s l", s=2, l=size)
                En = E[:, :, :].rearrange("p a b -> p (a b)").rearrange("p (n s l) -> p n s l", s=2, l=size)
                shape = [P, nodes, size]
                mid = bc(Bn[:, :, 0, size - 1:size], shape)
                if lv:
                    v.wait_ge(g["lk"], lv)
                if lv == 0:
                    v.wait_ge(g["tr"], 2 * WIN)
                v.wait_ge(g["kdec"], 2)
                v.tensor_tensor(En[:, :, 1, :], Bn[:, :, 1, :], mid, ALU.subtract).then_inc(g["lexp"], 1)
                v.tensor_tensor(En[:, :, 0, :], mid, Bn[:, :, 0, :], ALU.subtract).then_inc(g["lexp"], 1)
                v.wait_ge(g["exps"], 4 + lv)
                if lv:
                    v.wait_ge(g["lmm"], 2 + lv)
                qn = q_t.rearrange("p a b -> p (a b)").rearrange("p (n s l) -> p n s l", s=2, l=size)
                v.scalar_tensor_tensor(QE[:, :].rearrange("p (n l) -> p n l", l=size), qn[:, :, 1, :],
                                       GDK ** -0.5, En[:, :, 1, :], ALU.mult, ALU.mult).then_inc(g["lq"], 1)
                v.tensor_tensor(KE[:, :, :], k_t, E[:, :, :], ALU.mult).then_inc(g["lk"], 1)
                v.wait_ge(g["lmm"], 3 + lv)
                v.wait_ge(g["lcp"], 2 + lv)
                right = SC[:, :, :, :, :].rearrange("p a b w t -> p (a b w) t").rearrange(
                    "p x (n s l) -> p x n s l", s=2, l=size)[:, :, :, 1, :]
                msk = bc(lmask[:, lv:lv + 1, :].rearrange("p a (n l) -> p a n l", l=size), [P, 4 * WIN, CHUNK // size, size])
                v.copy_predicated(right, msk, banks(0, 4).rearrange("p (x n l) -> p x n l", x=4 * WIN, l=size))\
                 .then_inc(g["lcp"], 1)
            for h in range(GH):
                o, gr = Z[:, 4 + h, :], Z[:, 12 + h, :]
                v.wait_ge(g["rn"], h + 1)
                link(v.scalar_tensor_tensor(o, o, col[:, C_GOUT:C_GOUT + 1], head_root[h], ALU.mult, ALU.mult))
                v.wait_ge(g["sig"], h + 1)
                link(v.tensor_tensor(gr, gr, head_gate[h], ALU.mult))
                v.tensor_tensor(gr, gr, o, ALU.mult).then_inc(g["fin"], 1)
            v.wait_ge(g["fin"], GH)

            v.wait_ge(m["sq"], 2)
            v.tensor_tensor(SQ[:, 0, :], SQ[:, 0, :], SQ[:, 1, :], ALU.add).then_inc(m["lat"], 1)
            for a, tiles in ((0, (0, 1)), (1, (2,))):
                v.wait_ge(m["r"], a + 1)
                for z in tiles:
                    ins = v.scalar_tensor_tensor(Z[:, z, :], Z[:, z, :], col[:, C_QN + z:C_QN + z + 1], RR[:, a, :],
                                                 ALU.mult, ALU.mult)
                    link(ins)
                v.sem_inc(m["lat"], 1)
            v.wait_ge(m["misc"], 64)
            v.wait_ge(m["stat"], 2)
            rows = slice(64, 96)
            link(v.tensor_copy(ang[rows, :], pos_i[rows, :]))
            link(v.tensor_scalar(ang[rows, :], ang[rows, :], freq[rows, :], None, ALU.mult))
            link(v.tensor_scalar(kf[rows, :], ang[rows, :], 1.0 / (2 * math.pi), None, ALU.mult))
            link(v.tensor_copy(ki[rows, :], kf[rows, :]))
            link(v.tensor_copy(kf[rows, :], ki[rows, :]))
            c1 = 6.28125
            c2 = float(np.float32(np.round((2 * math.pi - c1) * 2 ** 20) / 2 ** 20))
            c3 = 2 * math.pi - c1 - c2
            for c in (c1, c2, c3):
                link(v.scalar_tensor_tensor(ang[rows, :], kf[rows, :], -c, ang[rows, :], ALU.mult, ALU.add))
            pi32 = float(np.nextafter(np.float32(math.pi), np.float32(0)))
            v.tensor_scalar(ang[rows, :], ang[rows, :], pi32, -pi32, ALU.min, ALU.max).then_inc(m["angle"], 1)
            v.wait_ge(m["sin"], 2)
            v.tensor_scalar(SN[rows, :], SN[rows, :], sgn[rows, :], None, ALU.mult).then_inc(m["tab"], 1)
            v.sem_inc(m["tab"], 1)

            def prep(h, slot, part):
                if part == 5 or part == 7:
                    a = part // 2 - 2
                    v.wait_ge(m["rr"], h * 4 + part - 3)
                    qk = QK[0:QKD, slot, a, :]
                    gain = col[0:QKD, C_QKQ + a:C_QKQ + a + 1]
                    v.scalar_tensor_tensor(qk, qk, gain, RR[0:QKD, a, :], ALU.mult, ALU.mult).then_inc(m["nrm"], 1)
                if part == 7:
                    v.wait_ge(m["nrm"], h * 2 + 2)
                    v.wait_ge(m["swap"], h * 32 + 32)
                    qk = QK[rows, slot, :, :]
                    v.tensor_tensor(SW[rows, :, :], SW[rows, :, :], bc(SN[rows, :].unsqueeze(1), [ROPE, 2, S]), ALU.mult)\
                     .then_inc(m["angle"], 1)
                    v.tensor_tensor(qk, qk, bc(CT[rows, :].unsqueeze(1), [ROPE, 2, S]), ALU.mult).then_inc(m["angle"], 1)
                    v.wait_ge(m["angle"], h * 2 + 3)
                    v.tensor_tensor(qk, qk, SW[rows, :, :], ALU.add).then_inc(m["rope"], 1)

            def unit_a(h, qt, slot):
                u, width = h * 8 + qt, (qt + 1) * P
                sc = banks(2 * slot, 2)
                v.wait_ge(m["qk"], u + 1)
                v.memset(sc[0:64, width - 64:width], NEG).then_inc(m["sfree"], 1)
                v.wait_ge(m["sfree"], u * 3 + 1)
                v.tensor_reduce(nmx[:, 2 + slot:3 + slot], sc[:, 0:width], AX_X, ALU.max).then_inc(m["sfree"], 1)
                v.wait_ge(m["sfree"], u * 3 + 2)
                v.tensor_scalar(nmx[:, slot:slot + 1], nmx[:, 2 + slot:3 + slot], -1.0 / math.sqrt(QKD), None, ALU.mult)\
                 .then_inc(m["mx"], 1)
                v.sem_inc(m["sfree"], 1)

            def unit_b(h, qt, slot):
                u, width = h * 8 + qt, (qt + 1) * P
                nb = (width + HALF - 1) // HALF
                for q in range(nb):
                    cnt = sum((x + 4) // 4 for x in range(qt)) + q
                    v.wait_ge(m["tr"], h * 12 + cnt + 1)
                    w = min(HALF, width - q * HALF)
                    v.tensor_copy(PT[:, slot, q * HALF:q * HALF + w], ps[:, 4 + q, 0:w]).then_inc(m["trc"], 1)
                v.wait_ge(m["exp"], u + 3)
                v.reciprocal(den[:, 2 + slot:3 + slot], den[:, slot:slot + 1]).then_inc(m["inv"], 1)

            def unit_c(h, qt, slot):
                u = h * 8 + qt
                v.wait_ge(m["pv"], u + 1)
                v.wait_ge(m["inv"], u + 1)
                v.tensor_scalar(OT[:, qt, bass.ds(h * 64, 64)], ps[:, 6, qt * 64:(qt + 1) * 64], den[:, 2 + slot:3 + slot],
                                None, ALU.mult).then_inc(m["ofree"], 1)

            v.sem_inc(m["trc"], 1)
            v.sem_inc(m["ofree"], 1)
            v.wait_ge(m["lat"], 3)
            for part in range(8):
                prep(0, 0, part)
            def head_pair(i, last):
                for j in range(2):
                    h = i * 2 + j
                    for qt in range(8):
                        unit_a(h, qt, qt % 2)
                        unit_b(h, qt, qt % 2)
                        unit_c(h, qt, qt % 2)
                        if not (last and j == 1):
                            prep(h + 1, 1 - j, qt)
            with v.Fori(0, MH // 2 - 1) as i:
                head_pair(i, False)
            head_pair(MH // 2 - 1, True)
            v.wait_ge(m["otr"], 4)
            v.sem_inc(m["done"], 4)

            for k in range(DT):
                low(opP_hi, opP_lo, Z[:, 8 + k, :], O_WOUT - 0, k)
            zero_squares(1)
            for k in range(DT):
                v.wait_ge(x_back[k], 16)

            def wout_step(b, turn, n, slot):
                next_low(b, turn, slot)
                v.wait_ge(mm_done, b + 1)
                v.tensor_tensor(tile(X, n), tile(X, n), banks(2 * slot, 2), ALU.add).then_inc(evac_done, 1)
                v.wait_ge(evac_done, b + 1)
                low(opQ_hi, opQ_lo, tile(X, n), O_UP1, n, C_MLP)
                add_square(1, n)
            stream(v, B_WOUT, 8, wout_step)

            def mlp(b0, norm, hi, lo, count0, ready0, down, last):
                v.wait_ge(r_done, norm + 1)

                def up(gi):
                    def body(b, turn, n, slot):
                        next_low(b, turn, slot)
                        v.wait_ge(mm_done, b + 1)
                        v.wait_ge(operand_hi, gi * 8 + n + (ready0 - 1))
                        tt = T[:, slot, :]
                        v.tensor_tensor(tt, banks(2 * slot, 2), R[:, :], ALU.mult).then_inc(evac_done, 1)
                        v.wait_ge(evac_done, b + 1)
                        v.scalar_tensor_tensor(tt, tt, 0.0, tt, ALU.max, ALU.mult).then_inc(relu_sq, 1)
                        v.wait_ge(relu_sq, gi * 8 + n + (count0 + 1))
                        v.wait_ge(operand_hi, gi * 8 + n + (ready0 + 1))
                        v.tensor_tensor(tile(lo, n), tt, tile(hi, n).bitcast(F32), ALU.subtract).then_inc(operand_ready, 1)
                    return body

                def run(gi, off, body, turns=4):
                    with v.Fori(0, turns) as i:
                        for j in range(2):
                            body(gi * 16 + i * 2 + (b0 + off + j), gi * 8 + i + (b0 + off) // 2, i * 2 + j, j)
                if down is not None:
                    with v.Fori(0, 3) as gi:
                        run(gi, 0, up(gi))
                        run(gi, 8, down)
                else:
                    run(0, 0, up(0))
                    v.wait_ge(x2_spilled, 16)
                    run(0, 8, first_down)
                    with v.Fori(1, 3) as gi:
                        run(gi, 0, up(gi))
                        run(gi, 8, acc_down)
                run(3, 0, up(3))
                zero_squares(2 if down is not None else 6)
                last()

            def acc_down(b, turn, n, slot):
                next_low(b, turn, slot)
                v.wait_ge(mm_done, b + 1)
                v.tensor_tensor(tile(X, n), tile(X, n), banks(2 * slot, 2), ALU.add).then_inc(evac_done, 1)

            def first_down(b, turn, n, slot):
                next_low(b, turn, slot)
                v.wait_ge(mm_done, b + 1)
                v.tensor_copy(tile(X, n), banks(2 * slot, 2)).then_inc(evac_done, 1)

            def down1():
                def body(b, turn, n, slot):
                    acc_down(b, turn, n, slot)
                    v.wait_ge(evac_done, b + 1)
                    low(opQ_hi, opQ_lo, tile(X, n), O_GATE, n, C_PLE)
                    add_square(2, n)
                stream(v, B_MLP1 + 56, 8, body)

            mlp(B_MLP1, 1, opP_hi, opP_lo, 0, O_H1, acc_down, down1)

            zero_squares(3)
            v.wait_ge(r_done, 3)

            def gate_step(b, turn, n, slot):
                next_low(b, turn, slot)
                v.wait_ge(mm_done, b + 1)
                v.tensor_tensor(T[:, 0, :], banks(2 * slot, 2), R[:, :], ALU.mult).then_inc(evac_done, 1)
                v.wait_ge(gated, n + 1)
                v.wait_ge(pp_back, n * 16 + 16)
                v.tensor_tensor(T[:, 0, :], T[:, 0, :], T[:, 1, :], ALU.mult).then_inc(pp_used, 1)
                v.wait_ge(pp_used, n + 1)
                v.tensor_tensor(tile(X, n), tile(X, n), T[:, 0, :], ALU.add).then_inc(x_upd, 1)
                v.wait_ge(x_upd, n + 1)
                low(opP_hi, opP_lo, tile(X, n), O_WIN2, n, C_MIXPRE)
                add_square(3, n)
            stream(v, B_GATE, 8, gate_step)

            v.wait_ge(r_done, 4)
            v.wait_ge(mm_done, B_WIN2)

            def win2_step(b, turn, n, slot):
                next_low(b, turn, slot)
                v.wait_ge(mm_done, b + 1)
                v.tensor_tensor(tile(Z2, n), banks(2 * slot, 2), R[:, :], ALU.mult).then_inc(evac_done, 1)
            stream(v, B_WIN2, 10, win2_step)

            v.wait_ge(s["consts"], 64)
            for gi, width in enumerate(POOL_W):
                v.wait_ge(s["z"], gi + 1)
                u = Z2[:, gi, :]
                src, step, slot = u, 1, 0
                while step < width:
                    dst = T[:, slot, :]
                    v.tensor_copy(dst[:, 0:step], src[:, 0:step]).then_inc(dve_step, 1)
                    link.n += 1
                    link(v.tensor_tensor(dst[:, step:S], src[:, step:S], src[:, 0:S - step], ALU.add))
                    src, step, slot = dst, step * 2, 1 - slot
                head = T[:, slot, 0:16]
                link(v.tensor_tensor(head, src[:, 0:16], icnt[:, gi, :], ALU.mult))
                link(v.scalar_tensor_tensor(src[:, 16:S], src[:, 16:S], 1.0 / width, u[:, 16:S], ALU.mult, ALU.subtract))
                link(v.tensor_tensor(src[:, 0:16], head, u[:, 0:16], ALU.subtract))
                v.tensor_copy(u, src).then_inc(s["pool"], 1)
                v.wait_ge(s["pool"], gi + 1)
            for a, (z, sw) in enumerate(((Z2[:, 4:8, :], swq[:, :, :]), (Z2[:, 8:9, :], swk[:, :].unsqueeze(1)))):
                n = 4 if a == 0 else 1
                v.wait_ge(s["swap"], 128)
                v.tensor_tensor(sw, sw, bc(tabS[:, :].unsqueeze(1), [P, n, S]), ALU.mult).then_inc(dve_step, 1)
                link.n += 1
                link(v.tensor_tensor(z, z, bc(tabC[:, :].unsqueeze(1), [P, n, S]), ALU.mult))
                if a == 0:
                    v.tensor_tensor(z, z, sw, ALU.add).then_inc(s["rope"], 1)
                else:
                    v.wait_ge(s["zero"], 1)
                    v.tensor_tensor(kpad[:, P:P + S], Z2[:, 8, :], swk[:, :], ALU.add).then_inc(s["rope"], 1)
            v.wait_ge(s["rope"], 2)
            v.wait_ge(s["consts"], 80)

            sink = col[:, C_SINK:C_SINK + NQ]

            def attend(n, slot, first):
                v.wait_ge(s["qk"], n + 1)
                if not isinstance(n, int) or n >= 1:
                    v.wait_ge(s["exp"], n * 9)
                mk = mask2[:, 0 if first else 1, :]
                v.scalar_tensor_tensor(S2[:, :, :], banks(0, 4).rearrange("p (h k) -> p h k", k=256), HD ** -0.5,
                                       bc(mk.unsqueeze(1), [P, NQ, 256]), ALU.mult, ALU.add).then_inc(s["sc"], 1)
                v.wait_ge(s["sc"], n * 5 + 1)
                v.tensor_reduce(m8, S2[:, :, :], AX_X, ALU.max).then_inc(s["sc"], 1)
                v.wait_ge(s["sc"], n * 5 + 2)
                v.tensor_tensor(m8, m8, sink, ALU.max).then_inc(s["sc"], 1)
                v.wait_ge(s["sc"], n * 5 + 3)
                v.tensor_scalar(nm8, m8, -1.0, None, ALU.mult).then_inc(s["sc"], 1)
                v.wait_ge(s["sc"], n * 5 + 4)
                v.tensor_tensor(m8, sink, m8, ALU.subtract).then_inc(s["mx"], 1)
                v.wait_ge(s["exp"], n * 9 + 9)
                v.tensor_tensor(r8, d8, e8, ALU.add).then_inc(s["sc"], 1)
                v.wait_ge(s["sc"], n * 5 + 5)
                v.reciprocal(r8, r8).then_inc(s["den"], 1)
                v.wait_ge(s["den"], n + 1)
                v.wait_ge(s["pv"], n + 1)
                if not isinstance(n, int) or n >= 1:
                    v.wait_ge(s["otr"], n)
                v.tensor_tensor(O2[:, :].rearrange("p (h d) -> p h d", d=HD), ps[:, 7, :].rearrange("p (h d) -> p h d", d=HD),
                                bc(r8.unsqueeze(2), [P, NQ, HD]), ALU.mult).then_inc(s["on"], 1)
            attend(0, 0, True)
            with v.Fori(0, 7) as i:
                attend(i + 1, 0, False)

            v.wait_ge(s["otc"], 8)
            for k in range(DT):
                low(opQ_hi, opQ_lo, X[:, k, :], O_Y, k)

            v.sem_inc(s["mrg"], 1)
            with v.Fori(0, 4) as i:
                for j in range(2):
                    n = i * 2 + j
                    for q in range(2):
                        o = 3 * j + q
                        b = i * 6 + (B_MRG + o)
                        next_low(b, None, o % 2)
                        v.wait_ge(mm_done, b + 1)
                        v.wait_ge(s["mrg"], n + 1)
                        v.tensor_tensor(T[:, q, :], banks(2 * (o % 2), 2), R[:, :], ALU.mult).then_inc(evac_done, 1)
                    o = 3 * j + 2
                    b = i * 6 + (B_MRG + o)
                    next_low(b, None, o % 2)
                    v.wait_ge(mm_done, b + 1)
                    v.wait_ge(s["sig"], n * 2 + 2)
                    v.tensor_tensor(T[:, 0, :], T[:, 0, :], banks(4, 2), ALU.mult).then_inc(s["ptmp"], 1)
                    v.tensor_tensor(T[:, 1, :], T[:, 1, :], banks(6, 2), ALU.mult).then_inc(s["ptmp"], 1)
                    v.wait_ge(s["ptmp"], n * 2 + 2)
                    v.sem_inc(evac_done, 1)
                    v.tensor_tensor(tile(X, n), T[:, 0, :], T[:, 1, :], ALU.add).then_inc(s["mrg"], 1)
            v.wait_ge(s["mrg"], DT + 1)
            for k in range(DT):
                low(opQ_hi, opQ_lo, X[:, k, :], O_WO2, k)
            zero_squares(4)

            def wo2_step(b, turn, n, slot):
                next_low(b, turn, slot)
                v.wait_ge(mm_done, b + 1)
                v.tensor_copy(tile(X, n), banks(2 * slot, 2)).then_inc(evac_done, 1)
                add_square(4, n)
            stream(v, B_WO2, 8, wo2_step)
            zero_squares(5)
            v.wait_ge(r_done, 5)
            v.wait_ge(evac_done, B_MLP2)
            for k in range(DT):
                v.scalar_tensor_tensor(X[:, k, :], X[:, k, :], col[:, C_MIXPOST + k:C_MIXPOST + k + 1], R[:, :],
                                       ALU.mult, ALU.mult).then_inc(dve_step, 1)
                link.n += 1
                v.wait_ge(dve_step, link.n)
                v.wait_ge(x_landed[k], 32)
                v.tensor_tensor(X[:, k, :], X[:, k, :], Xre[:, k, :], ALU.add).then_inc(s["mt"], 1)
                v.wait_ge(s["mt"], k + 1)
                low(opP_hi, opP_lo, X[:, k, :], O_UP2, k, C_MLPPRE)
                add_square(5, k)

            def down2():
                def body(b, turn, n, slot):
                    acc_down(b, turn, n, slot)
                    add_square(6, n)
                stream(v, B_MLP2 + 56, 6, body)
                body(B_END - 2, B_END // 2 - 1, 6, 0)
                v.wait_ge(mm_done, B_END)
                v.tensor_tensor(X[:, 7, :], X[:, 7, :], banks(2, 2), ALU.add).then_inc(evac_done, 1)
                add_square(6, 7)

            mlp(B_MLP2, 5, opQ_hi, opQ_lo, 32, O_H2, None, down2)
            v.wait_ge(r_done, 7)
            v.wait_ge(evac_done, B_END)
            for k in range(DT):
                link(v.scalar_tensor_tensor(X[:, k, :], X[:, k, :], col[:, C_MLPPOST + k:C_MLPPOST + k + 1], R[:, :],
                                            ALU.mult, ALU.mult))
                v.wait_ge(x_landed[k], 48)
                v.tensor_tensor(X[:, k, :], X[:, k, :], Xre[:, k, :], ALU.add).then_inc(fin, 1)

        @block.tensor
        def _(pe):
            def product(psum, wslot, wcols, hi, lo, ks, ready=None):
                for x, k in enumerate(ks):
                    if ready is not None:
                        pe.wait_ge(operand_ready, ready(k))
                    wh = w_hi[:, wslot, wcols(x)]
                    wl = w_lo[:, wslot, wcols(x)]
                    for weight, operand in ((wh, hi), (wh, lo), (wl, hi)):
                        for half in range(2):
                            mm = pe.matmul(ps[:, psum + half, :], weight, operand[:, k, half * HALF:(half + 1) * HALF],
                                           start=(x == 0 and weight is wh and operand is hi),
                                           stop=(x == len(ks) - 1 and weight is wl))
                return mm

            def wcols(x):
                return slice(x * P, (x + 1) * P)

            def dense(hi, lo, ready):
                def body(b, turn, n, slot):
                    pe.wait_ge(w_lo_done, b + 1)
                    pe.wait_ge(evac_done, b - 1)
                    product(2 * slot, slot, wcols, hi, lo, range(DT), ready).then_inc(mm_done, 1)
                return body

            def statistic(norm):
                pe.wait_ge(ssq_done, 9 * norm + 9)
                if norm:
                    pe.wait_ge(r_done, norm)
                for half in range(2):
                    mm = pe.matmul(ps[:, 4 + half, :], ones[:, :], ssq[:, half * HALF:(half + 1) * HALF], start=True, stop=True)
                mm.then_inc(stat_done, 1)

            for b in range(2):
                pe.wait_ge(w_lo_done, b + 1)
                for n in range(4):
                    if b:
                        pe.wait_ge(pp_evac, n + 1)
                    mm = product(2 * n, b, lambda x, n=n: slice((2 * n + x) * P, (2 * n + x + 1) * P),
                                 p_hi, p_lo, range(2), lambda k: O_PP + k + 1)
                    if n < 3:
                        mm.then_inc(pp_mm, 1)
                mm.then_inc(pp_mm, 1)
                pe.wait_ge(pp_mm, 4 * b + 4)
                pe.sem_inc(mm_done, 1)
            pe.wait_ge(pp_evac, 8)
            pe.wait_ge(ones_set, 4)
            statistic(0)
            stream(pe, B_WIN, 16, dense(opP_hi, opP_lo, lambda k: O_WIN + k + 1))

            pe.wait_ge(evac_done, B_WOUT)
            pe.wait_ge(g["consts"], 48)
            for pr in range(2):
                for half in range(2):
                    mm = pe.matmul(ps[:, 2 * pr + half, :], gw2[0:GRANK, pr * P:(pr + 1) * P],
                                   Z[0:GRANK, 3, half * HALF:(half + 1) * HALF], start=True, stop=True)
                mm.then_inc(g["logit"], 1)
            pe.wait_ge(cst_landed, 32)
            for w in range(WIN):
                if w >= 2:
                    pe.wait_ge(g["trc"], w - 1)
                for f in range(4):
                    mm = pe.transpose(ps[:, 4 + w % 2, f * P:(f + 1) * P], Z[:, 8 + f, w * P:(w + 1) * P], ident[:, :])
                mm.then_inc(g["tr"], 1)
            pe.wait_ge(g["cum"], 4)

            def scores(k_src, q_src, width, hf=None):
                for par in range(2):
                    for pr in range(2):
                        if hf is not None and par != hf:
                            continue
                        for w in range(WIN):
                            at_ = ((0 if hf is not None else par * 2 + pr) * WIN + w) * width if hf is None else \
                                (pr * WIN + w) * width
                            r = slice(64 * par, 64 * par + 64)
                            mm = pe.matmul(banks(0, 4)[:, at_:at_ + width], k_src(r, pr, w), q_src(r, pr, w),
                                           start=True, stop=True)
                return mm
            for hf in range(2):
                if hf:
                    pe.wait_ge(g["lcp"], 1)
                scores(lambda r, pr, w: Z[r, 6 + pr, w * P:(w + 1) * P],
                       lambda r, pr, w: Z[r, 4 + pr, w * P:(w + 1) * P], P, hf).then_inc(g["lmm"], 1)
            pe.wait_ge(g["kdec"], 2)
            for w in range(WIN):
                pe.wait_ge(g["trc"], WIN + w - 1)
                for pr in range(2):
                    mm = pe.transpose(ps[:, 4 + w % 2, pr * P:(pr + 1) * P], KE[:, pr, w * P:(w + 1) * P], ident[:, :])
                mm.then_inc(g["tr"], 1)
            pe.wait_ge(g["trc"], 2 * WIN)
            for pr in range(2):
                if pr:
                    pe.wait_ge(g["states"], 3 + 15)
                for c in range(NCH):
                    toks = slice(64 * (c % 2), 64 * (c % 2) + 64)
                    bank = 4 + 2 * (c % 2) + (c // 2) // 4
                    for hp in range(2):
                        h = 2 * pr + hp
                        mm = pe.matmul(ps[64 * hp:64 * hp + 64, bank, ((c // 2) % 4) * P:((c // 2) % 4 + 1) * P],
                                       KDT[toks, c // 2, h * 64:(h + 1) * 64], VT[toks, c // 2, h * P:(h + 1) * P],
                                       start=True, stop=True)
                mm.then_inc(g["upd"], 1)
            for lv in range(len(LEVELS)):
                pe.wait_ge(g["lq"], lv + 1)
                pe.wait_ge(g["lk"], lv + 1)
                pe.wait_ge(g["lcp"], 2 + lv)
                scores(lambda r, pr, w: KE[r, pr, w * P:(w + 1) * P],
                       lambda r, pr, w: QE[r, pr * HALF + w * 64:pr * HALF + (w + 1) * 64], 64).then_inc(g["lmm"], 1)
            pe.wait_ge(g["lcp"], 8)
            pe.wait_ge(g["states"], 3 + 30)
            for h in range(GH):
                pr, r = h // 2, slice(64 * (h % 2), 64 * (h % 2) + 64)
                for w in range(WIN):
                    dst = banks(2 * h, 2)[:, w * P:(w + 1) * P]
                    pe.matmul(dst, VT[:, w, h * P:(h + 1) * P], SC[:, h % 2, pr, w, :], start=True, stop=False)
                    for x in range(2):
                        c = 2 * w + x
                        mm = pe.matmul(dst[:, 64 * x:64 * x + 64], ST8[r, pr, c, :], QX[r, pr, c * 64:(c + 1) * 64],
                                       start=False, stop=(x == 1))
                mm.then_inc(g["out"], 1)
            for h in range(GH):
                pe.wait_ge(g["sq"], h + 1)
                for half in range(2):
                    mm = pe.matmul(ps[:, 2 * h + half, :], ones[:, :], T[:, h % 2, half * HALF:(half + 1) * HALF],
                                   start=True, stop=True)
                mm.then_inc(g["nst"], 1)

            pe.wait_ge(g["rn"], GH)
            pe.wait_ge(m["lat"], 1)
            for a, src in ((0, SQ[:, 0, :]), (1, SW[:, 0, :])):
                pe.wait_ge(m["sq"], 3)
                for half in range(2):
                    mm = pe.matmul(ps[:, 2 * a + half, :], ones[:, :], src[:, half * HALF:(half + 1) * HALF], start=True, stop=True)
                mm.then_inc(m["stat"], 1)
            pe.wait_ge(m["lat"], 3)
            pe.wait_ge(m["misc"], 64)
            for w in range(WIN):
                if w >= 2:
                    pe.wait_ge(m["vev"], w - 1)
                pe.matmul(ps[:, 4 + w % 2, :], Z[:, 2, w * P:(w + 1) * P], wv_m[:, :], start=True, stop=True).then_inc(m["vmm"], 1)

            def prep(h, slot, part):
                if isinstance(h, int) and h == 0 and part == 0:
                    pass
                else:
                    pe.wait_ge(m["pev"], h * 8 + part)
                if part < 4:
                    a, hf = part // 2, part % 2
                    cols = slice(hf * HALF, (hf + 1) * HALF)
                    if part == 0:
                        pe.wait_ge(m[f"w{slot}"], (h - slot) * 16 + 32)
                    if a == 0:
                        for k in range(2):
                            mm = pe.matmul(ps[0:QKD, 7, :], wq_h[:, slot, k * QKD:(k + 1) * QKD], Z[:, k, cols],
                                           start=(k == 0), stop=(k == 1))
                    else:
                        mm = pe.matmul(ps[0:NOPE, 7, :], wk_h[:, slot, :], Z[:, 2, cols], start=True, stop=True)
                    mm.then_inc(m["proj"], 1)
                else:
                    a, hf = part // 2 - 2, part % 2
                    pe.wait_ge(m["sq"], h + 4)
                    pe.matmul(ps[0:QKD, 7, :], ones[0:QKD, 0:QKD], SQ[0:QKD, a, hf * HALF:(hf + 1) * HALF],
                              start=True, stop=True).then_inc(m["nst"], 1)

            def qk(h, hslot, qt, slot):
                u, width = h * 8 + qt, (qt + 1) * P
                pe.wait_ge(m["rope"], h + 1)
                pe.wait_ge(m["exp"], u + 1)
                for a in range(0, width, HALF):
                    n = min(HALF, width - a)
                    mm = pe.matmul(banks(2 * slot, 2)[:, a:a + n], QK[0:QKD, hslot, 0, qt * P:(qt + 1) * P],
                                   QK[0:QKD, hslot, 1, a:a + n], start=True, stop=True)
                mm.then_inc(m["qk"], 1)
                if qt == 7:
                    pe.wait_ge(m["qk"], u + 1)
                    pe.sem_inc(m["prepfree"], 1)

            def tr(h, qt, slot):
                u, width = h * 8 + qt, (qt + 1) * P
                pe.wait_ge(m["exp"], u + 3)
                before = sum((x + 4) // 4 for x in range(qt))
                for q in range((width + HALF - 1) // HALF):
                    cnt = before + q
                    pe.wait_ge(m["trc"], h * 12 + (before + 1))
                    for kt in range(4 * q, min(4 * q + 4, qt + 1)):
                        mm = pe.transpose(ps[:, 4 + q, (kt - 4 * q) * P:(kt - 4 * q + 1) * P], PR[:, slot, kt * P:(kt + 1) * P],
                                          ident[:, :])
                    mm.then_inc(m["tr"], 1)
                pe.wait_ge(m["tr"], h * 12 + before + (width + HALF - 1) // HALF)
                pe.sem_inc(m["pfree"], 1)

            def pv(h, qt, slot):
                u, width = h * 8 + qt, (qt + 1) * P
                before = sum((x + 4) // 4 for x in range(qt)) + (width + HALF - 1) // HALF
                pe.wait_ge(m["trc"], h * 12 + (before + 1))
                pe.wait_ge(m["ofree"], u + 1)
                for kt in range(qt + 1):
                    mm = pe.matmul(ps[:, 6, qt * 64:(qt + 1) * 64], PT[:, slot, kt * P:(kt + 1) * P],
                                   VM[:, kt, bass.ds(h * 64, 64)], start=(kt == 0), stop=(kt == qt))
                mm.then_inc(m["pv"], 1)

            pe.wait_ge(m["vev"], WIN)
            for part in range(8):
                prep(0, 0, part)
            def head_pair(i, last):
                for j in range(2):
                    h = i * 2 + j
                    qk(h, j, 0, 0)
                    for qt in range(8):
                        if qt < 7:
                            qk(h, j, qt + 1, (qt + 1) % 2)
                        if not (last and j == 1):
                            prep(h + 1, 1 - j, qt)
                        tr(h, qt, qt % 2)
                        pv(h, qt, qt % 2)
            with pe.Fori(0, MH // 2 - 1) as i:
                head_pair(i, False)
            head_pair(MH // 2 - 1, True)
            pe.wait_ge(m["ofree"], 8 * MH + 1)
            for f in range(4):
                if f >= 2:
                    pe.wait_ge(m["otc"], f - 1)
                for w in range(WIN):
                    mm = pe.transpose(banks(2 * (f % 2), 2)[:, w * P:(w + 1) * P], OT[:, w, f * P:(f + 1) * P], ident[:, :])
                mm.then_inc(m["otr"], 1)

            pe.wait_ge(m["otc"], 4)
            stream(pe, B_WOUT, 8, dense(opP_hi, opP_lo, lambda k: O_WOUT + k + 1))

            def mlp(b0, norm, ahi, alo, a0, hhi, hlo, h0):
                statistic(norm)
                with pe.Fori(0, 4) as gi:
                    for off, hi, lo, ready in ((0, ahi, alo, lambda k: a0 + k + 1),
                                               (8, hhi, hlo, lambda k: gi * 8 + (h0 + k + 1))):
                        with pe.Fori(0, 4) as i:
                            for j in range(2):
                                dense(hi, lo, ready)(gi * 16 + i * 2 + (b0 + off + j), None, None, j)
            mlp(B_MLP1, 1, opQ_hi, opQ_lo, O_UP1, opP_hi, opP_lo, O_H1)
            statistic(2)
            stream(pe, B_GATE, 8, dense(opQ_hi, opQ_lo, lambda k: O_GATE + k + 1))

            statistic(3)
            stream(pe, B_WIN2, 10, dense(opP_hi, opP_lo, lambda k: O_WIN2 + k + 1))
            pe.wait_ge(evac_done, B_MRG)
            for gi in range(4):
                pe.wait_ge(s["pool"], gi + 1)
                if gi >= 2:
                    pe.wait_ge(s["y"], gi - 1)
                for half in range(2):
                    mm = pe.matmul(ps[:, 2 * (gi % 2) + half, :], wpool[:, gi, :], Z2[:, gi, half * HALF:(half + 1) * HALF],
                                   start=True, stop=True)
                mm.then_inc(s["pmm"], 1)
            pe.wait_ge(s["z"], 10)
            for w in range(2):
                for x in range(4):
                    mm = pe.transpose(ps[:, 4 + w, x * P:(x + 1) * P], Z2[:, 9, (4 * w + x) * P:(4 * w + x + 1) * P], ident[:, :])
                mm.then_inc(s["vtr"], 1)
            pe.wait_ge(s["vtc"], 2)
            pe.wait_ge(s["zero"], 2)
            pe.wait_ge(s["y"], 4)

            def scores2(n, slot):
                pe.wait_ge(s["blk"], n * 2 + 2)
                if not isinstance(n, int) or n >= 1:
                    pe.wait_ge(s["sc"], n * 5 - 4)
                for par in range(2):
                    for i in range(4):
                        h = 4 * par + i
                        mm = pe.matmul(banks(0, 4)[:, h * 256:(h + 1) * 256], qb2[64 * par:64 * par + 64, slot, i, :],
                                       kb2[64 * par:64 * par + 64, slot, :], start=True, stop=True)
                mm.then_inc(s["qk"], 1)

            def attend(n, slot, more):
                pe.wait_ge(s["exp"], n * 9 + 9)
                for name, done, half in (("tra", "tcb", 0), ("trb", "tca", 1)):
                    if half == 1:
                        pe.wait_ge(s[done], n + 1)
                    elif not isinstance(n, int) or n >= 1:
                        pe.wait_ge(s[done], n)
                    for h in range(4 * half, 4 * half + 4):
                        for kt in range(2):
                            mm = pe.transpose(banks(4, 2)[:, ((h % 4) * 2 + kt) * P:((h % 4) * 2 + kt + 1) * P],
                                              P2[:, h, kt * P:(kt + 1) * P], ident[:, :])
                    mm.then_inc(s[name], 1)
                if more:
                    scores2(n + 1, 1 - slot)
                pe.wait_ge(s["tcb"], n + 1)
                if not isinstance(n, int) or n >= 1:
                    pe.wait_ge(s["on"], n)
                for h in range(NQ):
                    for kt in range(2):
                        mm = pe.matmul(ps[:, 7, h * HD:(h + 1) * HD], PT2[:, h, kt, :],
                                       vpad[:, bass.ds(n + kt, 1), (h // 4) * HD:(h // 4 + 1) * HD].rearrange("p a b -> p (a b)"),
                                       start=(kt == 0), stop=(kt == 1))
                mm.then_inc(s["pv"], 1)
                pe.wait_ge(s["on"], n + 1)
                if not isinstance(n, int) or n >= 1:
                    pe.wait_ge(s["otc"], n)
                for f in range(4):
                    mm = pe.transpose(ps[:, 6, f * P:(f + 1) * P], O2[:, f * P:(f + 1) * P], ident[:, :])
                mm.then_inc(s["otr"], 1)

            scores2(0, 0)
            attend(0, 0, True)
            with pe.Fori(0, 3) as i:
                attend(i * 2 + 1, 1, True)
                attend(i * 2 + 2, 0, True)
            attend(7, 1, False)

            pe.wait_ge(s["otc"], 8)
            with pe.Fori(0, 4) as i:
                for j in range(2):
                    for q in range(2):
                        o = 3 * j + q
                        b = i * 6 + (B_MRG + o)
                        dense(opP_hi, opP_lo, None)(b, None, None, o % 2)
                    o = 3 * j + 2
                    b = i * 6 + (B_MRG + o)
                    pe.wait_ge(w_lo_done, b + 1)
                    pe.wait_ge(s["mrg"], i * 2 + (j + 1))
                    product(4, o % 2, wcols, opQ_hi, opQ_lo, range(4), lambda k: O_Y + k + 1)
                    product(6, o % 2, lambda x: wcols(x + 4), opQ_hi, opQ_lo, range(4, 8), lambda k: O_Y + k + 1)\
                        .then_inc(mm_done, 1)
            stream(pe, B_WO2, 8, dense(opQ_hi, opQ_lo, lambda k: O_WO2 + k + 1))
            statistic(4)
            mlp(B_MLP2, 5, opP_hi, opP_lo, O_UP2, opQ_hi, opQ_lo, O_H2)
            statistic(6)


def _layout(i):
    c = np.ascontiguousarray
    f = {k: np.asarray(v) for k, v in i.items()}

    def blocks(w):
        k, n = w.shape
        return w.reshape(k // P, P, n // P, P).transpose(2, 1, 0, 3).reshape(n // P * P, k // P * P)

    w_in = f["w_in"][0]
    q, k, v, low, r, cq, ckv, kr = np.split(w_in, np.cumsum([256, 256, 512, 16, 512, 256, 128]), axis=1)
    z = np.zeros((D, 48), np.float32)
    misc = np.concatenate([low, z, kr, z[:, :32]], axis=1)
    wp = f["w_ple_proj"][0]
    pp = [wp[:, b * 512:(b + 1) * 512].reshape(2, P, 4, P).transpose(1, 2, 0, 3).reshape(P, 1024) for b in range(2)]
    w_out = f["w_out"][0]
    w_out = np.concatenate([w_out[512:], w_out[:512]], axis=0)

    def mlp(up, down):
        u, out = blocks(up), []
        for gi in range(4):
            out += [u[gi * 1024:(gi + 1) * 1024], blocks(down[gi * 1024:(gi + 1) * 1024])]
        return out

    w2 = f["w_in_2"][0]
    q2 = w2[:, 512:1024].reshape(D, 2, 4, 64).transpose(0, 2, 1, 3).reshape(D, 512)
    gates = blocks(w2[:, 1280:])
    br = blocks(np.concatenate([f["w_branch_pool_2"][0], f["w_branch_attn_2"][0]], axis=0))
    merge = []
    for n in range(8):
        merge += [gates[n * P:(n + 1) * P], gates[(8 + n) * P:(9 + n) * P], br[n * P:(n + 1) * P]]
    stream = np.concatenate(
        pp + [blocks(np.concatenate([cq, ckv, misc, q, k, v, r], axis=1)), blocks(w_out)]
        + mlp(f["w_mlp_up"][0], f["w_mlp_down"][0]) + [blocks(f["w_ple_gate"][0])]
        + [blocks(np.concatenate([w2[:, :512], q2, w2[:, 1024:1280]], axis=1))] + merge
        + [blocks(f["w_out_2"][0])] + mlp(f["w_up_2"][0], f["w_down_2"][0]), axis=0)

    def vec(a):
        a = a.reshape(-1)
        if a.size % P:
            a = np.concatenate([a, np.zeros(P - a.size % P, a.dtype)])
        return a.reshape(-1, P).T

    b2 = f["b_in_2"][0]
    bq = b2[512:1024].reshape(2, 4, 64).transpose(1, 0, 2).reshape(-1)
    cols = np.concatenate(
        [vec(f[n][0]) for n in ("attn_norm", "mlp_norm", "ple_norm", "b_ple_gate")]
        + [vec(f[n][0]) for n in ("g_mix_pre_2", "g_mix_post_2", "g_mlp_pre_2", "g_mlp_post_2")]
        + [vec(np.concatenate([b2[:512], bq, b2[1024:]])), vec(f["pool_scale_2"][0]), vec(f["gla_gate_b"][0]),
           vec(f["gla_out_norm"][0]), vec(f["mla_q_norm"][0]), vec(f["mla_kv_norm"][0]),
           vec(f["qk_norm_q"][0]), vec(f["qk_norm_k"][0]), np.broadcast_to(f["attn_sinks_2"][0][None], (P, 8))], axis=1)
    ukv = f["mla_w_ukv"][0].reshape(P, 8, 2, 64)

    tok = np.arange(P)
    lmask = np.zeros((P, len(LEVELS), CHUNK), np.int32)
    for lv, size in enumerate(LEVELS):
        tt = np.concatenate([np.arange(n * 2 * size + size, (n + 1) * 2 * size) for n in range(P // (2 * size))])
        lmask[:, lv] = (tok[:, None] // (2 * size) == tt[None] // (2 * size)) & (tok[:, None] % (2 * size) < size)
    inv = (10000.0 ** (-np.arange(0, 32, 2, dtype=np.float32) / np.float32(32))).astype(np.float32)
    inv2 = (500000.0 ** (-np.arange(0, 16, 2, dtype=np.float32) / np.float32(16))).astype(np.float32)
    a2 = (np.arange(S, dtype=np.float32)[None] * inv2[:, None]).astype(np.float32)
    tabC, tabS = np.ones((P, S), np.float32), np.zeros((P, S), np.float32)
    for o in (0, 64):
        tabC[o:o + 8] = tabC[o + 8:o + 16] = np.cos(a2)
        tabS[o:o + 8], tabS[o + 8:o + 16] = -np.sin(a2), np.sin(a2)
    rel = tok[:, None] + P - np.arange(256)[None]
    band = (rel >= 0) & (rel < 128)
    mask2 = np.stack([np.where(band & (np.arange(256) >= P)[None], 0, NEG), np.where(band, 0, NEG)], 1).astype(np.float32)
    icnt = np.stack([1.0 / np.minimum(np.arange(16) + 1, w) for w in POOL_W]).astype(np.float32)
    return {
        "w_stream": c(stream), "xT": c(f["x"][0].T), "pT": c(f["p"][0, 0].T), "cols": c(cols),
        "ident": np.eye(P, dtype=np.float32), "lmask": lmask,
        "dmask": (np.eye(P) * GDK ** -0.5).astype(np.float32), "gw2": c(f["gla_gate_w2"][0]),
        "w_uv": c(ukv[:, :, 1].reshape(P, 512)), "freq": np.tile(inv, 2)[:, None],
        "sgn": np.repeat(np.float32([-1, 1]), 16)[:, None], "positions": c(f["positions"][0].astype(np.int32)),
        "w_uq": c(f["mla_w_uq"][0].reshape(2, P, 8, 96).transpose(2, 1, 0, 3).reshape(8 * P, 192)),
        "w_uk": c(ukv[:, :, 0].transpose(1, 0, 2).reshape(8 * P, 64)),
        "tabC": tabC, "tabS": tabS, "mask2": mask2,
        "icnt": c(np.broadcast_to(icnt[None], (P, 4, 16))), "w_pool": c(f["w_pool_2"][0].transpose(1, 0, 2)),
    }


def kernel(**inputs):
    import concourse.bacc as bacc
    from concourse.bass_utils import run_bass_kernel_spmd as run

    arrays = _layout(inputs)
    nc = bacc.Bacc("TRN2", target_bir_lowering=False, num_devices=1)
    t = {n: nc.dram_tensor("in_" + n, a.shape, mybir.dt.from_np(a.dtype), kind="ExternalInput").ap()
         for n, a in arrays.items()}
    t["out"] = nc.dram_tensor("out_T", (D, S), F32, kind="ExternalOutput").ap()
    for n in ("pp_spill", "x_spill"):
        t[n] = nc.dram_tensor(n, (D, S), F32, kind="Internal").ap()
    build(nc, t)
    r = run(nc, [{"in_" + n: a for n, a in arrays.items()}], core_ids=[0])
    return np.ascontiguousarray(r.results[0]["out_T"].T)[None]
```

```python
import math
from contextlib import ExitStack

import concourse.bass as bass
import numpy as np
from concourse import mybir

F32 = mybir.dt.float32
F32R = mybir.dt.float32r
I32 = mybir.dt.int32
ACT = mybir.ActivationFunctionType
ALU = mybir.AluOpType
AX_X = mybir.AxisListType.X

P = 128
S = 1024
D = 1024
DT = D // P
HALF = 512
WIN = S // P
EPS = 1e-6

CHUNK = 64
GH, GDK, GDV, GRANK = 4, 64, 128, 16
NCH = S // CHUNK
MH, NOPE, ROPE, QKD = 8, 64, 32, 96
LEVELS = [32, 16, 8, 4, 2, 1]
PIECES = [(qt, c0, min((qt + 1) * P - c0, HALF)) for qt in range(WIN) for c0 in range(0, (qt + 1) * P, HALF)]
PIECES_T = [(half, kt, max(half * HALF, kt * P), (half + 1) * HALF - max(half * HALF, kt * P))
            for half in range(2) for kt in range(4 * half + 4)]
HD, NQ, NKV = 64, 8, 2
POOL_W = (2, 4, 8, 16)
NEG = -1e30

B_PP, B_WIN, B_WOUT, B_MLP1 = 0, 2, 18, 26
B_GATE, B_WIN2, B_MRG, B_WO2, B_MLP2, B_END = 90, 98, 108, 132, 140, 204
O_PP, O_WIN, O_WOUT, O_UP1, O_H1, O_GATE, O_WIN2, O_Y, O_WO2, O_UP2, O_H2 = (
    0, 2, 10, 18, 26, 58, 66, 74, 82, 90, 98)
C_ATTN, C_MLP, C_PLE, C_BPLE, C_MIXPRE, C_MIXPOST, C_MLPPRE, C_MLPPOST = range(0, 64, 8)
C_BIN, C_POOLS, C_GATEB, C_GOUT, C_QN, C_KVN, C_QKQ, C_QKK, C_SINK = 64, 90, 94, 96, 97, 99, 100, 101, 102
NCOL = 110


def build(nc, t):
    ctx = ExitStack()
    with ctx:
        base = (nc.sbuf_base + 31) // 32 * 32
        nc.bump_sbuf(int(207.75 * 1024) + base - nc.sbuf_base)

        def at(name, shape, kb, dt=F32):
            return nc.alloc_sbuf_tensor_at(name, shape, dt, offset=base + int(kb * 1024))

        def sem(name):
            return ctx.enter_context(nc.semaphore(name))

        XB, PB, QB_, WB, TB, RB, CB = 0, 32, 96, 160, 184, 192, 204
        X = at("X", [P, DT, S], XB)
        opP_hi, opP_lo = at("opP_hi", [P, DT, S], PB, F32R), at("opP_lo", [P, DT, S], PB + 32, F32R)
        opQ_hi, opQ_lo = at("opQ_hi", [P, DT, S], QB_, F32R), at("opQ_lo", [P, DT, S], QB_ + 32, F32R)
        w_stage = at("w_stage", [P, 2, 1024], WB)
        w_hi, w_lo = at("w_hi", [P, 2, 1024], WB + 8, F32R), at("w_lo", [P, 2, 1024], WB + 16, F32R)
        T = at("T", [P, 2, S], TB)
        R = at("R", [P, S], RB)
        ssq = at("ssq", [P, S], RB + 4)
        sqs = at("sqs", [P, S], RB + 8)
        ones = at("ones", [P, P], CB)
        ident = at("ident", [P, P], CB + 0.5)
        col = at("col", [P, NCOL], CB + 1)
        small = at("small", [P, 64], CB + 1.5)
        eps_c, one_c, halfpi_c = small[:, 0:1], small[:, 1:2], small[:, 2:3]

        p_hi, p_lo = at("p_hi", [P, 2, S], QB_, F32R), at("p_lo", [P, 2, S], QB_ + 8, F32R)
        p_f = at("p_f", [P, 2, S], QB_ + 16)
        ppout = at("ppout", [P, DT, S], QB_ + 32)
        Z = at("Z", [P, 16, S], QB_)
        VT = at("VT", [P, WIN, 512], XB)
        Bc, E = at("Bc", [P, 2, S], XB + 16), at("E", [P, 2, S], XB + 24)
        KE = [at("KE0", [P, 2, S], TB), at("KE1", [P, 2, S], QB_ + 32)]
        QE = [at("QE0", [P, S], QB_ + 40), at("QE1", [P, S], QB_ + 44)]
        reset = at("reset", [P, S], RB + 4)
        gw2 = at("gw2", [P, 256], RB + 8)
        dmask = at("dmask", [P, P], RB + 9)
        lmask = at("lmask", [P, len(LEVELS), CHUNK], RB + 9.5, I32)
        SC = at("SC", [P, 2, 2, WIN, P], PB)
        ST8 = at("ST8", [P, 2, NCH, P], PB + 16)
        KDT = at("KDT", [P, WIN, 256], PB + 32)
        QX = at("QX", [P, 2, S], PB + 40)
        SQG = at("SQG", [P, 2, S], PB + 48)
        decay = small[:, 8:40]
        head_root = [KE[h // 2][:, h % 2, :] for h in range(GH)]
        head_gate = [E[:, 0, :], E[:, 1, :], Bc[:, 0, :], Bc[:, 1, :]]
        LSQ = at("LSQ", [P, 3, S], XB)
        LRT = at("LRT", [P, 2, S], XB + 16)
        QK = at("QK", [P, 2, 2, S], XB)
        SQ = at("SQ", [P, 2, S], XB + 16)
        SW = at("SW", [P, 2, S], XB + 24)
        RR = at("RR", [P, 2, S], PB)
        CT, SN = at("CT", [P, S], PB + 8), at("SN", [P, S], PB + 12)
        PT = at("PT", [P, 4, HALF], PB + 32)
        VA = at("VA", [P, 2, WIN, P], PB + 40)
        wq_h = at("wq_h", [P, 2, 192], RB)
        wk_h = at("wk_h", [P, 2, 64], RB + 1.5)
        wv_m = at("wv_m", [P, 512], RB + 2)
        freq = at("freq", [P, 1], QB_ + 20)
        sgn = at("sgn", [P, 1], QB_ + 20.03125)
        mrow = at("mrow", [P, P], QB_ + 20.5)
        pos_i = at("pos_i", [P, S], QB_ + 24, I32)
        ang, kf, ki = at("ang", [P, S], XB + 16), at("kf", [P, S], XB + 20), at("ki", [P, S], XB + 24, I32)
        mx8 = small[:, 40:48]
        mxb = small[:, 48:52]
        Z2 = at("Z2", [P, 10, S], QB_)
        tabC, tabS = at("tabC", [P, S], QB_ + 40), at("tabS", [P, S], QB_ + 44)
        swq = at("swq", [P, 4, S], QB_)
        swk = at("swk", [P, S], QB_ + 48)
        kpad = at("kpad", [P, P + S], QB_ + 52)
        vpad = at("vpad", [P, WIN + 1, P], QB_ + 56.5)
        O2 = at("O2", [P, 512], QB_ + 61)
        S2 = at("S2", [P, NQ, 256], QB_)
        P2 = at("P2", [P, NQ, 256], QB_ + 8)
        PT2 = at("PT2", [P, NQ, 2, P], QB_ + 40)
        kb2 = at("kb2", [P, 2, 256], QB_ + 48)
        mask2 = at("mask2", [P, 2, 256], QB_ + 50)
        qb2 = at("qb2", [P, 2, 4, P], RB + 8)
        wpool = at("wpool", [P, 4, P], RB + 4)
        icnt = at("icnt", [P, 4, 16], CB + 1.75)
        m8, e8, d8, r8 = (small[:, 48 + 0:56], small[:, 56:64], small[:, 8:16], small[:, 16:24])
        nm8 = small[:, 24:32]
        Xre = at("Xre", [P, DT, S], PB + 32)

        ps = ctx.enter_context(nc.psum_tensor("ps", [P, 8, HALF], F32))

        def banks(a, n):
            return ps[:, a:a + n, :].rearrange("p a b -> p (a b)")

        w_landed = [sem("w_landed0"), sem("w_landed1")]
        w_hi_done, w_lo_done = sem("w_hi_done"), sem("w_lo_done")
        mm_done, evac_done = sem("mm_done"), sem("evac_done")
        operand_hi, operand_ready = sem("operand_hi"), sem("operand_ready")
        sq_done, ssq_done, stat_done, r_done = sem("sq_done"), sem("ssq_done"), sem("stat_done"), sem("r_done")
        x_landed = [sem(f"x_landed{k}") for k in range(DT)]
        x_back = [sem("x_back0"), sem("x_back1")]
        p_landed, cst_landed, ones_set = sem("p_landed"), sem("cst_landed"), sem("ones_set")
        pp_mm, pp_evac, pp_spilled = sem("pp_mm"), sem("pp_evac"), sem("pp_spilled")
        act_step, dve_step, pool_step = sem("act_step"), sem("dve_step"), sem("pool_step")
        relu_sq = sem("relu_sq")
        pp_back, gated, pp_used, x_upd = sem("pp_back"), sem("gated"), sem("pp_used"), sem("x_upd")
        y_stored = sem("y_stored")
        g = {n: sem("gla_" + n) for n in (
            "consts", "w2", "logit", "lin", "soft", "cum", "exps", "kdec", "ln", "tr", "trc", "upd", "states",
            "lexp", "lq", "lk", "lmm", "lcp", "out", "oraw", "sq", "nst", "rn", "sig", "gated", "fin")}
        m = {n: sem("mla_" + n) for n in (
            "w0", "w1", "wv", "misc", "consts", "stat", "r", "lat", "tab", "angle", "sin", "job", "jev", "sq", "rr", "nrm",
            "swap", "swn", "rope", "scores", "corner", "red", "mx", "st", "exp", "pv", "inv", "ofree", "krot", "ln")}
        s = {n: sem("swa_" + n) for n in (
            "consts", "z", "pool", "ptmp", "pmm", "y", "vtr", "vtc", "zero", "swap", "rope", "blk", "qk", "sc", "mx",
            "exp", "den", "tra", "tca", "trb", "tcb", "pv", "on", "otr", "otc", "spill", "sig", "mrg", "mt")}
        fin, x2_spilled = sem("fin"), sem("x2_spilled")

        def bc(ap, shape):
            return ap.to_broadcast(shape)

        class Link:

            def __init__(self, eng, steps):
                self.eng, self.steps, self.n = eng, steps, 0

            def __call__(self, ins):
                ins.then_inc(self.steps, 1)
                self.n += 1
                self.eng.wait_ge(self.steps, self.n)

        def tile(ap, n):
            return ap[:, n, :] if isinstance(n, int) else ap[:, bass.ds(n, 1), :].rearrange("p a b -> p (a b)")

        def stream(eng, b0, n, body, n0=0):
            with eng.Fori(0, n // 2) as i:
                for j in range(2):
                    body(i * 2 + (b0 + j), i + b0 // 2, i * 2 + (n0 + j), j)

        block = ctx.enter_context(nc.Block())

        @block.sync
        def _(sp):
            def load(b, turn, n, slot):
                if not (isinstance(b, int) and b < 2):
                    sp.wait_ge(w_lo_done, b - 1)
                sp.dma_start(w_stage[:, slot, :], t["w_stream"][bass.ds(b * P, P), :]).then_inc(w_landed[slot], 16)

            load(0, 0, 0, 0)
            load(1, 0, 1, 1)
            stream(sp, 2, B_WOUT, load)
            sp.wait_ge(evac_done, B_WOUT)

            def head_weights(h, slot):
                if not isinstance(h, int) or h >= 2:
                    sp.wait_ge(m["job"], h * 12 - 20)
                sp.dma_start(wq_h[:, slot, :], t["w_uq"][bass.ds(h * P, P), :]).then_inc(m[f"w{slot}"], 16)
                sp.dma_start(wk_h[:, slot, :], t["w_uk"][bass.ds(h * P, P), :]).then_inc(m[f"w{slot}"], 16)

            def swap(h, slot):
                sp.wait_ge(m["nrm"], h * 2 + 2)
                if not isinstance(h, int) or h >= 1:
                    sp.wait_ge(m["rope"], h)
                sp.dma_start(SW[64:80, :, :], QK[80:96, slot, :, :]).then_inc(m["swap"], 16)
                sp.dma_start(SW[80:96, :, :], QK[64:80, slot, :, :]).then_inc(m["swap"], 16)

            head_weights(0, 0)
            head_weights(1, 1)
            swap(0, 0)
            with sp.Fori(0, MH // 2 - 1) as i:
                head_weights(i * 2 + 2, 0)
                swap(i * 2 + 1, 1)
                head_weights(i * 2 + 3, 1)
                swap(i * 2 + 2, 0)
            swap(MH - 1, 1)

            sp.wait_ge(m["st"], 12 * MH + 1)

            def residual(k, turn, slot):
                if not isinstance(k, int):
                    sp.wait_ge(x_back[slot], turn * 16)
                sp.dma_start(tile(X, k), t["xT"][bass.ds(k * P, P), :]).then_inc(x_back[slot], 16)

            residual(0, 0, 0)
            residual(1, 0, 1)
            with sp.Fori(0, 3) as i:
                for j in range(2):
                    load(i * 2 + (B_WOUT + 2 + j), None, None, j)
                    residual(i * 2 + (2 + j), i + 1, j)
            stream(sp, B_WOUT + 8, B_END - B_WOUT - 8, load)

        @block.gpsimd
        def _(pool):
            link = Link(pool, pool_step)
            pool.dma_start(col[:, :], t["cols"]).then_inc(cst_landed, 16)
            pool.dma_start(ident[:, :], t["ident"]).then_inc(cst_landed, 16)
            pool.dma_start(p_f[:, :, :], t["pT"].rearrange("(k p) n -> p k n", p=P)).then_inc(p_landed, 16)
            for k in range(DT):
                pool.dma_start(X[:, k, :], t["xT"][k * P:(k + 1) * P, :]).then_inc(x_landed[k], 16)
            pool.memset(ones[:, :], 1.0).then_inc(ones_set, 1)
            pool.memset(eps_c, EPS).then_inc(ones_set, 1)
            pool.memset(one_c, 1.0).then_inc(ones_set, 1)
            pool.memset(halfpi_c, math.pi / 2).then_inc(ones_set, 1)
            pool.wait_ge(pp_evac, 8)
            pool.dma_start(t["pp_spill"].rearrange("(k p) n -> p k n", p=P), ppout[:, :, :]).then_inc(pp_spilled, 16)

            pool.wait_ge(ssq_done, 9)
            pool.dma_start(gw2[0:GRANK, :], t["gw2"]).then_inc(g["w2"], 16)
            pool.dma_start(lmask[:, :, :], t["lmask"]).then_inc(g["consts"], 16)
            pool.dma_start(dmask[:, :], t["dmask"]).then_inc(g["consts"], 16)
            pool.wait_ge(stat_done, 1)
            link(pool.memset(reset[:, :], 1.0))
            pool.memset(reset[:, :].rearrange("p (c k) -> p c k", k=CHUNK)[:, :, 0:1], 0.0).then_inc(g["cum"], 1)

            pool.wait_ge(evac_done, B_WOUT)
            pool.dma_start(wv_m[:, :], t["w_uv"]).then_inc(m["wv"], 16)
            pool.wait_ge(g["out"], GH)
            pool.wait_ge(g["gated"], GH)
            pool.wait_ge(g["fin"], GH)
            pool.dma_start(freq[64:96, :], t["freq"]).then_inc(m["misc"], 16)
            pool.dma_start(sgn[64:96, :], t["sgn"]).then_inc(m["misc"], 16)
            pool.dma_start(pos_i[64:96, :], t["positions"].partition_broadcast(ROPE)).then_inc(m["misc"], 16)
            pool.memset(QK[96:97, :, 1, :], -1.0).then_inc(m["consts"], 1)
            pool.wait_ge(m["consts"], 1)
            pool.memset(VA[:, 0, :, 64:128], 1.0).then_inc(m["consts"], 1)
            pool.wait_ge(m["consts"], 2)
            pool.memset(VA[:, 1, :, 0:64], 1.0).then_inc(m["consts"], 1)
            pool.wait_ge(m["consts"], 3)
            pool.memset(mrow[0:1, 0:64], 0.0).then_inc(m["consts"], 1)
            pool.wait_ge(m["consts"], 4)
            pool.memset(mrow[0:1, 64:128], NEG).then_inc(m["consts"], 1)

            pool.wait_ge(m["tab"], 2)
            with pool.Fori(0, MH) as h:
                pool.wait_ge(m["swap"], h * 32 + 32)
                pool.tensor_tensor(SW[64:96, :, :], SW[64:96, :, :], bc(SN[64:96, :].unsqueeze(1), [ROPE, 2, S]), ALU.mult)\
                    .then_inc(m["swn"], 1)

            pool.wait_ge(pp_spilled, 16)
            pool.wait_ge(operand_ready, O_H1 + 32)
            pool.dma_start(T[:, 1, :], t["pp_spill"][0:P, :]).then_inc(pp_back, 16)
            with pool.Fori(1, DT) as i:
                pool.wait_ge(pp_used, i)
                pool.wait_ge(pp_spilled, 16)
                pool.dma_start(T[:, 1, :], t["pp_spill"][bass.ds(i * P, P), :]).then_inc(pp_back, 16)

            pool.wait_ge(x_upd, DT)
            pool.dma_start(t["x_spill"].rearrange("(k p) n -> p k n", p=P), X[:, :, :]).then_inc(s["spill"], 16)
            pool.wait_ge(mm_done, B_WIN2)
            pool.dma_start(tabC[:, :], t["tabC"]).then_inc(s["consts"], 16)
            pool.dma_start(tabS[:, :], t["tabS"]).then_inc(s["consts"], 16)
            pool.dma_start(icnt[:, :, :], t["icnt"]).then_inc(s["consts"], 16)
            pool.wait_ge(r_done, 4)
            pool.dma_start(wpool[:, :, :], t["w_pool"]).then_inc(s["consts"], 16)
            pool.memset(kpad[:, 0:P], 0.0).then_inc(s["zero"], 1)
            pool.memset(vpad[:, 0, :], 0.0).then_inc(s["zero"], 1)
            pool.memset(swk[:, :], 0.0).then_inc(s["zero"], 1)
            pool.wait_ge(s["pool"], 4)
            pool.wait_ge(s["pmm"], 4)
            pool.memset(swq[:, :, :], 0.0).then_inc(s["zero"], 1)
            pool.wait_ge(s["zero"], 4)
            pool.wait_ge(s["z"], 9)
            for a in (0, 64):
                for u, v in ((a, a + 8), (a + 8, a)):
                    pool.dma_start(swq[u:u + 8, :, :], Z2[v:v + 8, 4:8, :]).then_inc(s["swap"], 16)
                    pool.dma_start(swk[u:u + 8, :], Z2[v:v + 8, 8, :]).then_inc(s["swap"], 16)
            pool.wait_ge(s["rope"], 2)
            pool.dma_start(mask2[:, :, :], t["mask2"]).then_inc(s["consts"], 16)

            pool.wait_ge(mm_done, B_WO2)
            pool.wait_ge(s["spill"], 16)
            for k in range(DT):
                pool.dma_start(Xre[:, k, :], t["x_spill"][k * P:(k + 1) * P, :]).then_inc(x_landed[k], 16)
            pool.wait_ge(s["mt"], DT)
            pool.dma_start(t["x_spill"].rearrange("(k p) n -> p k n", p=P), X[:, :, :]).then_inc(x2_spilled, 16)
            pool.wait_ge(x2_spilled, 16)
            pool.wait_ge(mm_done, B_MLP2 + 56)
            for k in range(DT):
                pool.dma_start(Xre[:, k, :], t["x_spill"][k * P:(k + 1) * P, :]).then_inc(x_landed[k], 16)
            for k in range(DT):
                pool.wait_ge(fin, k + 1)
                pool.dma_start(t["out"][k * P:(k + 1) * P, :], X[:, k, :]).then_inc(y_stored, 16)
            pool.wait_ge(y_stored, 16 * DT)

        @block.scalar
        def _(act):
            link = Link(act, act_step)

            def w_high(b, turn, slot):
                act.wait_ge(w_landed[slot], turn * 16 + 16)
                if not isinstance(b, int) or b >= 2:
                    act.wait_ge(mm_done, b - 1)
                act.activation(w_hi[:, slot, :], w_stage[:, slot, :], ACT.Copy).then_inc(w_hi_done, 1)

            def settle(done=ones_set, value=4):
                act.wait_ge(done, value)

            def next_high(b, turn, slot):
                w_high(b + 1, turn + slot, 1 - slot)

            def square_free(norm, n):
                act.wait_ge(ssq_done, n + (9 * norm + 1))

            def square(src, norm, n, waited=False):
                if not waited:
                    square_free(norm, n)
                act.activation(sqs[:, :], src, ACT.Square).then_inc(sq_done, 1)

            def one(ap, n):
                return ap[:, n:n + 1] if isinstance(n, int) else ap[:, bass.ds(n, 1)]

            def high(hi, src, cbase, n):
                settle()
                act.activation(tile(hi, n), src, ACT.Copy, scale=one(col, n + cbase)).then_inc(operand_hi, 1)

            def inverse_root(norm, users_done):
                act.wait_ge(evac_done, users_done)
                act.wait_ge(stat_done, norm + 1)
                link(act.activation(R[:, :], banks(4, 2), ACT.Ln, scale=1.0 / D, bias=eps_c))
                act.activation(R[:, :], R[:, :], ACT.Exp, scale=-0.5).then_inc(r_done, 1)

            act.wait_ge(ones_set, 4)
            act.wait_ge(p_landed, 16)
            w_high(0, 0, 0)
            for k in range(2):
                act.activation(p_hi[:, k, :], p_f[:, k, :], ACT.Copy).then_inc(operand_hi, 1)
            w_high(1, 0, 1)
            act.wait_ge(cst_landed, 32)
            for k in range(DT):
                act.wait_ge(x_landed[k], 16)
                high(opP_hi, X[:, k, :], C_ATTN, k)
                square(X[:, k, :], 0, k)
            w_high(2, 1, 0)
            inverse_root(0, 0)

            def split(b, n):
                stream(act, b, n, lambda b, turn, n, slot: next_high(b, turn, slot))

            split(B_WIN, 4)
            act.wait_ge(operand_ready, O_WOUT)
            act.wait_ge(evac_done, B_WIN + 3)
            for z in range(3):
                act.activation(LSQ[:, z, :], Z[:, z, :], ACT.Square).then_inc(m["sq"], 1)
            split(B_WIN + 4, 4)
            act.wait_ge(m["stat"], 2)
            for a, width in ((0, 256), (1, 128)):
                act.activation(LRT[:, a, :], banks(4 + 2 * a, 2), ACT.Ln, scale=1.0 / width, bias=eps_c).then_inc(m["ln"], 1)
            act.wait_ge(m["ln"], 2)
            act.activation(LRT[:, :, :], LRT[:, :, :], ACT.Exp, scale=-0.5).then_inc(m["r"], 1)
            split(B_WIN + 8, 4)
            act.wait_ge(g["lin"], 2)
            link(act.activation(E[:, :, :], KE[0][:, :, :], ACT.Abs))
            link(act.activation(E[:, :, :], E[:, :, :], ACT.Exp, scale=-1.0))
            act.activation(E[:, :, :], E[:, :, :], ACT.Ln, bias=one_c).then_inc(g["soft"], 1)
            split(B_WIN + 12, 2)
            for w in range(WIN):
                act.wait_ge(g["tr"], w + 1)
                act.activation(VT[:, w, :], ps[:, 4 + w % 2, :], ACT.Copy).then_inc(g["trc"], 1)
            split(B_WIN + 14, 2)

            act.wait_ge(g["cum"], 4)
            act.activation(E[:, :, :], Bc[:, :, :], ACT.Exp, scale=1.0 / 16).then_inc(g["exps"], 1)
            act.activation(decay.rearrange("p (a c) -> p a c", a=2),
                           Bc[:, :, :].rearrange("p a (c k) -> p a c k", k=CHUNK)[:, :, :, CHUNK - 1],
                           ACT.Exp, scale=1.0 / 16).then_inc(g["exps"], 1)
            act.wait_ge(g["kdec"], 1)
            act.activation(E[:, :, :], E[:, :, :], ACT.Exp, scale=1.0 / 16).then_inc(g["exps"], 1)
            for w in range(WIN):
                act.wait_ge(g["tr"], WIN + w + 1)
                act.activation(KDT[:, w, :], ps[:, w % 2, 0:256], ACT.Copy).then_inc(g["trc"], 1)
            for lv in range(len(LEVELS)):
                act.wait_ge(g["lexp"], 2 * lv + 2)
                act.activation(E[:, :, :], E[:, :, :], ACT.Exp, scale=1.0 / 16).then_inc(g["exps"], 1)
            act.wait_ge(g["lk"], len(LEVELS))
            for h in range(GH):
                act.activation(head_gate[h], Z[:, 12 + h, :], ACT.Sigmoid).then_inc(g["sig"], 1)

            def root_log(h):
                act.wait_ge(g["nst"], h + 1)
                act.activation(head_root[h], banks(2 * h, 2), ACT.Ln, scale=1.0 / GDV, bias=eps_c).then_inc(g["ln"], 1)

            for h in range(GH):
                act.wait_ge(g["out"], h + 1)
                act.activation(Z[:, 4 + h, :], banks(2 * h, 2), ACT.Copy).then_inc(g["oraw"], 1)
                act.wait_ge(g["oraw"], h + 1)
                if h >= 2:
                    act.wait_ge(g["nst"], h - 1)
                act.activation(SQG[:, h % 2, :], Z[:, 4 + h, :], ACT.Square).then_inc(g["sq"], 1)
                if h:
                    root_log(h - 1)
            root_log(GH - 1)
            act.wait_ge(g["ln"], GH)
            for h in range(GH):
                act.activation(head_root[h], head_root[h], ACT.Exp, scale=-0.5).then_inc(g["rn"], 1)

            def angles():
                act.wait_ge(m["angle"], 1)
                act.activation(SN[64:96, :], ang[64:96, :], ACT.Sin).then_inc(m["sin"], 1)
                link(act.activation(CT[64:96, :], ang[64:96, :], ACT.Abs))
                act.activation(CT[64:96, :], CT[64:96, :], ACT.Sin, scale=-1.0, bias=halfpi_c[64:96, :]).then_inc(m["sin"], 1)

            def evacuate(h, slot, j):
                bank, half = 6 + j % 2, slice(j % 2 * HALF, (j % 2 + 1) * HALF)
                act.wait_ge(m["job"], h * 12 + (j + 1))
                if j < 4:
                    rows = QKD if j < 2 else NOPE
                    act.activation(QK[0:rows, slot, j // 2, half], ps[0:rows, bank, :], ACT.Copy).then_inc(m["jev"], 1)
                    if j == 3:
                        act.activation(QK[64:96, slot, 1, :], Z[64:96, 3, :], ACT.Copy).then_inc(m["krot"], 1)
                        act.wait_ge(m["krot"], h + 1)
                    if j % 2 == 1:
                        act.wait_ge(m["jev"], h * 12 + (j + 1))
                        act.activation(SQ[0:QKD, j // 2, :], QK[0:QKD, slot, j // 2, :], ACT.Square).then_inc(m["sq"], 1)
                elif j < 6:
                    act.activation(VA[:, slot, 4 * (j - 4):4 * (j - 3), 64 * slot:64 * slot + 64],
                                   ps[:, bank, 0:256].rearrange("p (a b) -> p a b", a=4), ACT.Copy).then_inc(m["jev"], 1)
                else:
                    a = (j - 6) // 2
                    act.activation(RR[0:QKD, a, half], ps[0:QKD, bank, :], ACT.Ln, scale=1.0 / QKD, bias=eps_c[0:QKD, :])\
                       .then_inc(m["jev"], 1)
                    if j == 9:
                        act.wait_ge(m["jev"], h * 12 + 10)
                        act.activation(RR[0:QKD, :, :], RR[0:QKD, :, :], ACT.Exp, scale=-0.5).then_inc(m["rr"], 1)

            def rows_in(h, slot, more, r):
                act.wait_ge(m["job"], h * 12 + (12 + (10 if more else 0) + r + 1))
                act.activation(QK[96:97, slot, 0, r * HALF:(r + 1) * HALF], ps[0:1, 6 + r, :], ACT.Copy).then_inc(m["jev"], 1)

            def head(h, slot, more):
                if more:
                    for j in range(10):
                        evacuate(h + 1, 1 - slot, j)
                for r in range(2):
                    rows_in(h, slot, more, r)
                for u, (half, kt, q0, width) in enumerate(PIECES_T):
                    act.wait_ge(m["st"], h * 12 + (u + 2))
                    act.wait_ge(m["pv"], h * 12 + (u + 1))
                    act.activation(PT[:, u % 4, 0:width], ps[:, 2 + u % 2, 0:width], ACT.Exp, scale=1.0 / math.sqrt(QKD))\
                       .then_inc(m["exp"], 1)

            act.sem_inc(m["exp"], 2)
            act.wait_ge(g["gated"], GH)
            for j in range(10):
                evacuate(0, 0, j)
            angles()
            act.wait_ge(g["fin"], GH)
            for k in range(4):
                act.activation(opP_hi[:, 4 + k, :], Z[:, 12 + k, :], ACT.Copy).then_inc(operand_hi, 1)
            act.wait_ge(m["jev"], 10)
            act.sem_inc(m["jev"], 2)
            head(0, 0, True)
            with act.Fori(0, 3) as i:
                head(i * 2 + 1, 1, True)
                head(i * 2 + 2, 0, True)
            head(7, 1, False)

            act.wait_ge(m["rope"], MH)
            for k in range(4):
                act.wait_ge(m["ofree"], 4 * k + 6)
                act.activation(opP_hi[:, k, :], Z[:, 8 + k, :], ACT.Copy).then_inc(operand_hi, 1)

            def wout_step(b, turn, n, slot):
                next_high(b, turn, slot)
                act.wait_ge(evac_done, b + 1)
                square_free(1, n)
                high(opQ_hi, tile(X, n), C_MLP, n)
                square(tile(X, n), 1, n, True)
            act.wait_ge(operand_ready, O_UP1)
            stream(act, B_WOUT, 8, wout_step)
            inverse_root(1, B_MLP1)

            def mlp(b0, hi, count0, down_last, last_group_steps):
                def up(gi):
                    def body(b, turn, n, slot):
                        next_high(b, turn, slot)
                        act.wait_ge(relu_sq, gi * 8 + n + (count0 + 1))
                        settle()
                        act.activation(tile(hi, n), T[:, slot, :], ACT.Copy).then_inc(operand_hi, 1)
                    return body

                def group(gi, down):
                    for n_blocks, off, body in ((8, 0, up(gi)), (8, 8, down)):
                        with act.Fori(0, n_blocks // 2) as i:
                            for j in range(2):
                                body(gi * 16 + i * 2 + (b0 + off + j), gi * 8 + i + (b0 + off) // 2, i * 2 + j, j)
                with act.Fori(0, 3) as gi:
                    group(gi, lambda b, turn, n, slot: next_high(b, turn, slot))
                with act.Fori(0, 4) as i:
                    for j in range(2):
                        up(3)(i * 2 + (b0 + 48 + j), i + (b0 + 48) // 2, i * 2 + j, j)
                last_group_steps()

            def down1():
                def body(b, turn, n, slot):
                    next_high(b, turn, slot)
                    act.wait_ge(evac_done, b + 1)
                    square_free(2, n)
                    high(opQ_hi, tile(X, n), C_PLE, n)
                    square(tile(X, n), 2, n, True)
                stream(act, B_MLP1 + 56, 8, body)

            mlp(B_MLP1, opP_hi, 0, None, down1)
            inverse_root(2, B_GATE)

            def gate_step(b, turn, n, slot):
                next_high(b, turn, slot)
                act.wait_ge(evac_done, b + 1)
                settle()
                act.activation(T[:, 0, :], T[:, 0, :], ACT.Sigmoid, bias=one(col, n + C_BPLE)).then_inc(gated, 1)
                act.wait_ge(x_upd, n + 1)
                square_free(3, n)
                high(opP_hi, tile(X, n), C_MIXPRE, n)
                square(tile(X, n), 3, n, True)
            stream(act, B_GATE, 8, gate_step)
            inverse_root(3, B_WIN2)

            def win2_step(b, turn, n, slot):
                next_high(b, turn, slot)
                act.wait_ge(evac_done, b + 1)
                settle()
                act.activation(tile(Z2, n), tile(Z2, n), ACT.Identity, bias=one(col, n + C_BIN)).then_inc(s["z"], 1)
            stream(act, B_WIN2, 10, win2_step)

            act.wait_ge(s["spill"], 16)
            for gi in range(4):
                act.wait_ge(s["pmm"], gi + 1)
                act.activation(X[:, gi, :], banks(2 * (gi % 2), 2), ACT.Copy,
                               scale=col[:, C_POOLS + gi:C_POOLS + gi + 1]).then_inc(s["y"], 1)
            for w in range(2):
                act.wait_ge(s["vtr"], w + 1)
                act.activation(vpad[:, 1 + 4 * w:5 + 4 * w, :].rearrange("p a b -> p (a b)"), ps[:, 4 + w, :], ACT.Copy)\
                   .then_inc(s["vtc"], 1)
            act.wait_ge(s["rope"], 2)
            act.wait_ge(r_done, 4)

            def blocks_in(n, slot):
                if not isinstance(n, int) or n >= 2:
                    act.wait_ge(s["qk"], n - 1)
                cols = bass.ds(n * P, P)
                settle()
                act.activation(qb2[:, slot, :, :], Z2[:, 4:8, cols], ACT.Copy).then_inc(s["blk"], 1)
                act.activation(kb2[:, slot, :], kpad[:, bass.ds(n * P, 2 * P)], ACT.Copy).then_inc(s["blk"], 1)

            def attend(n, slot, more):
                if more:
                    blocks_in(n + 1, 1 - slot)
                act.wait_ge(s["mx"], n + 1)
                if not isinstance(n, int) or n >= 1:
                    act.wait_ge(s["trb"], n)
                    act.wait_ge(s["den"], n)
                for h in range(NQ):
                    act.activation(P2[:, h, :], S2[:, h, :], ACT.Exp, bias=nm8[:, h:h + 1], accum_out=d8[:, h:h + 1])\
                       .then_inc(s["exp"], 1)
                act.activation(e8, m8, ACT.Exp).then_inc(s["exp"], 1)
                for name, half in (("tra", 0), ("trb", 1)):
                    act.wait_ge(s[name], n + 1)
                    if half == 0 and (not isinstance(n, int) or n >= 1):
                        act.wait_ge(s["pv"], n)
                    act.activation(PT2[:, 4 * half:4 * half + 4, :, :].rearrange("p a b c -> p (a b c)"), banks(4, 2), ACT.Copy)\
                       .then_inc(s["tca" if half == 0 else "tcb"], 1)
                act.wait_ge(s["otr"], n + 1)
                settle()
                act.activation(X[:, 4:8, bass.ds(n * P, P)], ps[:, 6, :].rearrange("p (a b) -> p a b", a=4), ACT.Copy)\
                   .then_inc(s["otc"], 1)

            blocks_in(0, 0)
            attend(0, 0, True)
            with act.Fori(0, 3) as i:
                attend(i * 2 + 1, 1, True)
                attend(i * 2 + 2, 0, True)
            attend(7, 1, False)

            act.wait_ge(s["y"], 4)
            act.wait_ge(s["otc"], 8)
            for k in range(DT):
                act.activation(opQ_hi[:, k, :], X[:, k, :], ACT.Copy).then_inc(operand_hi, 1)

            act.wait_ge(operand_ready, O_WO2)
            with act.Fori(0, 4) as i:
                for j in range(2):
                    for q in range(3):
                        o = 3 * j + q
                        next_high(i * 6 + (B_MRG + o), i * 3 + (B_MRG + o) // 2, o % 2)
                        if q < 2:
                            act.wait_ge(evac_done, i * 6 + (B_MRG + o + 1))
                            settle()
                            act.activation(T[:, q, :], T[:, q, :], ACT.Sigmoid,
                                           bias=one(col, i * 2 + (C_BIN + 10 + 8 * q + j))).then_inc(s["sig"], 1)

            for k in range(DT):
                act.wait_ge(s["mrg"], k + 2)
                if k == 0:
                    act.wait_ge(mm_done, B_WO2)
                act.activation(opQ_hi[:, k, :], X[:, k, :], ACT.Copy).then_inc(operand_hi, 1)

            def wo2_step(b, turn, n, slot):
                next_high(b, turn, slot)
                act.wait_ge(evac_done, b + 1)
                square(tile(X, n), 4, n)
            act.wait_ge(operand_ready, O_UP2)
            stream(act, B_WO2, 8, wo2_step)
            inverse_root(4, B_MLP2)
            for k in range(DT):
                act.wait_ge(s["mt"], k + 1)
                high(opP_hi, X[:, k, :], C_MLPPRE, k)
                square(X[:, k, :], 5, k)
            act.wait_ge(s["mt"], DT)
            inverse_root(5, B_MLP2)

            def down2():
                def body(b, turn, n, slot):
                    next_high(b, turn, slot)
                    act.wait_ge(evac_done, b + 1)
                    square(tile(X, n), 6, n)
                stream(act, B_MLP2 + 56, 6, body)
                body(B_END - 2, B_END // 2 - 1, 6, 0)
                act.wait_ge(evac_done, B_END)
                square(X[:, 7, :], 6, 7)

            mlp(B_MLP2, opQ_hi, 32, None, down2)
            inverse_root(6, B_END)

        @block.vector
        def _(v):
            link = Link(v, dve_step)

            def w_low(b, turn, slot):
                v.wait_ge(w_hi_done, b + 1)
                v.tensor_tensor(w_lo[:, slot, :], w_stage[:, slot, :], w_hi[:, slot, :].bitcast(F32), ALU.subtract)\
                 .then_inc(w_lo_done, 1)

            def next_low(b, turn, slot):
                w_low(b + 1, turn, 1 - slot)

            def one(ap, n):
                return ap[:, n:n + 1] if isinstance(n, int) else ap[:, bass.ds(n, 1)]

            def low(hi, lo, src, count, n, cbase=None):
                v.wait_ge(operand_hi, n + (count + 1))
                h = tile(hi, n).bitcast(F32)
                if cbase is None:
                    ins = v.tensor_tensor(tile(lo, n), src, h, ALU.subtract)
                else:
                    ins = v.scalar_tensor_tensor(tile(lo, n), src, one(col, n + cbase), h, ALU.mult, ALU.subtract)
                ins.then_inc(operand_ready, 1)

            def add_square(norm, n):
                v.wait_ge(ssq_done, n + (9 * norm + 1))
                v.wait_ge(sq_done, n + (8 * norm + 1))
                v.tensor_tensor(ssq[:, :], ssq[:, :], sqs[:, :], ALU.add).then_inc(ssq_done, 1)

            def zero_squares(norm):
                if norm:
                    v.wait_ge(stat_done, norm)
                v.memset(ssq[:, :], 0.0).then_inc(ssq_done, 1)

            zero_squares(0)
            w_low(0, 0, 0)
            for k in range(2):
                low(p_hi, p_lo, p_f[:, k, :], O_PP, k)
            w_low(1, 0, 1)
            v.wait_ge(cst_landed, 32)
            for k in range(DT):
                low(opP_hi, opP_lo, X[:, k, :], O_WIN, k, C_ATTN)
                add_square(0, k)
            w_low(2, 1, 0)
            for n in range(DT):
                v.wait_ge(pp_mm, n + 1)
                v.tensor_copy(ppout[:, n, :], banks(2 * (n % 4), 2)).then_inc(pp_evac, 1)
            v.wait_ge(pp_evac, 8)
            v.sem_inc(evac_done, 2)

            v.wait_ge(r_done, 1)
            v.wait_ge(pp_spilled, 16)

            def win_step(b, turn, n, slot):
                next_low(b, turn, slot)
                v.wait_ge(mm_done, b + 1)
                v.tensor_tensor(tile(Z, n), banks(2 * slot, 2), R[:, :], ALU.mult).then_inc(evac_done, 1)
            stream(v, B_WIN, 4, win_step)
            v.wait_ge(m["sq"], 2)
            v.tensor_tensor(LSQ[:, 0, :], LSQ[:, 0, :], LSQ[:, 1, :], ALU.add).then_inc(m["lat"], 1)
            stream(v, B_WIN + 4, 4, win_step, 4)
            v.wait_ge(m["r"], 1)
            v.wait_ge(evac_done, B_WIN + 3)
            for z in range(3):
                v.scalar_tensor_tensor(Z[:, z, :], Z[:, z, :], col[:, C_QN + z:C_QN + z + 1], LRT[:, z // 2, :],
                                       ALU.mult, ALU.mult).then_inc(m["lat"], 1)
            stream(v, B_WIN + 8, 4, win_step, 8)
            v.wait_ge(g["logit"], 2)
            for pr in range(2):
                v.tensor_scalar(KE[0][:, pr, :], banks(4 + 2 * pr, 2), col[:, C_GATEB + pr:C_GATEB + pr + 1], None,
                                ALU.add).then_inc(g["lin"], 1)
            stream(v, B_WIN + 12, 2, win_step, 12)
            v.wait_ge(g["soft"], 1)
            kef = KE[0][:, :, :].rearrange("p a b -> p (a b)")
            v.wait_ge(g["lin"], 2)
            link(v.scalar_tensor_tensor(kef, kef, 0.0, E[:, :, :].rearrange("p a b -> p (a b)"), ALU.min, ALU.subtract))
            v.wait_ge(m["lat"], 4)
            v.wait_ge(g["cum"], 1)
            for pr in range(2):
                v.tensor_tensor_scan(Bc[:, pr, :], reset[:, :], KE[0][:, pr, :], 0.0, ALU.mult, ALU.add).then_inc(g["cum"], 1)
            v.wait_ge(g["cum"], 3)
            v.sem_inc(g["cum"], 1)
            stream(v, B_WIN + 14, 2, win_step, 14)

            v.wait_ge(evac_done, B_WOUT)
            q_t, k_t = Z[:, 4:6, :], Z[:, 6:8, :]
            chunks = [P, 2 * NCH, CHUNK]
            Bf = Bc[:, :, :].rearrange("p a (c k) -> p (a c) k", k=CHUNK)
            Ef = E[:, :, :].rearrange("p a (c k) -> p (a c) k", k=CHUNK)
            v.wait_ge(g["exps"], 2)
            v.scalar_tensor_tensor(QX[:, :, :].rearrange("p a b -> p (a b)"), q_t.rearrange("p a b -> p (a b)"),
                                   GDK ** -0.5, E[:, :, :].rearrange("p a b -> p (a b)"), ALU.mult, ALU.mult)\
             .then_inc(g["states"], 1)
            v.wait_ge(g["states"], 1)
            v.tensor_tensor(Ef, bc(Bf[:, :, CHUNK - 1:CHUNK], chunks), Bf, ALU.subtract).then_inc(g["kdec"], 1)

            def diagonal(hf):
                v.wait_ge(g["lmm"], hf + 1)
                v.tensor_tensor(SC[:, hf, :, :, :].rearrange("p a w t -> p (a w) t"),
                                banks(4 * hf, 4).rearrange("p (x t) -> p x t", t=P),
                                bc(dmask[:, :].unsqueeze(1), [P, 2 * WIN, P]), ALU.mult).then_inc(g["lcp"], 1)
            v.wait_ge(g["consts"], 32)
            diagonal(0)
            v.wait_ge(g["exps"], 3)
            v.tensor_tensor(KE[0][:, :, :], k_t, E[:, :, :], ALU.mult).then_inc(g["kdec"], 1)
            diagonal(1)
            for pr in range(2):
                v.memset(ST8[:, pr, 0, :], 0.0).then_inc(g["states"], 1)

            def states(pr):
                v.wait_ge(g["upd"], pr + 1)
                for c in range(NCH - 1):
                    v.wait_ge(g["states"], 3 + pr * 15 + c if c else 3)
                    bank = 4 + 2 * (c % 2) + (c // 2) // 4
                    u = ps[:, bank, ((c // 2) % 4) * P:((c // 2) % 4 + 1) * P]
                    v.scalar_tensor_tensor(ST8[:, pr, c + 1, :], ST8[:, pr, c, :], decay[:, pr * NCH + c:pr * NCH + c + 1],
                                           u, ALU.mult, ALU.add).then_inc(g["states"], 1)

            def exponents(lv):
                size = LEVELS[lv]
                nodes = 2 * S // (2 * size)
                Bn = Bc[:, :, :].rearrange("p a b -> p (a b)").rearrange("p (n s l) -> p n s l", s=2, l=size)
                En = E[:, :, :].rearrange("p a b -> p (a b)").rearrange("p (n s l) -> p n s l", s=2, l=size)
                mid = bc(Bn[:, :, 0, size - 1:size], [P, nodes, size])
                if lv:
                    v.wait_ge(g["lk"], lv)
                else:
                    v.wait_ge(g["kdec"], 2)
                v.tensor_tensor(En[:, :, 1, :], Bn[:, :, 1, :], mid, ALU.subtract).then_inc(g["lexp"], 1)
                v.tensor_tensor(En[:, :, 0, :], mid, Bn[:, :, 0, :], ALU.subtract).then_inc(g["lexp"], 1)

            def factors(lv):
                size = LEVELS[lv]
                En = E[:, :, :].rearrange("p a b -> p (a b)").rearrange("p (n s l) -> p n s l", s=2, l=size)
                qn = q_t.rearrange("p a b -> p (a b)").rearrange("p (n s l) -> p n s l", s=2, l=size)
                v.wait_ge(g["exps"], 4 + lv)
                if lv == 0:
                    v.wait_ge(g["tr"], 2 * WIN)
                if lv >= 2:
                    v.wait_ge(g["lmm"], 2 * lv)
                v.scalar_tensor_tensor(QE[lv % 2][:, :].rearrange("p (n l) -> p n l", l=size), qn[:, :, 1, :],
                                       GDK ** -0.5, En[:, :, 1, :], ALU.mult, ALU.mult).then_inc(g["lq"], 1)
                v.tensor_tensor(KE[lv % 2][:, :, :], k_t, E[:, :, :], ALU.mult).then_inc(g["lk"], 1)

            def merge(lv, par):
                size = LEVELS[lv]
                v.wait_ge(g["lmm"], 3 + 2 * lv + par)
                v.wait_ge(g["lcp"], 2 + 2 * lv + par)
                right = SC[:, par, :, :, :].rearrange("p b w t -> p (b w) t").rearrange(
                    "p x (n s l) -> p x n s l", s=2, l=size)[:, :, :, 1, :]
                msk = bc(lmask[:, lv:lv + 1, :].rearrange("p a (n l) -> p a n l", l=size), [P, 2 * WIN, CHUNK // size, size])
                v.copy_predicated(right, msk, banks(2 * par, 2).rearrange("p (x n l) -> p x n l", x=2 * WIN, l=size))\
                 .then_inc(g["lcp"], 1)

            last = len(LEVELS) - 1
            exponents(0)
            factors(0)
            states(0)
            for lv in range(len(LEVELS)):
                if lv < last:
                    exponents(lv + 1)
                merge(lv, 0)
                if lv < last:
                    factors(lv + 1)
                merge(lv, 1)
                if lv == 0:
                    states(1)
            for h in range(GH):
                gr = Z[:, 12 + h, :]
                v.wait_ge(g["sig"], h + 1)
                v.tensor_tensor(gr, gr, head_gate[h], ALU.mult).then_inc(g["gated"], 1)
            for h in range(GH):
                o, gr = Z[:, 4 + h, :], Z[:, 12 + h, :]
                v.wait_ge(g["rn"], h + 1)
                link(v.scalar_tensor_tensor(o, o, col[:, C_GOUT:C_GOUT + 1], head_root[h], ALU.mult, ALU.mult))
                v.wait_ge(g["gated"], h + 1)
                v.tensor_tensor(gr, gr, o, ALU.mult).then_inc(g["fin"], 1)

            v.wait_ge(m["misc"], 48)
            v.wait_ge(m["job"], 10)
            rows = slice(64, 96)
            link(v.tensor_copy(ang[rows, :], pos_i[rows, :]))
            link(v.tensor_scalar(ang[rows, :], ang[rows, :], freq[rows, :], None, ALU.mult))
            link(v.tensor_scalar(kf[rows, :], ang[rows, :], 1.0 / (2 * math.pi), None, ALU.mult))
            link(v.tensor_copy(ki[rows, :], kf[rows, :]))
            link(v.tensor_copy(kf[rows, :], ki[rows, :]))
            c1 = 6.28125
            c2 = float(np.float32(np.round((2 * math.pi - c1) * 2 ** 20) / 2 ** 20))
            c3 = 2 * math.pi - c1 - c2
            for c in (c1, c2, c3):
                link(v.scalar_tensor_tensor(ang[rows, :], kf[rows, :], -c, ang[rows, :], ALU.mult, ALU.add))
            pi32 = float(np.nextafter(np.float32(math.pi), np.float32(0)))
            v.tensor_scalar(ang[rows, :], ang[rows, :], pi32, -pi32, ALU.min, ALU.max).then_inc(m["angle"], 1)
            v.wait_ge(m["sin"], 2)
            v.tensor_scalar(SN[rows, :], SN[rows, :], sgn[rows, :], None, ALU.mult).then_inc(m["tab"], 1)
            v.sem_inc(m["tab"], 1)

            def normalise(h, slot):
                v.wait_ge(m["rr"], h + 1)
                for a in range(2):
                    qk = QK[0:QKD, slot, a, :]
                    gain = col[0:QKD, C_QKQ + a:C_QKQ + a + 1]
                    v.scalar_tensor_tensor(qk, qk, gain, RR[0:QKD, a, :], ALU.mult, ALU.mult).then_inc(m["nrm"], 1)

            def rotate(h, slot):
                qk = QK[rows, slot, :, :]
                v.wait_ge(m["nrm"], h * 2 + 2)
                v.wait_ge(m["swap"], h * 32 + 32)
                v.tensor_tensor(qk, qk, bc(CT[rows, :].unsqueeze(1), [ROPE, 2, S]), ALU.mult).then_inc(m["angle"], 1)
                v.wait_ge(m["angle"], h + 2)
                v.wait_ge(m["swn"], h + 1)
                v.tensor_tensor(qk, qk, SW[rows, :, :], ALU.add).then_inc(m["rope"], 1)

            def maximum(h, u):
                qt, c0, width = PIECES[u]
                sc = ps[:, u % 2, 0:width]
                v.wait_ge(m["scores"], h * 12 + (u + 1))
                if c0 + width == (qt + 1) * P:
                    v.memset(sc[0:64, width - 64:width], NEG).then_inc(m["corner"], 1)
                    v.wait_ge(m["corner"], h * 8 + (qt + 1))
                dst = mx8[:, qt:qt + 1] if c0 == 0 else mxb[:, qt - 4:qt - 3]
                v.tensor_reduce(dst, sc, AX_X, ALU.max).then_inc(m["red"], 1)

            def output(h, n, slot, half):
                o, sums = slice(64 * slot, 64 * slot + 64), slice(64 - 64 * slot, 128 - 64 * slot)
                v.wait_ge(m["pv"], h * 12 + (8 if half == 0 else 16))
                v.wait_ge(m["ofree"], h * 2 + (2 + half))
                v.reciprocal(T[o, half, 0:HALF], ps[sums, 4 + half, :]).then_inc(m["inv"], 1)
                v.wait_ge(m["inv"], h * 2 + (1 + half))
                dst = Z[o, 8 + n, half * HALF:(half + 1) * HALF] if isinstance(n, int) else \
                    Z[o, bass.ds(n + 8, 1), half * HALF:(half + 1) * HALF].rearrange("p a b -> p (a b)")
                v.tensor_tensor(dst, ps[o, 4 + half, :], T[o, half, 0:HALF], ALU.mult).then_inc(m["ofree"], 1)

            def head(h, n, n_before, slot, first, more):
                for u in range(12):
                    maximum(h, u)
                    if u == 3:
                        v.wait_ge(m["red"], h * 12 + 6)
                        v.sem_inc(m["mx"], 1)
                    if u == 5 and not first:
                        output(h - 1, n_before, 1 - slot, 1)
                v.wait_ge(m["red"], h * 12 + 14)
                v.tensor_tensor(mx8[:, 4:8], mx8[:, 4:8], mxb, ALU.max).then_inc(m["mx"], 1)
                if more:
                    normalise(h + 1, 1 - slot)
                output(h, n, slot, 0)
                if more:
                    rotate(h + 1, 1 - slot)

            v.sem_inc(m["red"], 2)
            v.sem_inc(m["ofree"], 2)
            v.wait_ge(m["lat"], 4)
            normalise(0, 0)
            rotate(0, 0)
            for k in range(4):
                v.wait_ge(operand_hi, O_WOUT + k + 1)
                v.tensor_tensor(opP_lo[:, 4 + k, :], Z[:, 12 + k, :], opP_hi[:, 4 + k, :].bitcast(F32), ALU.subtract)\
                 .then_inc(operand_ready, 1)
            head(0, 0, None, 0, True, True)
            with v.Fori(0, 3) as i:
                head(i * 2 + 1, i, i, 1, False, True)
                head(i * 2 + 2, i + 1, i, 0, False, True)
            head(7, 3, 3, 1, False, False)
            output(7, 3, 1, 1)

            for k in range(4):
                v.wait_ge(operand_hi, O_WOUT + 5 + k)
                v.tensor_tensor(opP_lo[:, k, :], Z[:, 8 + k, :], opP_hi[:, k, :].bitcast(F32), ALU.subtract)\
                 .then_inc(operand_ready, 1)
            zero_squares(1)

            def wout_step(b, turn, n, slot):
                next_low(b, turn, slot)
                v.wait_ge(mm_done, b + 1)
                v.wait_ge(x_back[slot], turn * 16 - (B_WOUT * 8 - 16))
                v.tensor_tensor(tile(X, n), tile(X, n), banks(2 * slot, 2), ALU.add).then_inc(evac_done, 1)
                v.wait_ge(evac_done, b + 1)
                low(opQ_hi, opQ_lo, tile(X, n), O_UP1, n, C_MLP)
                add_square(1, n)
            stream(v, B_WOUT, 8, wout_step)

            def mlp(b0, norm, hi, lo, count0, ready0, down, last):
                v.wait_ge(r_done, norm + 1)

                def up(gi):
                    def body(b, turn, n, slot):
                        next_low(b, turn, slot)
                        v.wait_ge(mm_done, b + 1)
                        v.wait_ge(operand_hi, gi * 8 + n + (ready0 - 1))
                        tt = T[:, slot, :]
                        v.tensor_tensor(tt, banks(2 * slot, 2), R[:, :], ALU.mult).then_inc(evac_done, 1)
                        v.wait_ge(evac_done, b + 1)
                        v.scalar_tensor_tensor(tt, tt, 0.0, tt, ALU.max, ALU.mult).then_inc(relu_sq, 1)
                        v.wait_ge(relu_sq, gi * 8 + n + (count0 + 1))
                        v.wait_ge(operand_hi, gi * 8 + n + (ready0 + 1))
                        v.tensor_tensor(tile(lo, n), tt, tile(hi, n).bitcast(F32), ALU.subtract).then_inc(operand_ready, 1)
                    return body

                def run(gi, off, body, turns=4):
                    with v.Fori(0, turns) as i:
                        for j in range(2):
                            body(gi * 16 + i * 2 + (b0 + off + j), gi * 8 + i + (b0 + off) // 2, i * 2 + j, j)
                if down is not None:
                    with v.Fori(0, 3) as gi:
                        run(gi, 0, up(gi))
                        run(gi, 8, down)
                else:
                    run(0, 0, up(0))
                    v.wait_ge(x2_spilled, 16)
                    run(0, 8, first_down)
                    with v.Fori(1, 3) as gi:
                        run(gi, 0, up(gi))
                        run(gi, 8, acc_down)
                run(3, 0, up(3))
                zero_squares(2 if down is not None else 6)
                last()

            def acc_down(b, turn, n, slot):
                next_low(b, turn, slot)
                v.wait_ge(mm_done, b + 1)
                v.tensor_tensor(tile(X, n), tile(X, n), banks(2 * slot, 2), ALU.add).then_inc(evac_done, 1)

            def first_down(b, turn, n, slot):
                next_low(b, turn, slot)
                v.wait_ge(mm_done, b + 1)
                v.tensor_copy(tile(X, n), banks(2 * slot, 2)).then_inc(evac_done, 1)

            def down1():
                def body(b, turn, n, slot):
                    acc_down(b, turn, n, slot)
                    v.wait_ge(evac_done, b + 1)
                    low(opQ_hi, opQ_lo, tile(X, n), O_GATE, n, C_PLE)
                    add_square(2, n)
                stream(v, B_MLP1 + 56, 8, body)

            mlp(B_MLP1, 1, opP_hi, opP_lo, 0, O_H1, acc_down, down1)

            zero_squares(3)
            v.wait_ge(r_done, 3)

            def gate_step(b, turn, n, slot):
                next_low(b, turn, slot)
                v.wait_ge(mm_done, b + 1)
                v.tensor_tensor(T[:, 0, :], banks(2 * slot, 2), R[:, :], ALU.mult).then_inc(evac_done, 1)
                v.wait_ge(gated, n + 1)
                v.wait_ge(pp_back, n * 16 + 16)
                v.tensor_tensor(T[:, 0, :], T[:, 0, :], T[:, 1, :], ALU.mult).then_inc(pp_used, 1)
                v.wait_ge(pp_used, n + 1)
                v.tensor_tensor(tile(X, n), tile(X, n), T[:, 0, :], ALU.add).then_inc(x_upd, 1)
                v.wait_ge(x_upd, n + 1)
                low(opP_hi, opP_lo, tile(X, n), O_WIN2, n, C_MIXPRE)
                add_square(3, n)
            stream(v, B_GATE, 8, gate_step)

            v.wait_ge(r_done, 4)
            v.wait_ge(mm_done, B_WIN2)

            def win2_step(b, turn, n, slot):
                next_low(b, turn, slot)
                v.wait_ge(mm_done, b + 1)
                v.tensor_tensor(tile(Z2, n), banks(2 * slot, 2), R[:, :], ALU.mult).then_inc(evac_done, 1)
            stream(v, B_WIN2, 10, win2_step)

            v.wait_ge(s["consts"], 64)
            for gi, width in enumerate(POOL_W):
                v.wait_ge(s["z"], gi + 1)
                u = Z2[:, gi, :]
                src, step, slot = u, 1, 0
                while step < width:
                    dst = T[:, slot, :]
                    v.tensor_copy(dst[:, 0:step], src[:, 0:step]).then_inc(dve_step, 1)
                    link.n += 1
                    link(v.tensor_tensor(dst[:, step:S], src[:, step:S], src[:, 0:S - step], ALU.add))
                    src, step, slot = dst, step * 2, 1 - slot
                head = T[:, slot, 0:16]
                link(v.tensor_tensor(head, src[:, 0:16], icnt[:, gi, :], ALU.mult))
                link(v.scalar_tensor_tensor(src[:, 16:S], src[:, 16:S], 1.0 / width, u[:, 16:S], ALU.mult, ALU.subtract))
                link(v.tensor_tensor(src[:, 0:16], head, u[:, 0:16], ALU.subtract))
                v.tensor_copy(u, src).then_inc(s["pool"], 1)
                v.wait_ge(s["pool"], gi + 1)
            for a, (z, sw) in enumerate(((Z2[:, 4:8, :], swq[:, :, :]), (Z2[:, 8:9, :], swk[:, :].unsqueeze(1)))):
                n = 4 if a == 0 else 1
                v.wait_ge(s["swap"], 128)
                v.tensor_tensor(sw, sw, bc(tabS[:, :].unsqueeze(1), [P, n, S]), ALU.mult).then_inc(dve_step, 1)
                link.n += 1
                link(v.tensor_tensor(z, z, bc(tabC[:, :].unsqueeze(1), [P, n, S]), ALU.mult))
                if a == 0:
                    v.tensor_tensor(z, z, sw, ALU.add).then_inc(s["rope"], 1)
                else:
                    v.wait_ge(s["zero"], 1)
                    v.tensor_tensor(kpad[:, P:P + S], Z2[:, 8, :], swk[:, :], ALU.add).then_inc(s["rope"], 1)
            v.wait_ge(s["rope"], 2)
            v.wait_ge(s["consts"], 80)

            sink = col[:, C_SINK:C_SINK + NQ]

            def attend(n, slot, first):
                v.wait_ge(s["qk"], n + 1)
                if not isinstance(n, int) or n >= 1:
                    v.wait_ge(s["exp"], n * 9)
                mk = mask2[:, 0 if first else 1, :]
                v.scalar_tensor_tensor(S2[:, :, :], banks(0, 4).rearrange("p (h k) -> p h k", k=256), HD ** -0.5,
                                       bc(mk.unsqueeze(1), [P, NQ, 256]), ALU.mult, ALU.add).then_inc(s["sc"], 1)
                v.wait_ge(s["sc"], n * 5 + 1)
                v.tensor_reduce(m8, S2[:, :, :], AX_X, ALU.max).then_inc(s["sc"], 1)
                v.wait_ge(s["sc"], n * 5 + 2)
                v.tensor_tensor(m8, m8, sink, ALU.max).then_inc(s["sc"], 1)
                v.wait_ge(s["sc"], n * 5 + 3)
                v.tensor_scalar(nm8, m8, -1.0, None, ALU.mult).then_inc(s["sc"], 1)
                v.wait_ge(s["sc"], n * 5 + 4)
                v.tensor_tensor(m8, sink, m8, ALU.subtract).then_inc(s["mx"], 1)
                v.wait_ge(s["exp"], n * 9 + 9)
                v.tensor_tensor(r8, d8, e8, ALU.add).then_inc(s["sc"], 1)
                v.wait_ge(s["sc"], n * 5 + 5)
                v.reciprocal(r8, r8).then_inc(s["den"], 1)
                v.wait_ge(s["den"], n + 1)
                v.wait_ge(s["pv"], n + 1)
                if not isinstance(n, int) or n >= 1:
                    v.wait_ge(s["otr"], n)
                v.tensor_tensor(O2[:, :].rearrange("p (h d) -> p h d", d=HD), ps[:, 7, :].rearrange("p (h d) -> p h d", d=HD),
                                bc(r8.unsqueeze(2), [P, NQ, HD]), ALU.mult).then_inc(s["on"], 1)
            attend(0, 0, True)
            with v.Fori(0, 7) as i:
                attend(i + 1, 0, False)

            v.wait_ge(s["otc"], 8)
            for k in range(DT):
                low(opQ_hi, opQ_lo, X[:, k, :], O_Y, k)

            v.sem_inc(s["mrg"], 1)
            with v.Fori(0, 4) as i:
                for j in range(2):
                    n = i * 2 + j
                    for q in range(2):
                        o = 3 * j + q
                        b = i * 6 + (B_MRG + o)
                        next_low(b, None, o % 2)
                        v.wait_ge(mm_done, b + 1)
                        v.wait_ge(s["mrg"], n + 1)
                        v.tensor_tensor(T[:, q, :], banks(2 * (o % 2), 2), R[:, :], ALU.mult).then_inc(evac_done, 1)
                    o = 3 * j + 2
                    b = i * 6 + (B_MRG + o)
                    next_low(b, None, o % 2)
                    v.wait_ge(mm_done, b + 1)
                    v.wait_ge(s["sig"], n * 2 + 2)
                    v.tensor_tensor(T[:, 0, :], T[:, 0, :], banks(4, 2), ALU.mult).then_inc(s["ptmp"], 1)
                    v.tensor_tensor(T[:, 1, :], T[:, 1, :], banks(6, 2), ALU.mult).then_inc(s["ptmp"], 1)
                    v.wait_ge(s["ptmp"], n * 2 + 2)
                    v.sem_inc(evac_done, 1)
                    v.tensor_tensor(tile(X, n), T[:, 0, :], T[:, 1, :], ALU.add).then_inc(s["mrg"], 1)
            v.wait_ge(s["mrg"], DT + 1)
            for k in range(DT):
                low(opQ_hi, opQ_lo, X[:, k, :], O_WO2, k)
            zero_squares(4)

            def wo2_step(b, turn, n, slot):
                next_low(b, turn, slot)
                v.wait_ge(mm_done, b + 1)
                v.tensor_copy(tile(X, n), banks(2 * slot, 2)).then_inc(evac_done, 1)
                add_square(4, n)
            stream(v, B_WO2, 8, wo2_step)
            zero_squares(5)
            v.wait_ge(r_done, 5)
            v.wait_ge(evac_done, B_MLP2)
            for k in range(DT):
                v.scalar_tensor_tensor(X[:, k, :], X[:, k, :], col[:, C_MIXPOST + k:C_MIXPOST + k + 1], R[:, :],
                                       ALU.mult, ALU.mult).then_inc(dve_step, 1)
                link.n += 1
                v.wait_ge(dve_step, link.n)
                v.wait_ge(x_landed[k], 32)
                v.tensor_tensor(X[:, k, :], X[:, k, :], Xre[:, k, :], ALU.add).then_inc(s["mt"], 1)
                v.wait_ge(s["mt"], k + 1)
                low(opP_hi, opP_lo, X[:, k, :], O_UP2, k, C_MLPPRE)
                add_square(5, k)

            def down2():
                def body(b, turn, n, slot):
                    acc_down(b, turn, n, slot)
                    add_square(6, n)
                stream(v, B_MLP2 + 56, 6, body)
                body(B_END - 2, B_END // 2 - 1, 6, 0)
                v.wait_ge(mm_done, B_END)
                v.tensor_tensor(X[:, 7, :], X[:, 7, :], banks(2, 2), ALU.add).then_inc(evac_done, 1)
                add_square(6, 7)

            mlp(B_MLP2, 5, opQ_hi, opQ_lo, 32, O_H2, None, down2)
            v.wait_ge(r_done, 7)
            v.wait_ge(evac_done, B_END)
            for k in range(DT):
                link(v.scalar_tensor_tensor(X[:, k, :], X[:, k, :], col[:, C_MLPPOST + k:C_MLPPOST + k + 1], R[:, :],
                                            ALU.mult, ALU.mult))
                v.wait_ge(x_landed[k], 48)
                v.tensor_tensor(X[:, k, :], X[:, k, :], Xre[:, k, :], ALU.add).then_inc(fin, 1)

        @block.tensor
        def _(pe):
            def product(psum, wslot, wcols, hi, lo, ks, ready=None, by_tile=False):
                for x, k in enumerate(ks):
                    if ready is not None:
                        pe.wait_ge(operand_ready, ready(k))
                    wh = w_hi[:, wslot, wcols(k if by_tile else x)]
                    wl = w_lo[:, wslot, wcols(k if by_tile else x)]
                    for weight, operand in ((wh, hi), (wh, lo), (wl, hi)):
                        for half in range(2):
                            mm = pe.matmul(ps[:, psum + half, :], weight, operand[:, k, half * HALF:(half + 1) * HALF],
                                           start=(x == 0 and weight is wh and operand is hi),
                                           stop=(x == len(ks) - 1 and weight is wl))
                return mm

            def wcols(x):
                return slice(x * P, (x + 1) * P)

            def dense(hi, lo, ready, ks=range(DT)):
                def body(b, turn, n, slot):
                    pe.wait_ge(w_lo_done, b + 1)
                    pe.wait_ge(evac_done, b - 1)
                    product(2 * slot, slot, wcols, hi, lo, ks, ready, True).then_inc(mm_done, 1)
                return body

            def statistic(norm):
                pe.wait_ge(ssq_done, 9 * norm + 9)
                if norm:
                    pe.wait_ge(r_done, norm)
                for half in range(2):
                    mm = pe.matmul(ps[:, 4 + half, :], ones[:, :], ssq[:, half * HALF:(half + 1) * HALF], start=True, stop=True)
                mm.then_inc(stat_done, 1)

            for b in range(2):
                pe.wait_ge(w_lo_done, b + 1)
                for n in range(4):
                    if b:
                        pe.wait_ge(pp_evac, n + 1)
                    mm = product(2 * n, b, lambda x, n=n: slice((2 * n + x) * P, (2 * n + x + 1) * P),
                                 p_hi, p_lo, range(2), lambda k: O_PP + k + 1)
                    if n < 3:
                        mm.then_inc(pp_mm, 1)
                mm.then_inc(pp_mm, 1)
                pe.wait_ge(pp_mm, 4 * b + 4)
                pe.sem_inc(mm_done, 1)
            pe.wait_ge(pp_evac, 8)
            pe.wait_ge(ones_set, 4)
            statistic(0)
            w_in = dense(opP_hi, opP_lo, lambda k: O_WIN + k + 1)
            stream(pe, B_WIN, 4, w_in)
            pe.wait_ge(r_done, 1)
            pe.wait_ge(m["sq"], 3)
            pe.wait_ge(m["lat"], 1)
            for a in range(2):
                for half in range(2):
                    mm = pe.matmul(ps[:, 4 + 2 * a + half, :], ones[:, :], LSQ[:, 2 * a, half * HALF:(half + 1) * HALF],
                                   start=True, stop=True)
                mm.then_inc(m["stat"], 1)
            stream(pe, B_WIN + 4, 4, w_in)
            pe.wait_ge(m["ln"], 2)
            pe.wait_ge(g["w2"], 16)
            for pr in range(2):
                for half in range(2):
                    mm = pe.matmul(ps[:, 4 + 2 * pr + half, :], gw2[0:GRANK, pr * P:(pr + 1) * P],
                                   Z[0:GRANK, 3, half * HALF:(half + 1) * HALF], start=True, stop=True)
                mm.then_inc(g["logit"], 1)
            stream(pe, B_WIN + 8, 6, w_in)
            pe.wait_ge(g["lin"], 2)
            pe.wait_ge(evac_done, B_WIN + 12)
            for w in range(WIN):
                if w >= 2:
                    pe.wait_ge(g["trc"], w - 1)
                for f in range(4):
                    mm = pe.transpose(ps[:, 4 + w % 2, f * P:(f + 1) * P], Z[:, 8 + f, w * P:(w + 1) * P], ident[:, :])
                mm.then_inc(g["tr"], 1)
            stream(pe, B_WIN + 14, 2, w_in)

            def scores(bank, par, k_src, q_src, width):
                r = slice(64 * par, 64 * par + 64)
                for pr in range(2):
                    for w in range(WIN):
                        at_ = (pr * WIN + w) * width
                        mm = pe.matmul(banks(bank, 2 * width // 64)[:, at_:at_ + width], k_src(r, pr, w), q_src(r, pr, w),
                                       start=True, stop=True)
                return mm

            pe.wait_ge(evac_done, B_WOUT)
            pe.wait_ge(g["trc"], WIN)
            for par in range(2):
                scores(4 * par, par, lambda r, pr, w: Z[r, 6 + pr, w * P:(w + 1) * P],
                       lambda r, pr, w: Z[r, 4 + pr, w * P:(w + 1) * P], P).then_inc(g["lmm"], 1)
            pe.wait_ge(g["kdec"], 2)
            pe.wait_ge(g["lcp"], 1)
            for w in range(WIN):
                if w >= 2:
                    pe.wait_ge(g["trc"], WIN + w - 1)
                for pr in range(2):
                    mm = pe.transpose(ps[:, w % 2, pr * P:(pr + 1) * P], KE[0][:, pr, w * P:(w + 1) * P], ident[:, :])
                mm.then_inc(g["tr"], 1)
            pe.wait_ge(g["trc"], 2 * WIN)
            pe.wait_ge(g["lcp"], 2)

            def updates(pr):
                for c in range(NCH):
                    toks = slice(64 * (c % 2), 64 * (c % 2) + 64)
                    bank = 4 + 2 * (c % 2) + (c // 2) // 4
                    for hp in range(2):
                        h = 2 * pr + hp
                        mm = pe.matmul(ps[64 * hp:64 * hp + 64, bank, ((c // 2) % 4) * P:((c // 2) % 4 + 1) * P],
                                       KDT[toks, c // 2, h * 64:(h + 1) * 64], VT[toks, c // 2, h * P:(h + 1) * P],
                                       start=True, stop=True)
                mm.then_inc(g["upd"], 1)

            updates(0)
            for lv in range(len(LEVELS)):
                pe.wait_ge(g["lq"], lv + 1)
                pe.wait_ge(g["lk"], lv + 1)
                for par in range(2):
                    if lv:
                        pe.wait_ge(g["lcp"], 1 + 2 * lv + par)
                    scores(2 * par, par, lambda r, pr, w: KE[lv % 2][r, pr, w * P:(w + 1) * P],
                           lambda r, pr, w: QE[lv % 2][r, pr * HALF + w * 64:pr * HALF + (w + 1) * 64], 64)\
                        .then_inc(g["lmm"], 1)
                if lv == 0:
                    pe.wait_ge(g["states"], 18)
                    updates(1)
            pe.wait_ge(g["lcp"], 2 + 2 * len(LEVELS))
            pe.wait_ge(g["states"], 3 + 30)

            def outputs(h):
                pr, r = h // 2, slice(64 * (h % 2), 64 * (h % 2) + 64)
                for w in range(WIN):
                    dst = banks(2 * h, 2)[:, w * P:(w + 1) * P]
                    pe.matmul(dst, VT[:, w, h * P:(h + 1) * P], SC[:, h % 2, pr, w, :], start=True, stop=False)
                    for x in range(2):
                        c = 2 * w + x
                        mm = pe.matmul(dst[:, 64 * x:64 * x + 64], ST8[r, pr, c, :], QX[r, pr, c * 64:(c + 1) * 64],
                                       start=False, stop=(x == 1))
                mm.then_inc(g["out"], 1)

            def squares(h):
                pe.wait_ge(g["sq"], h + 1)
                for half in range(2):
                    mm = pe.matmul(ps[:, 2 * h + half, :], ones[:, :], SQG[:, h % 2, half * HALF:(half + 1) * HALF],
                                   start=True, stop=True)
                mm.then_inc(g["nst"], 1)

            for h in range(GH):
                outputs(h)
                if h:
                    squares(h - 1)
            squares(GH - 1)

            pe.wait_ge(m["lat"], 4)
            pe.wait_ge(m["wv"], 16)
            pe.wait_ge(g["ln"], GH)

            def job(g):
                if not isinstance(g, int) or g >= 2:
                    pe.wait_ge(m["jev"], g - 1)

            def make(h, slot, j):
                bank, cols = 6 + j % 2, slice(j % 2 * HALF, (j % 2 + 1) * HALF)
                job(h * 12 + j)
                if j == 0:
                    pe.wait_ge(m[f"w{slot}"], (h - slot) * 16 + 32)
                    if not isinstance(h, int) or h >= 1:
                        pe.wait_ge(m["st"], h * 12 - 11)
                        pe.wait_ge(m["pv"], h * 12 - 8)
                if j < 2:
                    for k in range(2):
                        mm = pe.matmul(ps[0:QKD, bank, :], wq_h[:, slot, k * QKD:(k + 1) * QKD], Z[:, k, cols],
                                       start=(k == 0), stop=(k == 1))
                elif j < 4:
                    mm = pe.matmul(ps[0:NOPE, bank, :], wk_h[:, slot, :], Z[:, 2, cols], start=True, stop=True)
                elif j < 6:
                    for x in range(4):
                        w = 4 * (j - 4) + x
                        mm = pe.matmul(ps[:, bank, x * 64:(x + 1) * 64], Z[:, 2, w * P:(w + 1) * P],
                                       wv_m[:, bass.ds(h * 64, 64)], start=True, stop=True)
                else:
                    a = (j - 6) // 2
                    pe.wait_ge(m["sq"], h * 2 + (4 + a))
                    mm = pe.matmul(ps[0:QKD, bank, :], ones[0:QKD, 0:QKD], SQ[0:QKD, a, cols], start=True, stop=True)
                mm.then_inc(m["job"], 1)

            def scores_of(h, slot, u):
                qt, c0, width = PIECES[u]
                if u == 0:
                    pe.wait_ge(m["rope"], h + 1)
                pe.wait_ge(m["red"], h * 12 + (u + 1))
                pe.matmul(ps[:, u % 2, 0:width], QK[0:QKD, slot, 0, qt * P:(qt + 1) * P],
                          QK[0:QKD, slot, 1, c0:c0 + width], start=True, stop=True).then_inc(m["scores"], 1)

            def maxima(h, more, r):
                g = h * 12 + (12 + (10 if more else 0) + r)
                job(g)
                pe.wait_ge(m["mx"], h * 2 + (r + 1))
                for x in range(4):
                    mm = pe.transpose(ps[0:1, 6 + r, x * P:(x + 1) * P], mx8[:, 4 * r + x:4 * r + x + 1], ident[:, :])
                mm.then_inc(m["job"], 1)

            def scores_t(h, slot, more, u):
                half, kt, q0, width = PIECES_T[u]
                if kt == 0:
                    pe.wait_ge(m["jev"], h * 12 + (12 + (10 if more else 0) + half + 1))
                pe.wait_ge(m["exp"], h * 12 + (u + 1))
                diagonal = q0 == kt * P
                mm = pe.matmul(ps[:, 2 + u % 2, 0:width], QK[0:QKD + 1, slot, 1, kt * P:(kt + 1) * P],
                               QK[0:QKD + 1, slot, 0, q0:q0 + width], start=True, stop=not diagonal)
                if diagonal:
                    mm = pe.matmul(ps[:, 2 + u % 2, 0:64], mrow[0:1, :], ones[0:1, 0:64], start=False, stop=True)
                mm.then_inc(m["st"], 1)

            def values(h, slot, u):
                half, kt, q0, width = PIECES_T[u]
                if kt == 0:
                    pe.wait_ge(m["ofree"], h * 2 + (1 + half))
                pe.wait_ge(m["exp"], h * 12 + (u + 3))
                c0 = q0 - half * HALF
                pe.matmul(ps[:, 4 + half, c0:c0 + width], VA[:, slot, kt, :], PT[:, u % 4, 0:width],
                          start=(kt == 0), stop=(kt == 4 * half + 3)).then_inc(m["pv"], 1)

            def head(h, slot, more):
                if isinstance(h, int) and h == 0:
                    pe.wait_ge(m["consts"], 5)
                for u in range(12):
                    scores_of(h, slot, u)
                    if more and u < 10:
                        make(h + 1, 1 - slot, u)
                for r in range(2):
                    maxima(h, more, r)
                scores_t(h, slot, more, 0)
                scores_t(h, slot, more, 1)
                for u in range(12):
                    if u + 2 < 12:
                        scores_t(h, slot, more, u + 2)
                    values(h, slot, u)

            pe.sem_inc(m["st"], 1)
            pe.sem_inc(m["pv"], 4)
            for j in range(10):
                make(0, 0, j)
            pe.wait_ge(m["job"], 10)
            pe.sem_inc(m["job"], 2)
            head(0, 0, True)
            with pe.Fori(0, 3) as i:
                head(i * 2 + 1, 1, True)
                head(i * 2 + 2, 0, True)
            head(7, 1, False)

            pe.wait_ge(m["exp"], 12 * MH + 2)
            stream(pe, B_WOUT, 8, dense(opP_hi, opP_lo, lambda k: O_WOUT + (k + 4) % 8 + 1, (4, 5, 6, 7, 0, 1, 2, 3)))

            def mlp(b0, norm, ahi, alo, a0, hhi, hlo, h0):
                statistic(norm)
                with pe.Fori(0, 4) as gi:
                    for off, hi, lo, ready in ((0, ahi, alo, lambda k: a0 + k + 1),
                                               (8, hhi, hlo, lambda k: gi * 8 + (h0 + k + 1))):
                        with pe.Fori(0, 4) as i:
                            for j in range(2):
                                dense(hi, lo, ready)(gi * 16 + i * 2 + (b0 + off + j), None, None, j)
            mlp(B_MLP1, 1, opQ_hi, opQ_lo, O_UP1, opP_hi, opP_lo, O_H1)
            statistic(2)
            stream(pe, B_GATE, 8, dense(opQ_hi, opQ_lo, lambda k: O_GATE + k + 1))

            statistic(3)
            stream(pe, B_WIN2, 10, dense(opP_hi, opP_lo, lambda k: O_WIN2 + k + 1))
            pe.wait_ge(evac_done, B_MRG)
            for gi in range(4):
                pe.wait_ge(s["pool"], gi + 1)
                if gi >= 2:
                    pe.wait_ge(s["y"], gi - 1)
                for half in range(2):
                    mm = pe.matmul(ps[:, 2 * (gi % 2) + half, :], wpool[:, gi, :], Z2[:, gi, half * HALF:(half + 1) * HALF],
                                   start=True, stop=True)
                mm.then_inc(s["pmm"], 1)
            pe.wait_ge(s["z"], 10)
            for w in range(2):
                for x in range(4):
                    mm = pe.transpose(ps[:, 4 + w, x * P:(x + 1) * P], Z2[:, 9, (4 * w + x) * P:(4 * w + x + 1) * P], ident[:, :])
                mm.then_inc(s["vtr"], 1)
            pe.wait_ge(s["vtc"], 2)
            pe.wait_ge(s["zero"], 2)
            pe.wait_ge(s["y"], 4)

            def scores2(n, slot):
                pe.wait_ge(s["blk"], n * 2 + 2)
                if not isinstance(n, int) or n >= 1:
                    pe.wait_ge(s["sc"], n * 5 - 4)
                for par in range(2):
                    for i in range(4):
                        h = 4 * par + i
                        mm = pe.matmul(banks(0, 4)[:, h * 256:(h + 1) * 256], qb2[64 * par:64 * par + 64, slot, i, :],
                                       kb2[64 * par:64 * par + 64, slot, :], start=True, stop=True)
                mm.then_inc(s["qk"], 1)

            def attend(n, slot, more):
                pe.wait_ge(s["exp"], n * 9 + 9)
                for name, done, half in (("tra", "tcb", 0), ("trb", "tca", 1)):
                    if half == 1:
                        pe.wait_ge(s[done], n + 1)
                    elif not isinstance(n, int) or n >= 1:
                        pe.wait_ge(s[done], n)
                    for h in range(4 * half, 4 * half + 4):
                        for kt in range(2):
                            mm = pe.transpose(banks(4, 2)[:, ((h % 4) * 2 + kt) * P:((h % 4) * 2 + kt + 1) * P],
                                              P2[:, h, kt * P:(kt + 1) * P], ident[:, :])
                    mm.then_inc(s[name], 1)
                if more:
                    scores2(n + 1, 1 - slot)
                pe.wait_ge(s["tcb"], n + 1)
                if not isinstance(n, int) or n >= 1:
                    pe.wait_ge(s["on"], n)
                for h in range(NQ):
                    for kt in range(2):
                        mm = pe.matmul(ps[:, 7, h * HD:(h + 1) * HD], PT2[:, h, kt, :],
                                       vpad[:, bass.ds(n + kt, 1), (h // 4) * HD:(h // 4 + 1) * HD].rearrange("p a b -> p (a b)"),
                                       start=(kt == 0), stop=(kt == 1))
                mm.then_inc(s["pv"], 1)
                pe.wait_ge(s["on"], n + 1)
                if not isinstance(n, int) or n >= 1:
                    pe.wait_ge(s["otc"], n)
                for f in range(4):
                    mm = pe.transpose(ps[:, 6, f * P:(f + 1) * P], O2[:, f * P:(f + 1) * P], ident[:, :])
                mm.then_inc(s["otr"], 1)

            scores2(0, 0)
            attend(0, 0, True)
            with pe.Fori(0, 3) as i:
                attend(i * 2 + 1, 1, True)
                attend(i * 2 + 2, 0, True)
            attend(7, 1, False)

            pe.wait_ge(s["otc"], 8)
            with pe.Fori(0, 4) as i:
                for j in range(2):
                    for q in range(2):
                        o = 3 * j + q
                        b = i * 6 + (B_MRG + o)
                        dense(opP_hi, opP_lo, None)(b, None, None, o % 2)
                    o = 3 * j + 2
                    b = i * 6 + (B_MRG + o)
                    pe.wait_ge(w_lo_done, b + 1)
                    pe.wait_ge(s["mrg"], i * 2 + (j + 1))
                    product(4, o % 2, wcols, opQ_hi, opQ_lo, range(4), lambda k: O_Y + k + 1)
                    product(6, o % 2, lambda x: wcols(x + 4), opQ_hi, opQ_lo, range(4, 8), lambda k: O_Y + k + 1)\
                        .then_inc(mm_done, 1)
            stream(pe, B_WO2, 8, dense(opQ_hi, opQ_lo, lambda k: O_WO2 + k + 1))
            statistic(4)
            mlp(B_MLP2, 5, opP_hi, opP_lo, O_UP2, opQ_hi, opQ_lo, O_H2)
            statistic(6)


def _layout(i):
    c = np.ascontiguousarray
    f = {k: np.asarray(v) for k, v in i.items()}

    def blocks(w):
        k, n = w.shape
        return w.reshape(k // P, P, n // P, P).transpose(2, 1, 0, 3).reshape(n // P * P, k // P * P)

    w_in = f["w_in"][0]
    q, k, v, low, r, cq, ckv, kr = np.split(w_in, np.cumsum([256, 256, 512, 16, 512, 256, 128]), axis=1)
    z = np.zeros((D, 48), np.float32)
    misc = np.concatenate([low, z, kr, z[:, :32]], axis=1)
    wp = f["w_ple_proj"][0]
    pp = [wp[:, b * 512:(b + 1) * 512].reshape(2, P, 4, P).transpose(1, 2, 0, 3).reshape(P, 1024) for b in range(2)]
    w_out = f["w_out"][0]
    w_out = np.concatenate([w_out[512:], w_out[:512]], axis=0)

    def mlp(up, down):
        u, out = blocks(up), []
        for gi in range(4):
            out += [u[gi * 1024:(gi + 1) * 1024], blocks(down[gi * 1024:(gi + 1) * 1024])]
        return out

    w2 = f["w_in_2"][0]
    q2 = w2[:, 512:1024].reshape(D, 2, 4, 64).transpose(0, 2, 1, 3).reshape(D, 512)
    gates = blocks(w2[:, 1280:])
    br = blocks(np.concatenate([f["w_branch_pool_2"][0], f["w_branch_attn_2"][0]], axis=0))
    merge = []
    for n in range(8):
        merge += [gates[n * P:(n + 1) * P], gates[(8 + n) * P:(9 + n) * P], br[n * P:(n + 1) * P]]
    stream = np.concatenate(
        pp + [blocks(np.concatenate([cq, ckv, misc, q, k, v, r], axis=1)), blocks(w_out)]
        + mlp(f["w_mlp_up"][0], f["w_mlp_down"][0]) + [blocks(f["w_ple_gate"][0])]
        + [blocks(np.concatenate([w2[:, :512], q2, w2[:, 1024:1280]], axis=1))] + merge
        + [blocks(f["w_out_2"][0])] + mlp(f["w_up_2"][0], f["w_down_2"][0]), axis=0)

    def vec(a):
        a = a.reshape(-1)
        if a.size % P:
            a = np.concatenate([a, np.zeros(P - a.size % P, a.dtype)])
        return a.reshape(-1, P).T

    b2 = f["b_in_2"][0]
    bq = b2[512:1024].reshape(2, 4, 64).transpose(1, 0, 2).reshape(-1)
    cols = np.concatenate(
        [vec(f[n][0]) for n in ("attn_norm", "mlp_norm", "ple_norm", "b_ple_gate")]
        + [vec(f[n][0]) for n in ("g_mix_pre_2", "g_mix_post_2", "g_mlp_pre_2", "g_mlp_post_2")]
        + [vec(np.concatenate([b2[:512], bq, b2[1024:]])), vec(f["pool_scale_2"][0]), vec(f["gla_gate_b"][0]),
           vec(f["gla_out_norm"][0]), vec(f["mla_q_norm"][0]), vec(f["mla_kv_norm"][0]),
           vec(f["qk_norm_q"][0]), vec(f["qk_norm_k"][0]), np.broadcast_to(f["attn_sinks_2"][0][None], (P, 8))], axis=1)
    ukv = f["mla_w_ukv"][0].reshape(P, 8, 2, 64)

    tok = np.arange(P)
    lmask = np.zeros((P, len(LEVELS), CHUNK), np.int32)
    for lv, size in enumerate(LEVELS):
        tt = np.concatenate([np.arange(n * 2 * size + size, (n + 1) * 2 * size) for n in range(P // (2 * size))])
        lmask[:, lv] = (tok[:, None] // (2 * size) == tt[None] // (2 * size)) & (tok[:, None] % (2 * size) < size)
    inv = (10000.0 ** (-np.arange(0, 32, 2, dtype=np.float32) / np.float32(32))).astype(np.float32)
    inv2 = (500000.0 ** (-np.arange(0, 16, 2, dtype=np.float32) / np.float32(16))).astype(np.float32)
    a2 = (np.arange(S, dtype=np.float32)[None] * inv2[:, None]).astype(np.float32)
    tabC, tabS = np.ones((P, S), np.float32), np.zeros((P, S), np.float32)
    for o in (0, 64):
        tabC[o:o + 8] = tabC[o + 8:o + 16] = np.cos(a2)
        tabS[o:o + 8], tabS[o + 8:o + 16] = -np.sin(a2), np.sin(a2)
    rel = tok[:, None] + P - np.arange(256)[None]
    band = (rel >= 0) & (rel < 128)
    mask2 = np.stack([np.where(band & (np.arange(256) >= P)[None], 0, NEG), np.where(band, 0, NEG)], 1).astype(np.float32)
    icnt = np.stack([1.0 / np.minimum(np.arange(16) + 1, w) for w in POOL_W]).astype(np.float32)
    return {
        "w_stream": c(stream), "xT": c(f["x"][0].T), "pT": c(f["p"][0, 0].T), "cols": c(cols),
        "ident": np.eye(P, dtype=np.float32), "lmask": lmask,
        "dmask": (np.eye(P) * GDK ** -0.5).astype(np.float32), "gw2": c(f["gla_gate_w2"][0]),
        "w_uv": c(ukv[:, :, 1].reshape(P, 512)), "freq": np.tile(inv, 2)[:, None],
        "sgn": np.repeat(np.float32([-1, 1]), 16)[:, None], "positions": c(f["positions"][0].astype(np.int32)),
        "w_uq": c(f["mla_w_uq"][0].reshape(2, P, 8, 96).transpose(2, 1, 0, 3).reshape(8 * P, 192)),
        "w_uk": c(ukv[:, :, 0].transpose(1, 0, 2).reshape(8 * P, 64)),
        "tabC": tabC, "tabS": tabS, "mask2": mask2,
        "icnt": c(np.broadcast_to(icnt[None], (P, 4, 16))), "w_pool": c(f["w_pool_2"][0].transpose(1, 0, 2)),
    }


def kernel(**inputs):
    import concourse.bacc as bacc
    from concourse.bass_utils import run_bass_kernel_spmd as run

    arrays = _layout(inputs)
    nc = bacc.Bacc("TRN2", target_bir_lowering=False, num_devices=1)
    t = {n: nc.dram_tensor("in_" + n, a.shape, mybir.dt.from_np(a.dtype), kind="ExternalInput").ap()
         for n, a in arrays.items()}
    t["out"] = nc.dram_tensor("out_T", (D, S), F32, kind="ExternalOutput").ap()
    for n in ("pp_spill", "x_spill"):
        t[n] = nc.dram_tensor(n, (D, S), F32, kind="Internal").ap()
    build(nc, t)
    r = run(nc, [{"in_" + n: a for n, a in arrays.items()}], core_ids=[0])
    return np.ascontiguousarray(r.results[0]["out_T"].T)[None]
```

```python
import math
from contextlib import ExitStack

import concourse.bass as bass
import numpy as np
from concourse import mybir

F32 = mybir.dt.float32
F32R = mybir.dt.float32r
I32 = mybir.dt.int32
ACT = mybir.ActivationFunctionType
ALU = mybir.AluOpType
AX_X = mybir.AxisListType.X

P = 128
S = 1024
D = 1024
DT = D // P
HALF = 512
WIN = S // P
EPS = 1e-6

CHUNK = 64
GH, GDK, GDV, GRANK = 4, 64, 128, 16
NCH = S // CHUNK
MH, NOPE, ROPE, QKD = 8, 64, 32, 96
LEVELS = [32, 16, 8, 4, 2, 1]
PIECES = [(qt, c0, min((qt + 1) * P - c0, HALF)) for qt in range(WIN) for c0 in range(0, (qt + 1) * P, HALF)]
PIECES_T = [(half, kt, max(half * HALF, kt * P), (half + 1) * HALF - max(half * HALF, kt * P))
            for half in range(2) for kt in range(4 * half + 4)]
HD, NQ, NKV = 64, 8, 2
POOL_W = (2, 4, 8, 16)
NEG = -1e30

B_PP, B_WIN, B_WOUT, B_MLP1 = 0, 2, 18, 26
B_GATE, B_WIN2, B_MRG, B_WO2, B_MLP2, B_END = 90, 98, 108, 132, 140, 204
O_PP, O_WIN, O_WOUT, O_UP1, O_H1, O_GATE, O_WIN2, O_Y, O_WO2, O_UP2, O_H2 = (
    0, 2, 10, 18, 26, 58, 66, 74, 82, 90, 98)
C_ATTN, C_MLP, C_PLE, C_BPLE, C_MIXPRE, C_MIXPOST, C_MLPPRE, C_MLPPOST = range(0, 64, 8)
C_BIN, C_POOLS, C_GATEB, C_GOUT, C_QN, C_KVN, C_QKQ, C_QKK, C_SINK = 64, 90, 94, 96, 97, 99, 100, 101, 102
NCOL = 110


def build(nc, t):
    ctx = ExitStack()
    with ctx:
        base = (nc.sbuf_base + 31) // 32 * 32
        nc.bump_sbuf(int(207.75 * 1024) + base - nc.sbuf_base)

        def at(name, shape, kb, dt=F32):
            return nc.alloc_sbuf_tensor_at(name, shape, dt, offset=base + int(kb * 1024))

        def sem(name):
            return ctx.enter_context(nc.semaphore(name))

        XB, PB, QB_, WB, TB, RB, CB = 0, 32, 96, 160, 184, 192, 204
        X = at("X", [P, DT, S], XB)
        opP_hi, opP_lo = at("opP_hi", [P, DT, S], PB, F32R), at("opP_lo", [P, DT, S], PB + 32, F32R)
        opQ_hi, opQ_lo = at("opQ_hi", [P, DT, S], QB_, F32R), at("opQ_lo", [P, DT, S], QB_ + 32, F32R)
        w_stage = at("w_stage", [P, 2, 1024], WB)
        w_hi, w_lo = at("w_hi", [P, 2, 1024], WB + 8, F32R), at("w_lo", [P, 2, 1024], WB + 16, F32R)
        T = at("T", [P, 2, S], TB)
        R = at("R", [P, S], RB)
        ssq = at("ssq", [P, S], RB + 4)
        sqs = at("sqs", [P, S], RB + 8)
        ones = at("ones", [P, P], CB)
        ident = at("ident", [P, P], CB + 0.5)
        col = at("col", [P, NCOL], CB + 1)
        small = at("small", [P, 64], CB + 1.5)
        eps_c, one_c, halfpi_c = small[:, 0:1], small[:, 1:2], small[:, 2:3]

        p_hi, p_lo = at("p_hi", [P, 2, S], QB_, F32R), at("p_lo", [P, 2, S], QB_ + 8, F32R)
        p_f = at("p_f", [P, 2, S], QB_ + 16)
        ppout = at("ppout", [P, DT, S], QB_ + 32)
        Z = at("Z", [P, 16, S], QB_)
        VT = at("VT", [P, WIN, 512], XB)
        Bc, E = at("Bc", [P, 2, S], XB + 16), at("E", [P, 2, S], XB + 24)
        EX = [at("EX1", [P, 2, S], PB + 56), E]
        KE = [at("KE0", [P, 2, S], TB), at("KE1", [P, 2, S], QB_ + 32)]
        QE = [at("QE0", [P, 2, WIN, 2, CHUNK], QB_ + 40), at("QE1", [P, 2, WIN, 2, CHUNK], PB + 48)]
        reset = at("reset", [P, S], RB + 4)
        gw2 = at("gw2", [P, 256], RB + 8)
        dmask = at("dmask", [P, P], RB + 9)
        lmask = at("lmask", [P, len(LEVELS), CHUNK], RB + 9.5, I32)
        SC = at("SC", [P, 2, 2, WIN, P], PB)
        ST8 = at("ST8", [P, 2, NCH, P], PB + 16)
        KDT = at("KDT", [P, WIN, 256], PB + 32)
        QX = at("QX", [P, 2, S], PB + 40)
        SQG = at("SQG", [P, 2, S], PB + 48)
        decay = small[:, 8:40]
        head_root = [KE[h // 2][:, h % 2, :] for h in range(GH)]
        head_gate = [E[:, 0, :], E[:, 1, :], Bc[:, 0, :], Bc[:, 1, :]]
        LSQ = at("LSQ", [P, 3, S], XB)
        LRT = at("LRT", [P, 2, S], XB + 16)
        QK = at("QK", [P, 2, 2, S], XB)
        SQ = at("SQ", [P, 2, S], XB + 16)
        SW = at("SW", [P, 2, S], XB + 24)
        RR = at("RR", [P, 2, S], PB)
        CT, SN = at("CT", [P, S], PB + 8), at("SN", [P, S], PB + 12)
        PT = at("PT", [P, 4, HALF], PB + 32)
        VA = at("VA", [P, 2, WIN, P], PB + 40)
        wq_h = at("wq_h", [P, 2, 192], RB)
        wk_h = at("wk_h", [P, 2, 64], RB + 1.5)
        wv_m = at("wv_m", [P, 512], RB + 2)
        freq = small[:, 52:53]
        mrow = at("mrow", [P, P], RB + 11)
        pos_i = at("pos_i", [P, S], XB + 28, I32)
        ang, kf, ki = at("ang", [P, S], PB + 56), at("kf", [P, S], PB + 60), at("ki", [P, S], XB + 24, I32)
        mx8 = small[:, 40:48]
        mxb = small[:, 48:52]
        Z2 = at("Z2", [P, 10, S], QB_)
        tabC, tabS = at("tabC", [P, S], QB_ + 40), at("tabS", [P, S], QB_ + 44)
        swq = at("swq", [P, 4, S], XB + 16)
        swk = at("swk", [P, S], QB_ + 48)
        kpad = at("kpad", [P, P + S], QB_ + 52)
        vpad = at("vpad", [P, WIN + 1, P], QB_ + 56.5)
        S2 = at("S2", [P, NQ, 256], QB_)
        P2 = at("P2", [P, NQ, 256], QB_ + 8)
        PT2 = at("PT2", [P, NQ, 2, P], QB_ + 40)
        DG = at("DG", [P, NQ, P], TB + 4)
        kb2 = at("kb2", [P, 2, 256], QB_ + 48)
        vb2 = at("vb2", [P, 2, 2, P], QB_ + 61)
        mask2 = at("mask2", [P, 2, 256], TB)
        qb2 = at("qb2", [P, 2, 4, P], RB + 8)
        wpool = at("wpool", [P, 4, P], RB + 4)
        icnt = at("icnt", [P, 4, 16], CB + 1.75)
        m8, e8, d8, r8 = (small[:, 48 + 0:56], small[:, 56:64], small[:, 8:16], small[:, 16:24])
        nm8 = small[:, 24:32]
        Xre = at("Xre", [P, DT, S], PB + 32)

        ps = ctx.enter_context(nc.psum_tensor("ps", [P, 8, HALF], F32))

        def banks(a, n):
            return ps[:, a:a + n, :].rearrange("p a b -> p (a b)")

        w_landed = [sem("w_landed0"), sem("w_landed1")]
        w_hi_done, w_lo_done = sem("w_hi_done"), sem("w_lo_done")
        mm_done, evac_done = sem("mm_done"), sem("evac_done")
        operand_hi, operand_ready = sem("operand_hi"), sem("operand_ready")
        sq_done, ssq_done, stat_done, r_done = sem("sq_done"), sem("ssq_done"), sem("stat_done"), sem("r_done")
        x_landed = [sem(f"x_landed{k}") for k in range(DT)]
        x_back = [sem("x_back0"), sem("x_back1")]
        p_landed, cst_landed, ones_set = sem("p_landed"), sem("cst_landed"), sem("ones_set")
        pp_mm, pp_evac, pp_spilled = sem("pp_mm"), sem("pp_evac"), sem("pp_spilled")
        act_step, dve_step, pool_step = sem("act_step"), sem("dve_step"), sem("pool_step")
        relu_sq = sem("relu_sq")
        pp_back, gated, pp_used, x_upd = sem("pp_back"), sem("gated"), sem("pp_used"), sem("x_upd")
        y_stored = sem("y_stored")
        g = {n: sem("gla_" + n) for n in (
            "consts", "w2", "zero", "logit", "lin", "soft", "cum", "exps", "kdec", "ln", "tr", "trc", "upd", "states",
            "lexp", "lq", "lk", "lmm", "lcp", "out", "oraw", "sq", "nst", "rn", "sig", "gated", "normed", "fin")}
        m = {n: sem("mla_" + n) for n in (
            "w0", "w1", "wv", "misc", "consts", "stat", "r", "lat", "angle", "sin", "job", "jev", "sq", "rr", "nrm",
            "swap", "swn", "rope", "scores", "corner", "red", "mx", "st", "exp", "pv", "inv", "ofree", "krot", "ln")}
        s = {n: sem("swa_" + n) for n in (
            "consts", "z", "pool", "ptmp", "pmm", "y", "vtr", "vtc", "zero", "swap", "rope", "swn", "blk", "vb", "qk", "sc", "mx",
            "exp", "den", "tra", "tca", "pv", "on", "otr", "otc", "spill", "sig", "mrg", "mt", "sqsum", "scaled")}
        fin, normed_out, x2_spilled = [sem("fin0"), sem("fin1")], sem("normed_out"), sem("x2_spilled")

        def bc(ap, shape):
            return ap.to_broadcast(shape)

        class Link:

            def __init__(self, eng, steps):
                self.eng, self.steps, self.n = eng, steps, 0

            def __call__(self, ins):
                ins.then_inc(self.steps, 1)
                self.n += 1
                self.eng.wait_ge(self.steps, self.n)

        def tile(ap, n):
            return ap[:, n, :] if isinstance(n, int) else ap[:, bass.ds(n, 1), :].rearrange("p a b -> p (a b)")

        def stream(eng, b0, n, body, n0=0, begun=0):
            with eng.Fori(begun, n // 2) as i:
                for j in range(2):
                    body(i * 2 + (b0 + j), i + b0 // 2, i * 2 + (n0 + j), j)

        def started(step):
            def body(b, turn, n, slot):
                return step(b, turn, n, slot, split_next=False)
            return body

        def normed(eng, b0, n, step, n0=0):
            started(step)(b0, b0 // 2, n0, 0)
            step(b0 + 1, b0 // 2, n0 + 1, 1)
            if n > 2:
                stream(eng, b0, n, step, n0, 1)

        block = ctx.enter_context(nc.Block())

        @block.sync
        def _(sp):
            def load(b, turn, n, slot):
                if not (isinstance(b, int) and b < 2):
                    sp.wait_ge(w_lo_done, b - 1)
                sp.dma_start(w_stage[:, slot, :], t["w_stream"][bass.ds(b * P, P), :]).then_inc(w_landed[slot], 16)

            load(0, 0, 0, 0)
            load(1, 0, 1, 1)
            stream(sp, 2, B_WOUT, load)
            sp.wait_ge(evac_done, B_WOUT)

            def head_weights(h, slot):
                if not isinstance(h, int) or h >= 2:
                    sp.wait_ge(m["job"], h * 12 - 20)
                sp.dma_start(wq_h[:, slot, :], t["w_uq"][bass.ds(h * P, P), :]).then_inc(m[f"w{slot}"], 16)
                sp.dma_start(wk_h[:, slot, :], t["w_uk"][bass.ds(h * P, P), :]).then_inc(m[f"w{slot}"], 16)

            def swap(h, slot):
                sp.wait_ge(m["nrm"], h * 2 + 2)
                if not isinstance(h, int) or h >= 1:
                    sp.wait_ge(m["rope"], h)
                sp.dma_start(SW[64:80, :, :], QK[80:96, slot, :, :]).then_inc(m["swap"], 16)
                sp.dma_start(SW[80:96, :, :], QK[64:80, slot, :, :]).then_inc(m["swap"], 16)

            head_weights(0, 0)
            head_weights(1, 1)
            swap(0, 0)
            with sp.Fori(0, MH // 2 - 1) as i:
                head_weights(i * 2 + 2, 0)
                swap(i * 2 + 1, 1)
                head_weights(i * 2 + 3, 1)
                swap(i * 2 + 2, 0)
            swap(MH - 1, 1)

            sp.wait_ge(m["st"], 12 * MH + 1)

            def residual(k, turn, slot):
                if not isinstance(k, int):
                    sp.wait_ge(x_back[slot], turn * 16)
                sp.dma_start(tile(X, k), t["xT"][bass.ds(k * P, P), :]).then_inc(x_back[slot], 16)

            residual(0, 0, 0)
            residual(1, 0, 1)
            with sp.Fori(0, 3) as i:
                for j in range(2):
                    load(i * 2 + (B_WOUT + 2 + j), None, None, j)
                    residual(i * 2 + (2 + j), i + 1, j)
            stream(sp, B_WOUT + 8, B_END - B_WOUT - 8, load)
            for k in range(DT):
                sp.wait_ge(fin[k % 2], k // 2 + 1)
                sp.dma_start(t["out"][k * P:(k + 1) * P, :], X[:, k, :]).then_inc(y_stored, 16)
            sp.wait_ge(y_stored, 16 * DT)

        @block.gpsimd
        def _(pool):
            link = Link(pool, pool_step)
            pool.dma_start(col[:, :], t["cols"]).then_inc(cst_landed, 16)
            pool.dma_start(ident[:, :], t["ident"]).then_inc(cst_landed, 16)
            pool.dma_start(p_f[:, :, :], t["pT"].rearrange("(k p) n -> p k n", p=P)).then_inc(p_landed, 16)
            for k in range(DT):
                pool.dma_start(X[:, k, :], t["xT"][k * P:(k + 1) * P, :]).then_inc(x_landed[k], 16)
            pool.memset(ones[:, :], 1.0).then_inc(ones_set, 1)
            pool.memset(eps_c, EPS).then_inc(ones_set, 1)
            pool.memset(one_c, 1.0).then_inc(ones_set, 1)
            pool.memset(halfpi_c, math.pi / 2).then_inc(ones_set, 1)
            pool.wait_ge(pp_evac, 8)
            pool.dma_start(t["pp_spill"].rearrange("(k p) n -> p k n", p=P), ppout[:, :, :]).then_inc(pp_spilled, 16)

            pool.wait_ge(ssq_done, 9)
            pool.dma_start(gw2[0:GRANK, :], t["gw2"]).then_inc(g["w2"], 16)
            pool.dma_start(lmask[:, :, :], t["lmask"]).then_inc(g["consts"], 16)
            pool.dma_start(dmask[:, :], t["dmask"]).then_inc(g["consts"], 16)
            pool.wait_ge(stat_done, 1)
            link(pool.memset(reset[:, :], 1.0))
            pool.memset(reset[:, :].rearrange("p (c k) -> p c k", k=CHUNK)[:, :, 0:1], 0.0).then_inc(g["cum"], 1)

            pool.wait_ge(g["tr"], WIN)
            pool.memset(QE[0][:, :, :, :, :], 0.0).then_inc(g["zero"], 1)
            pool.wait_ge(mm_done, B_WOUT)
            pool.memset(QE[1][:, :, :, :, :], 0.0).then_inc(g["zero"], 1)

            pool.wait_ge(evac_done, B_WOUT)
            pool.dma_start(wv_m[:, :], t["w_uv"]).then_inc(m["wv"], 16)
            pool.dma_start(freq[64:96, :], t["freq"]).then_inc(m["misc"], 16)
            pool.wait_ge(g["gated"], GH)
            pool.dma_start(pos_i[64:96, :], t["positions"].partition_broadcast(ROPE)).then_inc(m["misc"], 16)
            pool.wait_ge(g["out"], GH)
            pool.memset(QK[96:97, :, 1, :], -1.0).then_inc(m["consts"], 1)
            pool.wait_ge(m["consts"], 1)
            pool.memset(VA[:, 0, :, 64:128], 1.0).then_inc(m["consts"], 1)
            pool.wait_ge(m["consts"], 2)
            pool.memset(VA[:, 1, :, 0:64], 1.0).then_inc(m["consts"], 1)
            pool.wait_ge(m["consts"], 3)
            pool.memset(mrow[0:1, 0:64], 0.0).then_inc(m["consts"], 1)
            pool.wait_ge(m["consts"], 4)
            pool.memset(mrow[0:1, 64:128], NEG).then_inc(m["consts"], 1)

            pool.wait_ge(m["sin"], 2)
            with pool.Fori(0, MH) as h:
                pool.wait_ge(m["swap"], h * 32 + 32)
                pool.tensor_tensor(SW[64:96, :, :], SW[64:96, :, :], bc(SN[64:96, :].unsqueeze(1), [ROPE, 2, S]), ALU.mult)\
                    .then_inc(m["swn"], 1)

            pool.wait_ge(pp_spilled, 16)
            pool.wait_ge(operand_ready, O_H1 + 32)
            pool.dma_start(T[:, 1, :], t["pp_spill"][0:P, :]).then_inc(pp_back, 16)
            with pool.Fori(1, DT) as i:
                pool.wait_ge(pp_used, i)
                pool.wait_ge(pp_spilled, 16)
                pool.dma_start(T[:, 1, :], t["pp_spill"][bass.ds(i * P, P), :]).then_inc(pp_back, 16)

            pool.wait_ge(x_upd, DT)
            pool.dma_start(t["x_spill"].rearrange("(k p) n -> p k n", p=P), X[:, :, :]).then_inc(s["spill"], 16)
            pool.wait_ge(mm_done, B_WIN2)
            pool.dma_start(tabC[:, :], t["tabC"]).then_inc(s["consts"], 16)
            pool.dma_start(tabS[:, :], t["tabS"]).then_inc(s["consts"], 16)
            pool.dma_start(icnt[:, :, :], t["icnt"]).then_inc(s["consts"], 16)
            pool.wait_ge(r_done, 4)
            pool.dma_start(wpool[:, :, :], t["w_pool"]).then_inc(s["consts"], 16)
            pool.wait_ge(s["spill"], 16)
            pool.memset(kpad[:, 0:P], 0.0).then_inc(s["zero"], 1)
            pool.memset(vpad[:, 0, :], 0.0).then_inc(s["zero"], 1)
            pool.memset(swk[:, :], 0.0).then_inc(s["zero"], 1)
            pool.memset(swq[:, :, :], 0.0).then_inc(s["zero"], 1)
            pool.wait_ge(s["zero"], 4)
            for z, sw, tiles in ((8, swq[:, :, :], slice(4, 8)), (9, swk[:, :].unsqueeze(1), slice(8, 9))):
                pool.wait_ge(s["z"], z)
                for a in (0, 64):
                    for u, v in ((a, a + 8), (a + 8, a)):
                        pool.dma_start(sw[u:u + 8], Z2[v:v + 8, tiles, :]).then_inc(s["swap"], 16)
            pool.wait_ge(s["swap"], 128)
            pool.wait_ge(s["consts"], 64)
            for sw, n in ((swq[:, :, :], 4), (swk[:, :].unsqueeze(1), 1)):
                pool.tensor_tensor(sw, sw, bc(tabS[:, :].unsqueeze(1), [P, n, S]), ALU.mult).then_inc(s["swn"], 1)
            pool.wait_ge(s["pool"], 4)
            pool.dma_start(mask2[:, :, :], t["mask2"]).then_inc(s["consts"], 16)

            pool.wait_ge(mm_done, B_WO2)
            pool.wait_ge(s["spill"], 16)
            for k in range(DT):
                pool.dma_start(Xre[:, k, :], t["x_spill"][k * P:(k + 1) * P, :]).then_inc(x_landed[k], 16)
            for k in range(DT):
                pool.wait_ge(s["scaled"], k + 1)
                pool.wait_ge(x_landed[k], 32)
                pool.tensor_tensor(X[:, k, :], X[:, k, :], Xre[:, k, :], ALU.add).then_inc(s["mt"], 1)
            pool.wait_ge(s["mt"], DT)
            pool.dma_start(t["x_spill"].rearrange("(k p) n -> p k n", p=P), X[:, :, :]).then_inc(x2_spilled, 16)
            pool.wait_ge(x2_spilled, 16)
            pool.wait_ge(mm_done, B_MLP2 + 56)
            for k in range(DT):
                pool.dma_start(Xre[:, k, :], t["x_spill"][k * P:(k + 1) * P, :]).then_inc(x_landed[k], 16)
            for k in range(1, DT, 2):
                pool.wait_ge(normed_out, k + 1)
                pool.wait_ge(x_landed[k], 48)
                pool.tensor_tensor(X[:, k, :], X[:, k, :], Xre[:, k, :], ALU.add).then_inc(fin[1], 1)

        @block.scalar
        def _(act):
            link = Link(act, act_step)

            def w_high(b, turn, slot):
                act.wait_ge(w_landed[slot], turn * 16 + 16)
                if not isinstance(b, int) or b >= 2:
                    act.wait_ge(mm_done, b - 1)
                act.activation(w_hi[:, slot, :], w_stage[:, slot, :], ACT.Copy).then_inc(w_hi_done, 1)

            def settle(done=ones_set, value=4):
                act.wait_ge(done, value)

            def next_high(b, turn, slot):
                w_high(b + 1, turn + slot, 1 - slot)

            def square_free(norm, n):
                act.wait_ge(ssq_done, n + (9 * norm + 1))

            def square(src, norm, n, waited=False):
                if not waited:
                    square_free(norm, n)
                act.activation(sqs[:, :], src, ACT.Square).then_inc(sq_done, 1)

            def one(ap, n):
                return ap[:, n:n + 1] if isinstance(n, int) else ap[:, bass.ds(n, 1)]

            def high(hi, src, cbase, n):
                settle()
                act.activation(tile(hi, n), src, ACT.Copy, scale=one(col, n + cbase)).then_inc(operand_hi, 1)

            def inverse_root(norm, users_done):
                if users_done is not None:
                    act.wait_ge(evac_done, users_done)
                act.wait_ge(stat_done, norm + 1)
                link(act.activation(R[:, :], banks(4, 2), ACT.Ln, scale=1.0 / D, bias=eps_c))
                act.activation(R[:, :], R[:, :], ACT.Exp, scale=-0.5).then_inc(r_done, 1)

            act.wait_ge(ones_set, 4)
            act.wait_ge(p_landed, 16)
            w_high(0, 0, 0)
            for k in range(2):
                act.activation(p_hi[:, k, :], p_f[:, k, :], ACT.Copy).then_inc(operand_hi, 1)
            w_high(1, 0, 1)
            act.wait_ge(cst_landed, 32)
            for k in range(DT):
                act.wait_ge(x_landed[k], 16)
                high(opP_hi, X[:, k, :], C_ATTN, k)
                square(X[:, k, :], 0, k)
            w_high(2, 1, 0)
            w_high(3, 1, 1)
            inverse_root(0, None)

            def split(b, n):
                stream(act, b, n, lambda b, turn, n, slot: next_high(b, turn, slot))

            next_high(B_WIN + 1, B_WIN // 2, 1)
            split(B_WIN + 2, 2)
            act.wait_ge(operand_ready, O_WOUT)
            act.wait_ge(evac_done, B_WIN + 3)
            for z in range(3):
                act.activation(LSQ[:, z, :], Z[:, z, :], ACT.Square).then_inc(m["sq"], 1)
            split(B_WIN + 4, 4)
            act.wait_ge(m["stat"], 2)
            for a, width in ((0, 256), (1, 128)):
                act.activation(LRT[:, a, :], banks(4 + 2 * a, 2), ACT.Ln, scale=1.0 / width, bias=eps_c).then_inc(m["ln"], 1)
            act.wait_ge(m["ln"], 2)
            act.activation(LRT[:, :, :], LRT[:, :, :], ACT.Exp, scale=-0.5).then_inc(m["r"], 1)
            split(B_WIN + 8, 4)
            act.wait_ge(g["lin"], 2)
            link(act.activation(E[:, :, :], KE[0][:, :, :], ACT.Abs))
            link(act.activation(E[:, :, :], E[:, :, :], ACT.Exp, scale=-1.0))
            act.activation(E[:, :, :], E[:, :, :], ACT.Ln, bias=one_c).then_inc(g["soft"], 1)
            split(B_WIN + 12, 2)
            for w in range(WIN):
                act.wait_ge(g["tr"], w + 1)
                act.activation(VT[:, w, :], ps[:, 4 + w % 2, :], ACT.Copy).then_inc(g["trc"], 1)
            split(B_WIN + 14, 2)

            act.wait_ge(g["cum"], 4)
            act.activation(E[:, :, :], Bc[:, :, :], ACT.Exp, scale=1.0 / 16).then_inc(g["exps"], 1)
            act.activation(decay.rearrange("p (a c) -> p a c", a=2),
                           Bc[:, :, :].rearrange("p a (c k) -> p a c k", k=CHUNK)[:, :, :, CHUNK - 1],
                           ACT.Exp, scale=1.0 / 16).then_inc(g["exps"], 1)
            act.wait_ge(g["kdec"], 1)
            act.activation(E[:, :, :], E[:, :, :], ACT.Exp, scale=1.0 / 16).then_inc(g["exps"], 1)
            def level(lv):
                act.wait_ge(g["lexp"], 2 * lv + 2)
                act.activation(EX[lv % 2][:, :, :], EX[lv % 2][:, :, :], ACT.Exp, scale=1.0 / 16).then_inc(g["exps"], 1)

            level(0)
            for w in range(WIN):
                act.wait_ge(g["tr"], WIN + w + 1)
                act.activation(KDT[:, w, :], ps[:, w % 2, 0:256], ACT.Copy).then_inc(g["trc"], 1)
            for lv in range(1, len(LEVELS)):
                level(lv)
            act.wait_ge(g["lk"], len(LEVELS))
            for h in range(GH):
                act.activation(head_gate[h], Z[:, 12 + h, :], ACT.Sigmoid).then_inc(g["sig"], 1)

            def root_log(h):
                act.wait_ge(g["nst"], h + 1)
                act.activation(head_root[h], banks(2 * h, 2), ACT.Ln, scale=1.0 / GDV, bias=eps_c).then_inc(g["ln"], 1)

            for h in range(GH):
                act.wait_ge(g["out"], h + 1)
                act.activation(Z[:, 4 + h, :], banks(2 * h, 2), ACT.Copy).then_inc(g["oraw"], 1)
                act.wait_ge(g["oraw"], h + 1)
                if h >= 2:
                    act.wait_ge(g["nst"], h - 1)
                act.activation(SQG[:, h % 2, :], Z[:, 4 + h, :], ACT.Square).then_inc(g["sq"], 1)
                if h:
                    root_log(h - 1)
            root_log(GH - 1)

            def angles():
                act.wait_ge(m["angle"], 1)
                act.activation(SN[64:96, :], ang[64:96, :], ACT.Sin).then_inc(m["sin"], 1)
                link(act.activation(CT[64:96, :], ang[64:96, :], ACT.Abs))
                act.activation(CT[64:96, :], CT[64:96, :], ACT.Sin, scale=-1.0, bias=halfpi_c[64:96, :]).then_inc(m["sin"], 1)

            def evacuate(h, slot, j):
                bank, half = 6 + j % 2, slice(j % 2 * HALF, (j % 2 + 1) * HALF)
                act.wait_ge(m["job"], h * 12 + (j + 1))
                if j < 4:
                    rows = QKD if j < 2 else NOPE
                    act.activation(QK[0:rows, slot, j // 2, half], ps[0:rows, bank, :], ACT.Copy).then_inc(m["jev"], 1)
                    if j == 3:
                        act.activation(QK[64:96, slot, 1, :], Z[64:96, 3, :], ACT.Copy).then_inc(m["krot"], 1)
                        act.wait_ge(m["krot"], h + 1)
                    if j % 2 == 1:
                        act.wait_ge(m["jev"], h * 12 + (j + 1))
                        act.activation(SQ[0:QKD, j // 2, :], QK[0:QKD, slot, j // 2, :], ACT.Square).then_inc(m["sq"], 1)
                elif j >= 8:
                    act.activation(VA[:, slot, 4 * (j - 8):4 * (j - 7), 64 * slot:64 * slot + 64],
                                   ps[:, bank, 0:256].rearrange("p (a b) -> p a b", a=4), ACT.Copy).then_inc(m["jev"], 1)
                else:
                    a = (j - 4) // 2
                    act.activation(RR[0:QKD, a, half], ps[0:QKD, bank, :], ACT.Ln, scale=1.0 / QKD, bias=eps_c[0:QKD, :])\
                       .then_inc(m["jev"], 1)
                    if j == 7:
                        act.wait_ge(m["jev"], h * 12 + 8)
                        act.activation(RR[0:QKD, :, :], RR[0:QKD, :, :], ACT.Exp, scale=-0.5).then_inc(m["rr"], 1)

            def rows_in(h, slot, more, r):
                act.wait_ge(m["job"], h * 12 + (12 + (10 if more else 0) + r + 1))
                act.activation(QK[96:97, slot, 0, r * HALF:(r + 1) * HALF], ps[0:1, 6 + r, :], ACT.Copy).then_inc(m["jev"], 1)

            def head(h, slot, more):
                if more:
                    for j in range(10):
                        evacuate(h + 1, 1 - slot, j)
                for r in range(2):
                    rows_in(h, slot, more, r)
                for u, (half, kt, q0, width) in enumerate(PIECES_T):
                    act.wait_ge(m["st"], h * 12 + (u + 2))
                    act.wait_ge(m["pv"], h * 12 + (u + 1))
                    act.activation(PT[:, u % 4, 0:width], ps[:, 2 + u % 2, 0:width], ACT.Exp, scale=1.0 / math.sqrt(QKD))\
                       .then_inc(m["exp"], 1)
                    if isinstance(h, int) and h == 0 and u % 2 and u < 8:
                        k = u // 2
                        act.wait_ge(g["fin"], k + 1)
                        act.activation(opP_hi[:, 4 + k, :], Z[:, 12 + k, :], ACT.Copy).then_inc(operand_hi, 1)

            act.sem_inc(m["exp"], 2)
            act.wait_ge(g["gated"], GH)
            for j in range(10):
                evacuate(0, 0, j)
            angles()
            act.wait_ge(g["ln"], GH)
            for h in range(GH):
                act.activation(head_root[h], head_root[h], ACT.Exp, scale=-0.5).then_inc(g["rn"], 1)
            act.wait_ge(m["jev"], 10)
            act.sem_inc(m["jev"], 2)
            head(0, 0, True)
            with act.Fori(0, 3) as i:
                head(i * 2 + 1, 1, True)
                head(i * 2 + 2, 0, True)
            head(7, 1, False)

            act.wait_ge(m["rope"], MH)
            for k in range(4):
                act.wait_ge(m["ofree"], 4 * k + 6)
                act.activation(opP_hi[:, k, :], Z[:, 8 + k, :], ACT.Copy).then_inc(operand_hi, 1)

            def wout_step(b, turn, n, slot):
                next_high(b, turn, slot)
                act.wait_ge(evac_done, b + 1)
                square_free(1, n)
                high(opQ_hi, tile(X, n), C_MLP, n)
                square(tile(X, n), 1, n, True)
            act.wait_ge(operand_ready, O_UP1)
            stream(act, B_WOUT, 8, wout_step)
            next_high(B_MLP1, B_MLP1 // 2, 0)
            inverse_root(1, B_MLP1)

            def mlp(b0, hi, count0, last_group_steps):
                def up(gi):
                    def body(b, turn, n, slot, split_next=True):
                        if split_next:
                            next_high(b, turn, slot)
                        act.wait_ge(relu_sq, gi * 8 + n + (count0 + 1))
                        settle()
                        act.activation(tile(hi, n), T[:, slot, :], ACT.Copy).then_inc(operand_hi, 1)
                    return body

                def down(b, turn, n, slot):
                    next_high(b, turn, slot)

                def run(gi, off, body):
                    with act.Fori(0, 4) as i:
                        for j in range(2):
                            body(gi * 16 + i * 2 + (b0 + off + j), gi * 8 + i + (b0 + off) // 2, i * 2 + j, j)
                normed(act, b0, 8, up(0))
                run(0, 8, down)
                with act.Fori(1, 3) as gi:
                    run(gi, 0, up(gi))
                    run(gi, 8, down)
                run(3, 0, up(3))
                last_group_steps()

            def down1():
                def body(b, turn, n, slot):
                    next_high(b, turn, slot)
                    act.wait_ge(evac_done, b + 1)
                    square_free(2, n)
                    high(opQ_hi, tile(X, n), C_PLE, n)
                    square(tile(X, n), 2, n, True)
                stream(act, B_MLP1 + 56, 8, body)

            mlp(B_MLP1, opP_hi, 0, down1)
            next_high(B_GATE, B_GATE // 2, 0)
            inverse_root(2, B_GATE)

            def gate_step(b, turn, n, slot, split_next=True):
                if split_next:
                    next_high(b, turn, slot)
                act.wait_ge(evac_done, b + 1)
                settle()
                act.activation(T[:, 0, :], T[:, 0, :], ACT.Sigmoid, bias=one(col, n + C_BPLE)).then_inc(gated, 1)
                act.wait_ge(x_upd, n + 1)
                square_free(3, n)
                high(opP_hi, tile(X, n), C_MIXPRE, n)
                square(tile(X, n), 3, n, True)
            normed(act, B_GATE, 8, gate_step)
            next_high(B_WIN2, B_WIN2 // 2, 0)
            inverse_root(3, B_WIN2)

            def win2_step(b, turn, n, slot, split_next=True):
                if split_next:
                    next_high(b, turn, slot)
                act.wait_ge(evac_done, b + 1)
                settle()
                act.activation(tile(Z2, n), tile(Z2, n), ACT.Identity, bias=one(col, n + C_BIN)).then_inc(s["z"], 1)
            normed(act, B_WIN2, 10, win2_step)

            act.wait_ge(s["spill"], 16)
            for gi in range(4):
                act.wait_ge(s["pmm"], gi + 1)
                act.activation(X[:, gi, :], banks(2 * (gi % 2), 2), ACT.Copy,
                               scale=col[:, C_POOLS + gi:C_POOLS + gi + 1]).then_inc(s["y"], 1)
            for w in range(2):
                act.wait_ge(s["vtr"], w + 1)
                act.activation(vpad[:, 1 + 4 * w:5 + 4 * w, :].rearrange("p a b -> p (a b)"), ps[:, 4 + w, :], ACT.Copy)\
                   .then_inc(s["vtc"], 1)
            act.wait_ge(s["rope"], 2)
            act.wait_ge(r_done, 4)

            def blocks_in(n, slot):
                if not isinstance(n, int) or n >= 2:
                    act.wait_ge(s["qk"], n - 1)
                cols = bass.ds(n * P, P)
                settle()
                act.activation(qb2[:, slot, :, :], Z2[:, 4:8, cols], ACT.Copy).then_inc(s["blk"], 1)
                act.activation(kb2[:, slot, :], kpad[:, bass.ds(n * P, 2 * P)], ACT.Copy).then_inc(s["blk"], 1)

            def values_in(n, slot):
                if not isinstance(n, int) or n >= 2:
                    act.wait_ge(s["pv"], n)
                settle()
                act.activation(vb2[:, slot, :, :], vpad[:, bass.ds(n, 2), :], ACT.Copy).then_inc(s["vb"], 1)

            def weights(n):
                act.wait_ge(s["mx"], n + 1)
                if not isinstance(n, int) or n >= 1:
                    act.wait_ge(s["tra"], n * 4)
                    act.wait_ge(s["den"], n)
                for h in range(NQ):
                    act.activation(P2[:, h, :], S2[:, h, :], ACT.Exp, bias=nm8[:, h:h + 1], accum_out=d8[:, h:h + 1])\
                       .then_inc(s["exp"], 1)
                act.activation(e8, m8, ACT.Exp).then_inc(s["exp"], 1)

            def attend(n, slot, more, blocks):
                if blocks:
                    blocks_in(n + 2, slot)
                for q in range(4):
                    act.wait_ge(s["tra"], n * 4 + (q + 1))
                    if q == 0:
                        act.wait_ge(s["pv"], n + 1)
                    act.activation(PT2[:, 2 * q:2 * q + 2, :, :].rearrange("p a b c -> p (a b c)"), ps[:, 4 + q % 2, :],
                                   ACT.Copy).then_inc(s["tca"], 1)
                if more:
                    weights(n + 1)
                act.wait_ge(s["pv"], n + 2)
                settle()
                act.activation(X[:, 4:8, bass.ds(n * P, P)], ps[:, 6 + slot, :].rearrange("p (a b) -> p a b", a=4), ACT.Copy)\
                   .then_inc(s["otc"], 1)
                if blocks:
                    values_in(n + 2, slot)

            act.sem_inc(s["otc"], 1)
            blocks_in(0, 0)
            blocks_in(1, 1)
            act.wait_ge(s["vtc"], 2)
            act.wait_ge(s["zero"], 4)
            values_in(0, 0)
            values_in(1, 1)
            weights(0)
            with act.Fori(0, 3) as i:
                attend(i * 2, 0, True, True)
                attend(i * 2 + 1, 1, True, True)
            attend(6, 0, True, False)
            attend(7, 1, False, False)

            def split_y(k):
                if k == 0:
                    act.wait_ge(s["y"], 4)
                if k == 4:
                    act.wait_ge(s["otc"], 9)
                act.activation(opQ_hi[:, k, :], X[:, k, :], ACT.Copy).then_inc(operand_hi, 1)

            def merged(i, first):
                for j in range(2):
                    for q in range(3):
                        o = 3 * j + q
                        next_high(i * 6 + (B_MRG + o), i * 3 + (B_MRG + o) // 2, o % 2)
                        if first and o < 2:
                            for k in range(4 * o, 4 * o + 4):
                                split_y(k)
                        if q < 2:
                            act.wait_ge(evac_done, i * 6 + (B_MRG + o + 1))
                            settle()
                            act.activation(T[:, q, :], T[:, q, :], ACT.Sigmoid,
                                           bias=one(col, i * 2 + (C_BIN + 10 + 8 * q + j))).then_inc(s["sig"], 1)
            merged(0, True)
            with act.Fori(1, 4) as i:
                merged(i, False)

            for k in range(DT):
                act.wait_ge(s["mrg"], k + 2)
                if k == 0:
                    act.wait_ge(mm_done, B_WO2)
                act.activation(opQ_hi[:, k, :], X[:, k, :], ACT.Copy).then_inc(operand_hi, 1)

            def wo2_step(b, turn, n, slot):
                next_high(b, turn, slot)
                act.wait_ge(evac_done, b + 1)
                square(tile(X, n), 4, n)
            act.wait_ge(operand_ready, O_UP2)
            stream(act, B_WO2, 8, wo2_step)
            next_high(B_MLP2, B_MLP2 // 2, 0)
            inverse_root(4, B_MLP2)
            for k in range(DT):
                act.wait_ge(s["mt"], k + 1)
                high(opP_hi, X[:, k, :], C_MLPPRE, k)
                if k >= 2:
                    act.wait_ge(s["sqsum"], k - 1)
                act.activation((sqs if k % 2 == 0 else ssq)[:, :], X[:, k, :], ACT.Square).then_inc(sq_done, 1)
            act.wait_ge(s["scaled"], DT)
            inverse_root(5, B_MLP2)

            def down2():
                def body(b, turn, n, slot):
                    next_high(b, turn, slot)
                    act.wait_ge(evac_done, b + 1)
                    square(tile(X, n), 6, n)
                stream(act, B_MLP2 + 56, 6, body)
                body(B_END - 2, B_END // 2 - 1, 6, 0)
                act.wait_ge(evac_done, B_END)
                square(X[:, 7, :], 6, 7)

            mlp(B_MLP2, opQ_hi, 32, down2)
            inverse_root(6, B_END)

        @block.vector
        def _(v):
            link = Link(v, dve_step)

            def w_low(b, turn, slot):
                v.wait_ge(w_hi_done, b + 1)
                v.tensor_tensor(w_lo[:, slot, :], w_stage[:, slot, :], w_hi[:, slot, :].bitcast(F32), ALU.subtract)\
                 .then_inc(w_lo_done, 1)

            def next_low(b, turn, slot):
                w_low(b + 1, turn, 1 - slot)

            def one(ap, n):
                return ap[:, n:n + 1] if isinstance(n, int) else ap[:, bass.ds(n, 1)]

            def low(hi, lo, src, count, n, cbase=None):
                v.wait_ge(operand_hi, n + (count + 1))
                h = tile(hi, n).bitcast(F32)
                if cbase is None:
                    ins = v.tensor_tensor(tile(lo, n), src, h, ALU.subtract)
                else:
                    ins = v.scalar_tensor_tensor(tile(lo, n), src, one(col, n + cbase), h, ALU.mult, ALU.subtract)
                ins.then_inc(operand_ready, 1)

            def add_square(norm, n):
                v.wait_ge(ssq_done, n + (9 * norm + 1))
                v.wait_ge(sq_done, n + (8 * norm + 1))
                v.tensor_tensor(ssq[:, :], ssq[:, :], sqs[:, :], ALU.add).then_inc(ssq_done, 1)

            def zero_squares(norm):
                if norm:
                    v.wait_ge(stat_done, norm)
                v.memset(ssq[:, :], 0.0).then_inc(ssq_done, 1)

            zero_squares(0)
            w_low(0, 0, 0)
            for k in range(2):
                low(p_hi, p_lo, p_f[:, k, :], O_PP, k)
            w_low(1, 0, 1)
            v.wait_ge(cst_landed, 32)

            def pp_out(n):
                v.wait_ge(pp_mm, n + 1)
                v.tensor_copy(ppout[:, n, :], banks(2 * (n % 4), 2)).then_inc(pp_evac, 1)

            for k in range(DT):
                low(opP_hi, opP_lo, X[:, k, :], O_WIN, k, C_ATTN)
                add_square(0, k)
                if k % 2:
                    pp_out(k // 2)
            w_low(2, 1, 0)
            for n in range(4, DT):
                pp_out(n)
            v.wait_ge(pp_evac, 8)
            v.sem_inc(evac_done, 2)

            next_low(B_WIN, None, 0)
            v.wait_ge(r_done, 1)
            v.wait_ge(pp_spilled, 16)

            def win_step(b, turn, n, slot, split_next=True):
                if split_next:
                    next_low(b, turn, slot)
                v.wait_ge(mm_done, b + 1)
                v.tensor_tensor(tile(Z, n), banks(2 * slot, 2), R[:, :], ALU.mult).then_inc(evac_done, 1)
            normed(v, B_WIN, 4, win_step)
            v.wait_ge(m["sq"], 2)
            v.tensor_tensor(LSQ[:, 0, :], LSQ[:, 0, :], LSQ[:, 1, :], ALU.add).then_inc(m["lat"], 1)
            stream(v, B_WIN + 4, 4, win_step, 4)
            v.wait_ge(m["r"], 1)
            v.wait_ge(evac_done, B_WIN + 3)
            for z in range(3):
                v.scalar_tensor_tensor(Z[:, z, :], Z[:, z, :], col[:, C_QN + z:C_QN + z + 1], LRT[:, z // 2, :],
                                       ALU.mult, ALU.mult).then_inc(m["lat"], 1)
            stream(v, B_WIN + 8, 4, win_step, 8)
            v.wait_ge(g["logit"], 2)
            for pr in range(2):
                v.tensor_scalar(KE[0][:, pr, :], banks(4 + 2 * pr, 2), col[:, C_GATEB + pr:C_GATEB + pr + 1], None,
                                ALU.add).then_inc(g["lin"], 1)
            stream(v, B_WIN + 12, 2, win_step, 12)
            v.wait_ge(g["soft"], 1)
            kef = KE[0][:, :, :].rearrange("p a b -> p (a b)")
            v.wait_ge(g["lin"], 2)
            link(v.scalar_tensor_tensor(kef, kef, 0.0, E[:, :, :].rearrange("p a b -> p (a b)"), ALU.min, ALU.subtract))
            v.wait_ge(m["lat"], 4)
            v.wait_ge(g["cum"], 1)
            for pr in range(2):
                v.tensor_tensor_scan(Bc[:, pr, :], reset[:, :], KE[0][:, pr, :], 0.0, ALU.mult, ALU.add).then_inc(g["cum"], 1)
            v.wait_ge(g["cum"], 3)
            v.sem_inc(g["cum"], 1)
            stream(v, B_WIN + 14, 2, win_step, 14)

            v.wait_ge(evac_done, B_WOUT)
            q_t, k_t = Z[:, 4:6, :], Z[:, 6:8, :]
            chunks = [P, 2 * NCH, CHUNK]
            Bf = Bc[:, :, :].rearrange("p a (c k) -> p (a c) k", k=CHUNK)
            Ef = E[:, :, :].rearrange("p a (c k) -> p (a c) k", k=CHUNK)
            v.wait_ge(g["exps"], 2)
            v.scalar_tensor_tensor(QX[:, :, :].rearrange("p a b -> p (a b)"), q_t.rearrange("p a b -> p (a b)"),
                                   GDK ** -0.5, E[:, :, :].rearrange("p a b -> p (a b)"), ALU.mult, ALU.mult)\
             .then_inc(g["states"], 1)
            v.wait_ge(g["states"], 1)
            v.tensor_tensor(Ef, bc(Bf[:, :, CHUNK - 1:CHUNK], chunks), Bf, ALU.subtract).then_inc(g["kdec"], 1)

            def exponents(lv):
                size = LEVELS[lv]
                nodes = 2 * S // (2 * size)
                Bn = Bc[:, :, :].rearrange("p a b -> p (a b)").rearrange("p (n s l) -> p n s l", s=2, l=size)
                En = EX[lv % 2][:, :, :].rearrange("p a b -> p (a b)").rearrange("p (n s l) -> p n s l", s=2, l=size)
                mid = bc(Bn[:, :, 0, size - 1:size], [P, nodes, size])
                if lv >= 2:
                    v.wait_ge(g["lk"], lv - 1)
                elif lv == 1:
                    v.wait_ge(g["kdec"], 2)
                v.tensor_tensor(En[:, :, 1, :], Bn[:, :, 1, :], mid, ALU.subtract).then_inc(g["lexp"], 1)
                v.tensor_tensor(En[:, :, 0, :], mid, Bn[:, :, 0, :], ALU.subtract).then_inc(g["lexp"], 1)

            def factors(lv):
                size = LEVELS[lv]
                v.wait_ge(g["exps"], 4 + lv)
                if lv == 0:
                    v.wait_ge(g["tr"], 2 * WIN)
                if lv >= 2:
                    v.wait_ge(g["lmm"], 1 + lv)
                else:
                    v.wait_ge(g["zero"], 2)
                for par in range(2):
                    r = slice(64 * par, 64 * par + 64)
                    dst = QE[lv % 2][r, :, :, par, :].rearrange("p a w t -> p (a w) t").rearrange("p x (n l) -> p x n l", l=size)
                    qh = q_t[r].rearrange("p a b -> p (a b)").rearrange("p (x n s l) -> p x n s l", x=2 * WIN, s=2, l=size)
                    eh = EX[lv % 2][r, :, :].rearrange("p a b -> p (a b)").rearrange("p (x n s l) -> p x n s l", x=2 * WIN, s=2, l=size)
                    v.scalar_tensor_tensor(dst, qh[:, :, :, 1, :], GDK ** -0.5, eh[:, :, :, 1, :], ALU.mult, ALU.mult)\
                     .then_inc(g["lq"], 1)
                left = lambda ap: ap.rearrange("p a b -> p (a b)").rearrange("p (n s l) -> p n s l", s=2, l=size)[:, :, 0, :]
                if lv == 1:
                    v.tensor_tensor(KE[1][:, :, :], k_t, EX[1][:, :, :], ALU.mult).then_inc(g["lk"], 1)
                else:
                    v.tensor_tensor(left(KE[lv % 2][:, :, :]), left(k_t), left(EX[lv % 2][:, :, :]), ALU.mult).then_inc(g["lk"], 1)

            exponents(0)
            def diagonal(hf):
                v.wait_ge(g["lmm"], hf + 1)
                v.tensor_tensor(SC[:, hf, :, :, :].rearrange("p a w t -> p (a w) t"),
                                banks(4 * hf, 4).rearrange("p (x t) -> p x t", t=P),
                                bc(dmask[:, :].unsqueeze(1), [P, 2 * WIN, P]), ALU.mult).then_inc(g["lcp"], 1)
            v.wait_ge(g["consts"], 32)
            diagonal(0)
            v.wait_ge(g["exps"], 3)
            v.tensor_tensor(KE[0][:, :, :], k_t, E[:, :, :], ALU.mult).then_inc(g["kdec"], 1)
            exponents(1)
            diagonal(1)
            for pr in range(2):
                v.memset(ST8[:, pr, 0, :], 0.0).then_inc(g["states"], 1)

            def states(pr):
                v.wait_ge(g["upd"], pr + 1)
                for c in range(NCH - 1):
                    v.wait_ge(g["states"], 3 + pr * 15 + c if c else 3)
                    bank = 4 + 2 * (c % 2) + (c // 2) // 4
                    u = ps[:, bank, ((c // 2) % 4) * P:((c // 2) % 4 + 1) * P]
                    v.scalar_tensor_tensor(ST8[:, pr, c + 1, :], ST8[:, pr, c, :], decay[:, pr * NCH + c:pr * NCH + c + 1],
                                           u, ALU.mult, ALU.add).then_inc(g["states"], 1)

            def merge(lv, pr):
                size = LEVELS[lv]
                v.wait_ge(g["lmm"], 3 + lv)
                v.wait_ge(g["lcp"], 2 + 2 * lv + pr)
                right = SC[:, :, pr, :, :].rearrange("p b w (n s l) -> p b w n s l", s=2, l=size)[:, :, :, :, 1, :]
                msk = lmask[:, lv, :].rearrange("p (n l) -> p n l", l=size)
                src = banks(2 * pr, 2).rearrange("p (w b n l) -> p b w n l", w=WIN, b=2, l=size)
                for par in range(2):
                    ins = v.copy_predicated(right[:, par], bc(msk.unsqueeze(1), [P, WIN, CHUNK // size, size]), src[:, par])
                ins.then_inc(g["lcp"], 1)

            last = len(LEVELS) - 1
            factors(0)
            states(0)
            for lv in range(len(LEVELS)):
                if lv + 2 <= last:
                    exponents(lv + 2)
                merge(lv, 0)
                if lv < last:
                    factors(lv + 1)
                merge(lv, 1)
                if lv == 0:
                    states(1)
            for h in range(GH):
                gr = Z[:, 12 + h, :]
                v.wait_ge(g["sig"], h + 1)
                v.tensor_tensor(gr, gr, head_gate[h], ALU.mult).then_inc(g["gated"], 1)
            v.wait_ge(m["misc"], 32)
            rows = slice(64, 96)
            link(v.tensor_copy(ang[rows, :], pos_i[rows, :]))
            link(v.tensor_scalar(ang[rows, :], ang[rows, :], freq[rows, :], None, ALU.mult))
            link(v.tensor_scalar(kf[rows, :], ang[rows, :], 1.0 / (2 * math.pi), None, ALU.mult))
            link(v.tensor_copy(ki[rows, :], kf[rows, :]))
            link(v.tensor_copy(kf[rows, :], ki[rows, :]))
            c1 = 6.28125
            c2 = float(np.float32(np.round((2 * math.pi - c1) * 2 ** 20) / 2 ** 20))
            c3 = 2 * math.pi - c1 - c2
            for c in (c1, c2, c3):
                link(v.scalar_tensor_tensor(ang[rows, :], kf[rows, :], -c, ang[rows, :], ALU.mult, ALU.add))
            pi32 = float(np.nextafter(np.float32(math.pi), np.float32(0)))
            v.tensor_scalar(ang[rows, :], ang[rows, :], pi32, -pi32, ALU.min, ALU.max).then_inc(m["angle"], 1)
            def normalise(h, slot):
                v.wait_ge(m["rr"], h + 1)
                for a in range(2):
                    qk = QK[0:QKD, slot, a, :]
                    gain = col[0:QKD, C_QKQ + a:C_QKQ + a + 1]
                    v.scalar_tensor_tensor(qk, qk, gain, RR[0:QKD, a, :], ALU.mult, ALU.mult).then_inc(m["nrm"], 1)

            def rotate(h, slot):
                qk = QK[rows, slot, :, :]
                v.wait_ge(m["nrm"], h * 2 + 2)
                v.wait_ge(m["swap"], h * 32 + 32)
                if isinstance(h, int) and h == 0:
                    v.wait_ge(m["sin"], 2)
                v.tensor_tensor(qk, qk, bc(CT[rows, :].unsqueeze(1), [ROPE, 2, S]), ALU.mult).then_inc(m["angle"], 1)
                v.wait_ge(m["angle"], h + 2)
                v.wait_ge(m["swn"], h + 1)
                v.tensor_tensor(qk, qk, SW[rows, :, :], ALU.add).then_inc(m["rope"], 1)

            def maximum(h, u):
                qt, c0, width = PIECES[u]
                sc = ps[:, u % 2, 0:width]
                v.wait_ge(m["scores"], h * 12 + (u + 1))
                if c0 + width == (qt + 1) * P:
                    v.memset(sc[0:64, width - 64:width], NEG).then_inc(m["corner"], 1)
                    v.wait_ge(m["corner"], h * 8 + (qt + 1))
                dst = mx8[:, qt:qt + 1] if c0 == 0 else mxb[:, qt - 4:qt - 3]
                v.tensor_reduce(dst, sc, AX_X, ALU.max).then_inc(m["red"], 1)

            def invert(h, slot, half, piece, pieces):
                o, sums = slice(64 * slot, 64 * slot + 64), slice(64 - 64 * slot, 128 - 64 * slot)
                c = slice(piece * HALF // pieces, (piece + 1) * HALF // pieces)
                if piece == 0:
                    v.wait_ge(m["pv"], h * 12 + (8 if half == 0 else 16))
                    v.wait_ge(m["ofree"], h * 2 + (2 + half))
                ins = v.reciprocal(T[o, half, c], ps[sums, 4 + half, c])
                if piece == pieces - 1:
                    ins.then_inc(m["inv"], 1)

            def divide(h, n, slot, half):
                o = slice(64 * slot, 64 * slot + 64)
                v.wait_ge(m["inv"], h * 2 + (1 + half))
                dst = Z[o, 8 + n, half * HALF:(half + 1) * HALF] if isinstance(n, int) else \
                    Z[o, bass.ds(n + 8, 1), half * HALF:(half + 1) * HALF].rearrange("p a b -> p (a b)")
                v.tensor_tensor(dst, ps[o, 4 + half, :], T[o, half, 0:HALF], ALU.mult).then_inc(m["ofree"], 1)

            def gla_out(step):
                h = step // 2
                o, gr = Z[:, 4 + h, :], Z[:, 12 + h, :]
                if step % 2 == 0:
                    v.wait_ge(g["rn"], h + 1)
                    v.scalar_tensor_tensor(o, o, col[:, C_GOUT:C_GOUT + 1], head_root[h], ALU.mult, ALU.mult)\
                     .then_inc(g["normed"], 1)
                else:
                    v.wait_ge(g["normed"], h + 1)
                    v.wait_ge(g["gated"], h + 1)
                    v.tensor_tensor(gr, gr, o, ALU.mult).then_inc(g["fin"], 1)

            def head(h, n, n_before, slot, first, more):
                for u in range(12):
                    maximum(h, u)
                    if first and u < 8:
                        gla_out(u)
                    if u == 3:
                        v.wait_ge(m["red"], h * 12 + 6)
                        v.sem_inc(m["mx"], 1)
                    if 3 <= u < 7 and not first:
                        invert(h - 1, 1 - slot, 1, u - 3, 4)
                    if u == 8 and not first:
                        divide(h - 1, n_before, 1 - slot, 1)
                v.wait_ge(m["red"], h * 12 + 14)
                v.tensor_tensor(mx8[:, 4:8], mx8[:, 4:8], mxb, ALU.max).then_inc(m["mx"], 1)
                if more:
                    normalise(h + 1, 1 - slot)
                invert(h, slot, 0, 0, 1)
                divide(h, n, slot, 0)
                if more:
                    rotate(h + 1, 1 - slot)
                if first:
                    for k in range(4):
                        v.wait_ge(operand_hi, O_WOUT + k + 1)
                        v.tensor_tensor(opP_lo[:, 4 + k, :], Z[:, 12 + k, :], opP_hi[:, 4 + k, :].bitcast(F32), ALU.subtract)\
                         .then_inc(operand_ready, 1)

            v.sem_inc(m["red"], 2)
            v.sem_inc(m["ofree"], 2)
            v.wait_ge(m["lat"], 4)
            normalise(0, 0)
            rotate(0, 0)
            head(0, 0, None, 0, True, True)
            with v.Fori(0, 3) as i:
                head(i * 2 + 1, i, i, 1, False, True)
                head(i * 2 + 2, i + 1, i, 0, False, True)
            head(7, 3, 3, 1, False, False)
            invert(7, 1, 1, 0, 1)
            divide(7, 3, 1, 1)

            for k in range(4):
                v.wait_ge(operand_hi, O_WOUT + 5 + k)
                v.tensor_tensor(opP_lo[:, k, :], Z[:, 8 + k, :], opP_hi[:, k, :].bitcast(F32), ALU.subtract)\
                 .then_inc(operand_ready, 1)
            zero_squares(1)

            def wout_step(b, turn, n, slot):
                next_low(b, turn, slot)
                v.wait_ge(mm_done, b + 1)
                v.wait_ge(x_back[slot], turn * 16 - (B_WOUT * 8 - 16))
                v.tensor_tensor(tile(X, n), tile(X, n), banks(2 * slot, 2), ALU.add).then_inc(evac_done, 1)
                v.wait_ge(evac_done, b + 1)
                low(opQ_hi, opQ_lo, tile(X, n), O_UP1, n, C_MLP)
                add_square(1, n)
            stream(v, B_WOUT, 8, wout_step)

            def mlp(b0, norm, hi, lo, count0, ready0, down, last):
                if norm == 1:
                    next_low(b0, None, 0)
                v.wait_ge(r_done, norm + 1)

                def up(gi):
                    def body(b, turn, n, slot, split_next=True):
                        if split_next:
                            next_low(b, turn, slot)
                        v.wait_ge(mm_done, b + 1)
                        v.wait_ge(operand_hi, gi * 8 + n + (ready0 - 1))
                        tt = T[:, slot, :]
                        v.tensor_tensor(tt, banks(2 * slot, 2), R[:, :], ALU.mult).then_inc(evac_done, 1)
                        v.wait_ge(evac_done, b + 1)
                        v.scalar_tensor_tensor(tt, tt, 0.0, tt, ALU.max, ALU.mult).then_inc(relu_sq, 1)
                        v.wait_ge(relu_sq, gi * 8 + n + (count0 + 1))
                        v.wait_ge(operand_hi, gi * 8 + n + (ready0 + 1))
                        v.tensor_tensor(tile(lo, n), tt, tile(hi, n).bitcast(F32), ALU.subtract).then_inc(operand_ready, 1)
                    return body

                def run(gi, off, body, turns=4):
                    with v.Fori(0, turns) as i:
                        for j in range(2):
                            body(gi * 16 + i * 2 + (b0 + off + j), gi * 8 + i + (b0 + off) // 2, i * 2 + j, j)
                normed(v, b0, 8, up(0))
                if down is not None:
                    run(0, 8, down)
                else:
                    v.wait_ge(x2_spilled, 16)
                    run(0, 8, first_down)
                with v.Fori(1, 3) as gi:
                    run(gi, 0, up(gi))
                    run(gi, 8, acc_down)
                run(3, 0, up(3))
                zero_squares(2 if down is not None else 6)
                last()

            def acc_down(b, turn, n, slot):
                next_low(b, turn, slot)
                v.wait_ge(mm_done, b + 1)
                v.tensor_tensor(tile(X, n), tile(X, n), banks(2 * slot, 2), ALU.add).then_inc(evac_done, 1)

            def first_down(b, turn, n, slot):
                next_low(b, turn, slot)
                v.wait_ge(mm_done, b + 1)
                v.tensor_copy(tile(X, n), banks(2 * slot, 2)).then_inc(evac_done, 1)

            def down1():
                def body(b, turn, n, slot):
                    acc_down(b, turn, n, slot)
                    v.wait_ge(evac_done, b + 1)
                    low(opQ_hi, opQ_lo, tile(X, n), O_GATE, n, C_PLE)
                    add_square(2, n)
                stream(v, B_MLP1 + 56, 8, body)

            mlp(B_MLP1, 1, opP_hi, opP_lo, 0, O_H1, acc_down, down1)

            next_low(B_GATE, None, 0)
            zero_squares(3)
            v.wait_ge(r_done, 3)

            def gate_step(b, turn, n, slot, split_next=True):
                if split_next:
                    next_low(b, turn, slot)
                v.wait_ge(mm_done, b + 1)
                v.tensor_tensor(T[:, 0, :], banks(2 * slot, 2), R[:, :], ALU.mult).then_inc(evac_done, 1)
                v.wait_ge(gated, n + 1)
                v.wait_ge(pp_back, n * 16 + 16)
                v.tensor_tensor(T[:, 0, :], T[:, 0, :], T[:, 1, :], ALU.mult).then_inc(pp_used, 1)
                v.wait_ge(pp_used, n + 1)
                v.tensor_tensor(tile(X, n), tile(X, n), T[:, 0, :], ALU.add).then_inc(x_upd, 1)
                v.wait_ge(x_upd, n + 1)
                low(opP_hi, opP_lo, tile(X, n), O_WIN2, n, C_MIXPRE)
                add_square(3, n)
            normed(v, B_GATE, 8, gate_step)

            next_low(B_WIN2, None, 0)
            v.wait_ge(r_done, 4)
            v.wait_ge(mm_done, B_WIN2)

            def win2_step(b, turn, n, slot, split_next=True):
                if split_next:
                    next_low(b, turn, slot)
                v.wait_ge(mm_done, b + 1)
                v.tensor_tensor(tile(Z2, n), banks(2 * slot, 2), R[:, :], ALU.mult).then_inc(evac_done, 1)
            def pooled(gi):
                width = POOL_W[gi]
                v.wait_ge(s["z"], gi + 1)
                u = Z2[:, gi, :]
                src, step, slot = u, 1, 0
                while step < width:
                    dst = T[:, slot, :]
                    v.tensor_copy(dst[:, 0:step], src[:, 0:step]).then_inc(dve_step, 1)
                    link.n += 1
                    link(v.tensor_tensor(dst[:, step:S], src[:, step:S], src[:, 0:S - step], ALU.add))
                    src, step, slot = dst, step * 2, 1 - slot
                head = T[:, slot, 0:16]
                link(v.tensor_tensor(head, src[:, 0:16], icnt[:, gi, :], ALU.mult))
                v.tensor_tensor(u[:, 0:16], head, u[:, 0:16], ALU.subtract).then_inc(dve_step, 1)
                link.n += 1
                v.scalar_tensor_tensor(u[:, 16:S], src[:, 16:S], 1.0 / width, u[:, 16:S], ALU.mult, ALU.subtract)\
                 .then_inc(s["pool"], 1)
                v.wait_ge(s["pool"], gi + 1)
                v.wait_ge(dve_step, link.n)

            for n in range(0, 10, 2):
                if n:
                    if n == 2:
                        v.wait_ge(s["consts"], 64)
                    pooled(n // 2 - 1)
                for j in range(2):
                    win2_step(B_WIN2 + n + j, None, n + j, j, n + j > 0)
            v.wait_ge(s["swap"], 128)
            q_z = Z2[:, 4:8, :]
            v.wait_ge(s["z"], 9)
            v.tensor_tensor(Z2[:, 8, :], Z2[:, 8, :], tabC[:, :], ALU.mult).then_inc(dve_step, 1)
            link.n += 1
            link(v.tensor_tensor(q_z, q_z, bc(tabC[:, :].unsqueeze(1), [P, 4, S]), ALU.mult))
            v.wait_ge(s["swn"], 1)
            v.tensor_tensor(q_z, q_z, swq[:, :, :], ALU.add).then_inc(s["rope"], 1)
            v.wait_ge(s["swn"], 2)
            v.tensor_tensor(kpad[:, P:P + S], Z2[:, 8, :], swk[:, :], ALU.add).then_inc(s["rope"], 1)
            v.wait_ge(s["rope"], 2)
            v.wait_ge(s["consts"], 80)

            sink = col[:, C_SINK:C_SINK + NQ]

            def shift(n, first):
                v.wait_ge(s["qk"], n + 1)
                if not isinstance(n, int) or n >= 1:
                    v.wait_ge(s["exp"], n * 9)
                mk = mask2[:, 0 if first else 1, :]
                v.scalar_tensor_tensor(S2[:, :, :], banks(0, 4).rearrange("p (h k) -> p h k", k=256), HD ** -0.5,
                                       bc(mk.unsqueeze(1), [P, NQ, 256]), ALU.mult, ALU.add).then_inc(s["sc"], 1)
                v.wait_ge(s["sc"], n * 5 + 1)
                v.tensor_reduce(m8, S2[:, :, :], AX_X, ALU.max).then_inc(s["sc"], 1)
                v.wait_ge(s["sc"], n * 5 + 2)
                v.tensor_tensor(m8, m8, sink, ALU.max).then_inc(s["sc"], 1)
                v.wait_ge(s["sc"], n * 5 + 3)
                v.tensor_scalar(nm8, m8, -1.0, None, ALU.mult).then_inc(s["sc"], 1)
                v.wait_ge(s["sc"], n * 5 + 4)
                v.tensor_tensor(m8, sink, m8, ALU.subtract).then_inc(s["mx"], 1)

            def reciprocals(n):
                v.wait_ge(s["exp"], n * 9 + 9)
                v.tensor_tensor(r8, d8, e8, ALU.add).then_inc(s["sc"], 1)
                v.wait_ge(s["sc"], n * 5 + 5)
                v.reciprocal(r8, r8).then_inc(s["den"], 1)
                v.wait_ge(s["den"], n + 1)
                if not isinstance(n, int) or n >= 1:
                    v.wait_ge(s["tra"], n * 4)
                v.tensor_tensor(DG[:, :, :], bc(ident[:, :].unsqueeze(1), [P, NQ, P]), bc(r8.unsqueeze(2), [P, NQ, P]),
                                ALU.mult).then_inc(s["on"], 1)

            shift(0, True)
            reciprocals(0)
            with v.Fori(0, 7) as i:
                shift(i + 1, False)
                reciprocals(i + 1)

            v.sem_inc(s["mrg"], 1)

            def merged(i, first):
                for j in range(2):
                    n = i * 2 + j
                    for q in range(2):
                        o = 3 * j + q
                        b = i * 6 + (B_MRG + o)
                        next_low(b, None, o % 2)
                        if first and o < 2:
                            for k in range(4 * o, 4 * o + 4):
                                low(opQ_hi, opQ_lo, X[:, k, :], O_Y, k)
                        v.wait_ge(mm_done, b + 1)
                        v.wait_ge(s["mrg"], n + 1)
                        v.tensor_tensor(T[:, q, :], banks(2 * (o % 2), 2), R[:, :], ALU.mult).then_inc(evac_done, 1)
                    o = 3 * j + 2
                    b = i * 6 + (B_MRG + o)
                    next_low(b, None, o % 2)
                    v.wait_ge(mm_done, b + 1)
                    v.wait_ge(s["sig"], n * 2 + 2)
                    v.tensor_tensor(T[:, 0, :], T[:, 0, :], banks(4, 2), ALU.mult).then_inc(s["ptmp"], 1)
                    v.tensor_tensor(T[:, 1, :], T[:, 1, :], banks(6, 2), ALU.mult).then_inc(s["ptmp"], 1)
                    v.wait_ge(s["ptmp"], n * 2 + 2)
                    v.sem_inc(evac_done, 1)
                    v.tensor_tensor(tile(X, n), T[:, 0, :], T[:, 1, :], ALU.add).then_inc(s["mrg"], 1)
            merged(0, True)
            with v.Fori(1, 4) as i:
                merged(i, False)
            v.wait_ge(s["mrg"], DT + 1)
            for k in range(DT):
                low(opQ_hi, opQ_lo, X[:, k, :], O_WO2, k)
            zero_squares(4)

            def wo2_step(b, turn, n, slot):
                next_low(b, turn, slot)
                v.wait_ge(mm_done, b + 1)
                v.tensor_copy(tile(X, n), banks(2 * slot, 2)).then_inc(evac_done, 1)
                add_square(4, n)
            stream(v, B_WO2, 8, wo2_step)
            next_low(B_MLP2, None, 0)
            v.wait_ge(r_done, 5)
            v.wait_ge(evac_done, B_MLP2)
            v.wait_ge(ssq_done, 45)
            v.sem_inc(ssq_done, 9)

            def scaled(k):
                v.scalar_tensor_tensor(X[:, k, :], X[:, k, :], col[:, C_MIXPOST + k:C_MIXPOST + k + 1], R[:, :],
                                       ALU.mult, ALU.mult).then_inc(s["scaled"], 1)
            scaled(0)
            scaled(1)
            for k in range(DT):
                if k + 2 < DT:
                    scaled(k + 2)
                low(opP_hi, opP_lo, X[:, k, :], O_UP2, k, C_MLPPRE)

            def down2():
                def body(b, turn, n, slot):
                    acc_down(b, turn, n, slot)
                    add_square(6, n)
                stream(v, B_MLP2 + 56, 6, body)
                body(B_END - 2, B_END // 2 - 1, 6, 0)
                v.wait_ge(mm_done, B_END)
                v.tensor_tensor(X[:, 7, :], X[:, 7, :], banks(2, 2), ALU.add).then_inc(evac_done, 1)
                add_square(6, 7)

            mlp(B_MLP2, 5, opQ_hi, opQ_lo, 32, O_H2, None, down2)
            v.wait_ge(r_done, 7)
            v.wait_ge(evac_done, B_END)
            for k in range(DT):
                v.scalar_tensor_tensor(X[:, k, :], X[:, k, :], col[:, C_MLPPOST + k:C_MLPPOST + k + 1], R[:, :],
                                       ALU.mult, ALU.mult).then_inc(normed_out, 1)
                if k % 2 == 0:
                    v.wait_ge(normed_out, k + 1)
                    v.wait_ge(x_landed[k], 48)
                    v.tensor_tensor(X[:, k, :], X[:, k, :], Xre[:, k, :], ALU.add).then_inc(fin[0], 1)

        @block.tensor
        def _(pe):
            def product(psum, wslot, wcols, hi, lo, ks, ready=None, by_tile=False, begin=True, end=True):
                for x, k in enumerate(ks):
                    if ready is not None:
                        pe.wait_ge(operand_ready, ready(k))
                    wh = w_hi[:, wslot, wcols(k if by_tile else x)]
                    wl = w_lo[:, wslot, wcols(k if by_tile else x)]
                    for weight, operand in ((wh, hi), (wh, lo), (wl, hi)):
                        for half in range(2):
                            mm = pe.matmul(ps[:, psum + half, :], weight, operand[:, k, half * HALF:(half + 1) * HALF],
                                           start=(begin and x == 0 and weight is wh and operand is hi),
                                           stop=(end and x == len(ks) - 1 and weight is wl))
                return mm

            def wcols(x):
                return slice(x * P, (x + 1) * P)

            def dense(hi, lo, ready, ks=range(DT)):
                def body(b, turn, n, slot, split_next=True):
                    pe.wait_ge(w_lo_done, b + 1)
                    pe.wait_ge(evac_done, b - 1)
                    product(2 * slot, slot, wcols, hi, lo, ks, ready, True).then_inc(mm_done, 1)
                return body

            def statistic(norm):
                pe.wait_ge(ssq_done, 9 * norm + 9)
                if norm:
                    pe.wait_ge(r_done, norm)
                for half in range(2):
                    mm = pe.matmul(ps[:, 4 + half, :], ones[:, :], ssq[:, half * HALF:(half + 1) * HALF], start=True, stop=True)
                mm.then_inc(stat_done, 1)

            def behind(norm, b0, n, step):
                step(b0, b0 // 2, 0, 0)
                statistic(norm)
                step(b0 + 1, b0 // 2, 1, 1)
                if n > 2:
                    stream(pe, b0, n, step, 0, 1)

            for b in range(2):
                pe.wait_ge(w_lo_done, b + 1)
                for n in range(4):
                    if b:
                        pe.wait_ge(pp_evac, n + 1)
                    mm = product(2 * n, b, lambda x, n=n: slice((2 * n + x) * P, (2 * n + x + 1) * P),
                                 p_hi, p_lo, range(2), lambda k: O_PP + k + 1)
                    if n < 3:
                        mm.then_inc(pp_mm, 1)
                mm.then_inc(pp_mm, 1)
                pe.wait_ge(pp_mm, 4 * b + 4)
                pe.sem_inc(mm_done, 1)
            pe.wait_ge(pp_evac, 8)
            pe.wait_ge(ones_set, 4)
            w_in = dense(opP_hi, opP_lo, lambda k: O_WIN + k + 1)
            behind(0, B_WIN, 4, w_in)
            pe.wait_ge(r_done, 1)
            pe.wait_ge(m["sq"], 3)
            pe.wait_ge(m["lat"], 1)
            for a in range(2):
                for half in range(2):
                    mm = pe.matmul(ps[:, 4 + 2 * a + half, :], ones[:, :], LSQ[:, 2 * a, half * HALF:(half + 1) * HALF],
                                   start=True, stop=True)
                mm.then_inc(m["stat"], 1)
            stream(pe, B_WIN + 4, 4, w_in)
            pe.wait_ge(m["ln"], 2)
            pe.wait_ge(g["w2"], 16)
            for pr in range(2):
                for half in range(2):
                    mm = pe.matmul(ps[:, 4 + 2 * pr + half, :], gw2[0:GRANK, pr * P:(pr + 1) * P],
                                   Z[0:GRANK, 3, half * HALF:(half + 1) * HALF], start=True, stop=True)
                mm.then_inc(g["logit"], 1)
            stream(pe, B_WIN + 8, 6, w_in)
            pe.wait_ge(g["lin"], 2)
            pe.wait_ge(evac_done, B_WIN + 12)
            for w in range(WIN):
                if w >= 2:
                    pe.wait_ge(g["trc"], w - 1)
                for f in range(4):
                    mm = pe.transpose(ps[:, 4 + w % 2, f * P:(f + 1) * P], Z[:, 8 + f, w * P:(w + 1) * P], ident[:, :])
                mm.then_inc(g["tr"], 1)
            stream(pe, B_WIN + 14, 2, w_in)

            def scores(bank, par, k_src, q_src, width):
                r = slice(64 * par, 64 * par + 64)
                for pr in range(2):
                    for w in range(WIN):
                        at_ = (pr * WIN + w) * width
                        mm = pe.matmul(banks(bank, 2 * width // 64)[:, at_:at_ + width], k_src(r, pr, w), q_src(r, pr, w),
                                       start=True, stop=True)
                return mm

            pe.wait_ge(evac_done, B_WOUT)
            pe.wait_ge(g["trc"], WIN)
            for par in range(2):
                scores(4 * par, par, lambda r, pr, w: Z[r, 6 + pr, w * P:(w + 1) * P],
                       lambda r, pr, w: Z[r, 4 + pr, w * P:(w + 1) * P], P).then_inc(g["lmm"], 1)
            pe.wait_ge(g["kdec"], 2)
            pe.wait_ge(g["lcp"], 1)
            for w in range(WIN):
                if w >= 2:
                    pe.wait_ge(g["trc"], WIN + w - 1)
                for pr in range(2):
                    mm = pe.transpose(ps[:, w % 2, pr * P:(pr + 1) * P], KE[0][:, pr, w * P:(w + 1) * P], ident[:, :])
                mm.then_inc(g["tr"], 1)
            pe.wait_ge(g["trc"], 2 * WIN)
            pe.wait_ge(g["lcp"], 2)

            def updates(pr):
                for c in range(NCH):
                    toks = slice(64 * (c % 2), 64 * (c % 2) + 64)
                    bank = 4 + 2 * (c % 2) + (c // 2) // 4
                    for hp in range(2):
                        h = 2 * pr + hp
                        mm = pe.matmul(ps[64 * hp:64 * hp + 64, bank, ((c // 2) % 4) * P:((c // 2) % 4 + 1) * P],
                                       KDT[toks, c // 2, h * 64:(h + 1) * 64], VT[toks, c // 2, h * P:(h + 1) * P],
                                       start=True, stop=True)
                mm.then_inc(g["upd"], 1)

            updates(0)
            for lv in range(len(LEVELS)):
                pe.wait_ge(g["lq"], 2 * lv + 2)
                pe.wait_ge(g["lk"], lv + 1)
                for pr in range(2):
                    if lv:
                        pe.wait_ge(g["lcp"], 1 + 2 * lv + pr)
                    for w in range(WIN):
                        mm = pe.matmul(banks(2 * pr, 2)[:, w * P:(w + 1) * P], KE[lv % 2][:, pr, w * P:(w + 1) * P],
                                       QE[lv % 2][:, pr, w, :, :], start=True, stop=True)
                mm.then_inc(g["lmm"], 1)
                if lv == 0:
                    pe.wait_ge(g["states"], 18)
                    updates(1)
            pe.wait_ge(g["lcp"], 2 + 2 * len(LEVELS))
            pe.wait_ge(g["states"], 3 + 30)

            def outputs(h):
                pr, r = h // 2, slice(64 * (h % 2), 64 * (h % 2) + 64)
                for w in range(WIN):
                    dst = banks(2 * h, 2)[:, w * P:(w + 1) * P]
                    pe.matmul(dst, VT[:, w, h * P:(h + 1) * P], SC[:, h % 2, pr, w, :], start=True, stop=False)
                    for x in range(2):
                        c = 2 * w + x
                        mm = pe.matmul(dst[:, 64 * x:64 * x + 64], ST8[r, pr, c, :], QX[r, pr, c * 64:(c + 1) * 64],
                                       start=False, stop=(x == 1))
                mm.then_inc(g["out"], 1)

            def squares(h):
                pe.wait_ge(g["sq"], h + 1)
                for half in range(2):
                    mm = pe.matmul(ps[:, 2 * h + half, :], ones[:, :], SQG[:, h % 2, half * HALF:(half + 1) * HALF],
                                   start=True, stop=True)
                mm.then_inc(g["nst"], 1)

            for h in range(GH):
                outputs(h)
                if h:
                    squares(h - 1)
            squares(GH - 1)

            pe.wait_ge(m["lat"], 4)
            pe.wait_ge(m["wv"], 16)
            pe.wait_ge(g["ln"], GH)

            def job(g):
                if not isinstance(g, int) or g >= 2:
                    pe.wait_ge(m["jev"], g - 1)

            def make(h, slot, j):
                bank, cols = 6 + j % 2, slice(j % 2 * HALF, (j % 2 + 1) * HALF)
                job(h * 12 + j)
                if j == 0:
                    pe.wait_ge(m[f"w{slot}"], (h - slot) * 16 + 32)
                    if not isinstance(h, int) or h >= 1:
                        pe.wait_ge(m["st"], h * 12 - 11)
                        pe.wait_ge(m["pv"], h * 12 - 8)
                if j < 2:
                    for k in range(2):
                        mm = pe.matmul(ps[0:QKD, bank, :], wq_h[:, slot, k * QKD:(k + 1) * QKD], Z[:, k, cols],
                                       start=(k == 0), stop=(k == 1))
                elif j < 4:
                    mm = pe.matmul(ps[0:NOPE, bank, :], wk_h[:, slot, :], Z[:, 2, cols], start=True, stop=True)
                elif j >= 8:
                    for x in range(4):
                        w = 4 * (j - 8) + x
                        mm = pe.matmul(ps[:, bank, x * 64:(x + 1) * 64], Z[:, 2, w * P:(w + 1) * P],
                                       wv_m[:, bass.ds(h * 64, 64)], start=True, stop=True)
                else:
                    a = (j - 4) // 2
                    pe.wait_ge(m["sq"], h * 2 + (4 + a))
                    mm = pe.matmul(ps[0:QKD, bank, :], ones[0:QKD, 0:QKD], SQ[0:QKD, a, cols], start=True, stop=True)
                mm.then_inc(m["job"], 1)

            def scores_of(h, slot, u):
                qt, c0, width = PIECES[u]
                if u == 0:
                    pe.wait_ge(m["rope"], h + 1)
                pe.wait_ge(m["red"], h * 12 + (u + 1))
                pe.matmul(ps[:, u % 2, 0:width], QK[0:QKD, slot, 0, qt * P:(qt + 1) * P],
                          QK[0:QKD, slot, 1, c0:c0 + width], start=True, stop=True).then_inc(m["scores"], 1)

            def maxima(h, more, r):
                g = h * 12 + (12 + (10 if more else 0) + r)
                job(g)
                pe.wait_ge(m["mx"], h * 2 + (r + 1))
                for x in range(4):
                    mm = pe.transpose(ps[0:1, 6 + r, x * P:(x + 1) * P], mx8[:, 4 * r + x:4 * r + x + 1], ident[:, :])
                mm.then_inc(m["job"], 1)

            def scores_t(h, slot, more, u):
                half, kt, q0, width = PIECES_T[u]
                if kt == 0:
                    pe.wait_ge(m["jev"], h * 12 + (12 + (10 if more else 0) + half + 1))
                pe.wait_ge(m["exp"], h * 12 + (u + 1))
                diagonal = q0 == kt * P
                mm = pe.matmul(ps[:, 2 + u % 2, 0:width], QK[0:QKD + 1, slot, 1, kt * P:(kt + 1) * P],
                               QK[0:QKD + 1, slot, 0, q0:q0 + width], start=True, stop=not diagonal)
                if diagonal:
                    mm = pe.matmul(ps[:, 2 + u % 2, 0:64], mrow[0:1, :], ones[0:1, 0:64], start=False, stop=True)
                mm.then_inc(m["st"], 1)

            def values(h, slot, u):
                half, kt, q0, width = PIECES_T[u]
                if kt == 0:
                    pe.wait_ge(m["ofree"], h * 2 + (1 + half))
                pe.wait_ge(m["exp"], h * 12 + (u + 3))
                c0 = q0 - half * HALF
                pe.matmul(ps[:, 4 + half, c0:c0 + width], VA[:, slot, kt, :], PT[:, u % 4, 0:width],
                          start=(kt == 0), stop=(kt == 4 * half + 3)).then_inc(m["pv"], 1)

            def head(h, slot, more):
                if isinstance(h, int) and h == 0:
                    pe.wait_ge(m["consts"], 5)
                for u in range(12):
                    scores_of(h, slot, u)
                    if more and u < 10:
                        make(h + 1, 1 - slot, u)
                for r in range(2):
                    maxima(h, more, r)
                scores_t(h, slot, more, 0)
                scores_t(h, slot, more, 1)
                for u in range(12):
                    if u + 2 < 12:
                        scores_t(h, slot, more, u + 2)
                    values(h, slot, u)

            pe.sem_inc(m["st"], 1)
            pe.sem_inc(m["pv"], 4)
            for j in range(10):
                make(0, 0, j)
            pe.wait_ge(m["job"], 10)
            pe.sem_inc(m["job"], 2)
            head(0, 0, True)
            with pe.Fori(0, 3) as i:
                head(i * 2 + 1, 1, True)
                head(i * 2 + 2, 0, True)
            head(7, 1, False)

            pe.wait_ge(m["exp"], 12 * MH + 2)
            stream(pe, B_WOUT, 8, dense(opP_hi, opP_lo, lambda k: O_WOUT + (k + 4) % 8 + 1, (4, 5, 6, 7, 0, 1, 2, 3)))

            def mlp(b0, norm, ahi, alo, a0, hhi, hlo, h0, first):
                up = dense(ahi, alo, lambda k: a0 + k + 1)

                def down(gi):
                    return dense(hhi, hlo, lambda k: gi * 8 + (h0 + k + 1))

                def run(gi, off, step):
                    with pe.Fori(0, 4) as i:
                        for j in range(2):
                            step(gi * 16 + i * 2 + (b0 + off + j), None, None, j)
                first(up)
                run(0, 8, down(0))
                with pe.Fori(1, 4) as gi:
                    run(gi, 0, up)
                    run(gi, 8, down(gi))
            mlp(B_MLP1, 1, opQ_hi, opQ_lo, O_UP1, opP_hi, opP_lo, O_H1, lambda up: behind(1, B_MLP1, 8, up))
            behind(2, B_GATE, 8, dense(opQ_hi, opQ_lo, lambda k: O_GATE + k + 1))

            behind(3, B_WIN2, 10, dense(opP_hi, opP_lo, lambda k: O_WIN2 + k + 1))
            pe.wait_ge(evac_done, B_MRG)
            for gi in range(4):
                pe.wait_ge(s["pool"], gi + 1)
                if gi >= 2:
                    pe.wait_ge(s["y"], gi - 1)
                for half in range(2):
                    mm = pe.matmul(ps[:, 2 * (gi % 2) + half, :], wpool[:, gi, :], Z2[:, gi, half * HALF:(half + 1) * HALF],
                                   start=True, stop=True)
                mm.then_inc(s["pmm"], 1)
            pe.wait_ge(s["z"], 10)
            for w in range(2):
                for x in range(4):
                    mm = pe.transpose(ps[:, 4 + w, x * P:(x + 1) * P], Z2[:, 9, (4 * w + x) * P:(4 * w + x + 1) * P], ident[:, :])
                mm.then_inc(s["vtr"], 1)
            pe.wait_ge(s["vtc"], 2)
            pe.wait_ge(s["zero"], 2)
            pe.wait_ge(s["y"], 4)

            def scores2(n, slot):
                pe.wait_ge(s["blk"], n * 2 + 2)
                if not isinstance(n, int) or n >= 1:
                    pe.wait_ge(s["sc"], n * 5 - 4)
                for par in range(2):
                    for i in range(4):
                        h = 4 * par + i
                        mm = pe.matmul(banks(0, 4)[:, h * 256:(h + 1) * 256], qb2[64 * par:64 * par + 64, slot, i, :],
                                       kb2[64 * par:64 * par + 64, slot, :], start=True, stop=True)
                mm.then_inc(s["qk"], 1)

            def attend(n, slot, first, more):
                if more:
                    scores2(n + 1, 1 - slot)
                pe.wait_ge(s["on"], n + 1)
                for q in range(4):
                    if not first or q >= 2:
                        pe.wait_ge(s["tca"], n * 4 + (q - 1))
                    for x in range(4):
                        h, kt = 2 * q + x // 2, x % 2
                        mm = pe.matmul(ps[:, 4 + q % 2, x * P:(x + 1) * P], P2[:, h, kt * P:(kt + 1) * P], DG[:, h, :],
                                       start=True, stop=True)
                    mm.then_inc(s["tra"], 1)
                pe.wait_ge(s["tca"], n * 4 + 4)
                pe.wait_ge(s["vb"], n + 1)
                if not isinstance(n, int) or n >= 2:
                    pe.wait_ge(s["otc"], n - 1 + 1)
                for grp in range(2):
                    for kt in range(2):
                        mm = pe.matmul(ps[64 * grp:64 * grp + 64, 6 + slot, :], vb2[:, slot, kt, 64 * grp:64 * grp + 64],
                                       PT2[:, 4 * grp:4 * grp + 4, kt, :], start=(kt == 0), stop=(kt == 1))
                mm.then_inc(s["pv"], 1)

            pe.sem_inc(s["pv"], 1)
            scores2(0, 0)
            attend(0, 0, True, True)
            with pe.Fori(0, 3) as i:
                attend(i * 2 + 1, 1, False, True)
                attend(i * 2 + 2, 0, False, True)
            attend(7, 1, False, False)

            pe.wait_ge(s["sc"], 40)
            with pe.Fori(0, 4) as i:
                for j in range(2):
                    for q in range(2):
                        o = 3 * j + q
                        b = i * 6 + (B_MRG + o)
                        dense(opP_hi, opP_lo, None)(b, None, None, o % 2)
                    o = 3 * j + 2
                    b = i * 6 + (B_MRG + o)
                    pe.wait_ge(w_lo_done, b + 1)
                    pe.wait_ge(s["mrg"], i * 2 + (j + 1))
                    product(4, o % 2, wcols, opQ_hi, opQ_lo, range(4), lambda k: O_Y + k + 1)
                    product(6, o % 2, lambda x: wcols(x + 4), opQ_hi, opQ_lo, range(4, 8), lambda k: O_Y + k + 1)\
                        .then_inc(mm_done, 1)
            stream(pe, B_WO2, 8, dense(opQ_hi, opQ_lo, lambda k: O_WO2 + k + 1))
            statistic(4)

            def first_up(up):
                pe.wait_ge(w_lo_done, B_MLP2 + 1)
                pe.wait_ge(evac_done, B_MLP2)
                pe.wait_ge(r_done, 5)
                for k in range(DT):
                    pe.wait_ge(sq_done, 8 * 5 + k + 1)
                    for half in range(2):
                        mm = pe.matmul(ps[:, 4 + half, :], ones[:, :],
                                       (sqs if k % 2 == 0 else ssq)[:, half * HALF:(half + 1) * HALF],
                                       start=(k == 0), stop=(k == DT - 1))
                    mm.then_inc(s["sqsum"], 1)
                    mm = product(0, 0, wcols, opP_hi, opP_lo, (k,), lambda k: O_UP2 + k + 1, True, k == 0, k == DT - 1)
                pe.wait_ge(s["sqsum"], DT)
                pe.sem_inc(stat_done, 1)
                mm.then_inc(mm_done, 1)
                up(B_MLP2 + 1, None, None, 1)
                stream(pe, B_MLP2, 8, up, 0, 1)
            mlp(B_MLP2, 5, opP_hi, opP_lo, O_UP2, opQ_hi, opQ_lo, O_H2, first_up)
            statistic(6)


def _layout(i):
    c = np.ascontiguousarray
    f = {k: np.asarray(v) for k, v in i.items()}

    def blocks(w):
        k, n = w.shape
        return w.reshape(k // P, P, n // P, P).transpose(2, 1, 0, 3).reshape(n // P * P, k // P * P)

    w_in = f["w_in"][0]
    q, k, v, low, r, cq, ckv, kr = np.split(w_in, np.cumsum([256, 256, 512, 16, 512, 256, 128]), axis=1)
    z = np.zeros((D, 48), np.float32)
    misc = np.concatenate([low, z, kr, z[:, :32]], axis=1)
    wp = f["w_ple_proj"][0]
    pp = [wp[:, b * 512:(b + 1) * 512].reshape(2, P, 4, P).transpose(1, 2, 0, 3).reshape(P, 1024) for b in range(2)]
    w_out = f["w_out"][0]
    w_out = np.concatenate([w_out[512:], w_out[:512]], axis=0)

    def mlp(up, down):
        u, out = blocks(up), []
        for gi in range(4):
            out += [u[gi * 1024:(gi + 1) * 1024], blocks(down[gi * 1024:(gi + 1) * 1024])]
        return out

    w2 = f["w_in_2"][0]
    q2 = w2[:, 512:1024].reshape(D, 2, 4, 64).transpose(0, 2, 1, 3).reshape(D, 512)
    gates = blocks(w2[:, 1280:])
    attn = f["w_branch_attn_2"][0].reshape(2, 4, 64, D).transpose(1, 0, 2, 3).reshape(512, D)
    br = blocks(np.concatenate([f["w_branch_pool_2"][0], attn], axis=0))
    merge = []
    for n in range(8):
        merge += [gates[n * P:(n + 1) * P], gates[(8 + n) * P:(9 + n) * P], br[n * P:(n + 1) * P]]
    stream = np.concatenate(
        pp + [blocks(np.concatenate([cq, ckv, misc, q, k, v, r], axis=1)), blocks(w_out)]
        + mlp(f["w_mlp_up"][0], f["w_mlp_down"][0]) + [blocks(f["w_ple_gate"][0])]
        + [blocks(np.concatenate([w2[:, :512], q2, w2[:, 1024:1280]], axis=1))] + merge
        + [blocks(f["w_out_2"][0])] + mlp(f["w_up_2"][0], f["w_down_2"][0]), axis=0)

    def vec(a):
        a = a.reshape(-1)
        if a.size % P:
            a = np.concatenate([a, np.zeros(P - a.size % P, a.dtype)])
        return a.reshape(-1, P).T

    b2 = f["b_in_2"][0]
    bq = b2[512:1024].reshape(2, 4, 64).transpose(1, 0, 2).reshape(-1)
    cols = np.concatenate(
        [vec(f[n][0]) for n in ("attn_norm", "mlp_norm", "ple_norm", "b_ple_gate")]
        + [vec(f[n][0]) for n in ("g_mix_pre_2", "g_mix_post_2", "g_mlp_pre_2", "g_mlp_post_2")]
        + [vec(np.concatenate([b2[:512], bq, b2[1024:]])), vec(f["pool_scale_2"][0]), vec(f["gla_gate_b"][0]),
           vec(f["gla_out_norm"][0]), vec(f["mla_q_norm"][0]), vec(f["mla_kv_norm"][0]),
           vec(f["qk_norm_q"][0]), vec(f["qk_norm_k"][0]), np.broadcast_to(f["attn_sinks_2"][0][None], (P, 8))], axis=1)
    ukv = f["mla_w_ukv"][0].reshape(P, 8, 2, 64)

    tok = np.arange(P)
    lmask = np.zeros((P, len(LEVELS), CHUNK), np.int32)
    for lv, size in enumerate(LEVELS):
        tt = np.concatenate([np.arange(n * 2 * size + size, (n + 1) * 2 * size) for n in range(P // (2 * size))])
        lmask[:, lv] = (tok[:, None] // (2 * size) == tt[None] // (2 * size)) & (tok[:, None] % (2 * size) < size)
    inv = (10000.0 ** (-np.arange(0, 32, 2, dtype=np.float32) / np.float32(32))).astype(np.float32)
    inv2 = (500000.0 ** (-np.arange(0, 16, 2, dtype=np.float32) / np.float32(16))).astype(np.float32)
    a2 = (np.arange(S, dtype=np.float32)[None] * inv2[:, None]).astype(np.float32)
    tabC, tabS = np.ones((P, S), np.float32), np.zeros((P, S), np.float32)
    for o in (0, 64):
        tabC[o:o + 8] = tabC[o + 8:o + 16] = np.cos(a2)
        tabS[o:o + 8], tabS[o + 8:o + 16] = -np.sin(a2), np.sin(a2)
    rel = tok[:, None] + P - np.arange(256)[None]
    band = (rel >= 0) & (rel < 128)
    mask2 = np.stack([np.where(band & (np.arange(256) >= P)[None], 0, NEG), np.where(band, 0, NEG)], 1).astype(np.float32)
    icnt = np.stack([1.0 / np.minimum(np.arange(16) + 1, w) for w in POOL_W]).astype(np.float32)
    return {
        "w_stream": c(stream), "xT": c(f["x"][0].T), "pT": c(f["p"][0, 0].T), "cols": c(cols),
        "ident": np.eye(P, dtype=np.float32), "lmask": lmask,
        "dmask": (np.eye(P) * GDK ** -0.5).astype(np.float32), "gw2": c(f["gla_gate_w2"][0]),
        "w_uv": c(ukv[:, :, 1].reshape(P, 512)), "freq": np.concatenate([-inv, inv])[:, None],
        "positions": c(f["positions"][0].astype(np.int32)),
        "w_uq": c(f["mla_w_uq"][0].reshape(2, P, 8, 96).transpose(2, 1, 0, 3).reshape(8 * P, 192)),
        "w_uk": c(ukv[:, :, 0].transpose(1, 0, 2).reshape(8 * P, 64)),
        "tabC": tabC, "tabS": tabS, "mask2": mask2,
        "icnt": c(np.broadcast_to(icnt[None], (P, 4, 16))), "w_pool": c(f["w_pool_2"][0].transpose(1, 0, 2)),
    }


def kernel(**inputs):
    import concourse.bacc as bacc
    from concourse.bass_utils import run_bass_kernel_spmd as run

    arrays = _layout(inputs)
    nc = bacc.Bacc("TRN2", target_bir_lowering=False, num_devices=1)
    t = {n: nc.dram_tensor("in_" + n, a.shape, mybir.dt.from_np(a.dtype), kind="ExternalInput").ap()
         for n, a in arrays.items()}
    t["out"] = nc.dram_tensor("out_T", (D, S), F32, kind="ExternalOutput").ap()
    for n in ("pp_spill", "x_spill"):
        t[n] = nc.dram_tensor(n, (D, S), F32, kind="Internal").ap()
    build(nc, t)
    r = run(nc, [{"in_" + n: a for n, a in arrays.items()}], core_ids=[0])
    return np.ascontiguousarray(r.results[0]["out_T"].T)[None]
```
